# Optimizing a Trainium2 kernel written in Bass

```python
import math, functools
import jax, jax.numpy as jnp
from jax import lax
import numpy as np

D_MODEL = 1024
BATCH = 1
SEQ = 512
DEPTH = 1
DEC_BATCH = 8
DEC_SEQ = 1
PAST_LEN = 1024
PAGE_SIZE = 128

N_META = 16
NORM_EPS = 1e-6
RW_HEAD = 64
RW_DIM = D_MODEL // 2
RW_HEADS = RW_DIM // RW_HEAD
W_LORA = 64
A_LORA = 64
G_LORA = 128
RW_PROJ = 3 * RW_DIM + W_LORA + A_LORA + G_LORA
RW_LN_EPS = 64e-5
DA_DK = 64
DA_DV = 2 * DA_DK
DA_DIM = D_MODEL // 2
DA_HEADS = DA_DIM // DA_DV
DA_QK = DA_HEADS * 2 * DA_DK
DA_V = DA_HEADS * DA_DV
Q_BLOCK = 128
IN_WIDTH = RW_PROJ + 2 * DA_QK + DA_V + 2 * D_MODEL
N_KEYS = 128
N_EXPERTS = N_KEYS * N_KEYS
PEER_HEADS = 8
PEER_TOPK = 16
PEER_DQ = 256
PEER_DHALF = PEER_DQ // 2
PEER_BLOCK = 256

kernel_name = "rwkv7_diffattn_peer_hybrid_step"

F32 = jnp.float32

def rms_norm(x, g, eps=NORM_EPS):
    xf = x.astype(F32)
    y = xf * lax.rsqrt(jnp.mean(xf * xf, axis=-1, keepdims=True) + eps)
    return (y * g.astype(F32)).astype(x.dtype)

def alibi_slopes(n):
    return jnp.exp2(-8.0 * jnp.arange(1, n + 1, dtype=F32) / n)

def rwkv_branch(p, shift_prev, S0, lp):
    B, T, _ = p.shape
    p_prev = jnp.concatenate([shift_prev[:, None, :].astype(p.dtype), p[:, :-1]], axis=1)
    ps = (p + (p_prev - p) * lp['rw_mu']).astype(F32)
    r, k, v, wl, al, gl = jnp.split(ps, [RW_DIM, 2 * RW_DIM, 3 * RW_DIM, 3 * RW_DIM + W_LORA,
                                        3 * RW_DIM + W_LORA + A_LORA], axis=-1)
    w = -jax.nn.softplus(-(lp['rw_w0'] + jnp.tanh(wl) @ lp['rw_w2'])) - 0.5
    decay = jnp.exp(-jnp.exp(w))
    a = jax.nn.sigmoid(lp['rw_a0'] + al @ lp['rw_a2'])
    g = jax.nn.sigmoid(gl) @ lp['rw_g2']
    heads = lambda t: t.reshape(B, T, RW_HEADS, RW_HEAD)
    kk = heads(k * lp['rw_kk'])
    kk = kk / jnp.maximum(jnp.sqrt(jnp.sum(kk * kk, axis=-1, keepdims=True)), 1e-12)
    k = k * (1.0 + (a - 1.0) * lp['rw_ka'])
    rh, kh, vh, wh, ah = heads(r), heads(k), heads(v), heads(decay), heads(a)
    a_vec, b_vec = -kk, kk * ah

    def step(S, inp):
        r_t, w_t, k_t, v_t, a_t, b_t = inp
        sa = jnp.einsum('bhvk,bhk->bhv', S, a_t)
        S = S * w_t[:, :, None, :] + sa[..., None] * b_t[:, :, None, :] + v_t[..., None] * k_t[:, :, None, :]
        return S, jnp.einsum('bhvk,bhk->bhv', S, r_t)

    seq = tuple(jnp.moveaxis(t, 1, 0) for t in (rh, wh, kh, vh, a_vec, b_vec))
    S_fin, ys = lax.scan(step, S0.astype(F32), seq)
    y = jnp.moveaxis(ys, 0, 1)
    mu = jnp.mean(y, axis=-1, keepdims=True)
    var = jnp.mean(jnp.square(y - mu), axis=-1, keepdims=True)
    y = ((y - mu) * lax.rsqrt(var + RW_LN_EPS)).reshape(B, T, RW_DIM) * lp['rw_ln_g'] + lp['rw_ln_b']
    bonus = (jnp.sum(rh * kh * lp['rw_rk'], axis=-1, keepdims=True) * vh).reshape(B, T, RW_DIM)
    y = ((y + bonus) * g).astype(p.dtype)
    return y @ lp['w_rw_br'], p[:, -1], S_fin.astype(p.dtype)

def diff_attn_prompt(q, k, v, lam):
    B, T = q.shape[:2]
    nb = -(-T // Q_BLOCK)
    Tp = nb * Q_BLOCK
    pad = ((0, 0), (0, Tp - T), (0, 0), (0, 0), (0, 0))
    qp, kp, vp = jnp.pad(q, pad), jnp.pad(k, pad), jnp.pad(v, pad[:4])
    slopes = alibi_slopes(DA_HEADS)[None, :, None, None, None]
    kpos = jnp.arange(Tp)
    qblocks = jnp.moveaxis(qp.reshape(B, nb, Q_BLOCK, DA_HEADS, 2, DA_DK), 1, 0)
    starts = jnp.arange(nb) * Q_BLOCK

    def block(args):
        qb, start = args
        qpos = start + jnp.arange(Q_BLOCK)
        s = jnp.einsum('bqhcd,bkhcd->bhcqk', qb, kp).astype(F32) * (DA_DK ** -0.5)
        dist = (qpos[:, None] - kpos[None, :]).astype(F32)
        s = jnp.where(dist >= 0, s - slopes * dist, -jnp.inf)
        pr = jax.nn.softmax(s, axis=-1)
        att = pr[:, :, 0] - lam * pr[:, :, 1]
        return jnp.einsum('bhqk,bkhv->bqhv', att.astype(vp.dtype), vp)

    o = lax.map(block, (qblocks, starts))
    return jnp.moveaxis(o, 0, 1).reshape(B, Tp, DA_HEADS, DA_DV)[:, :T]

def diff_attn_sample(q, k, v, lam, k_past, v_past):
    S = q.shape[1]
    P = k_past.shape[1]
    scale = DA_DK ** -0.5
    slopes = alibi_slopes(DA_HEADS)[None, :, None, None, None]
    qpos = P + jnp.arange(S)
    s_past = jnp.einsum('bqhcd,bkhcd->bhcqk', q, k_past).astype(F32) * scale
    d_past = (qpos[:, None] - jnp.arange(P)[None, :]).astype(F32)
    s_past = s_past - slopes * d_past
    s_new = jnp.einsum('bqhcd,bkhcd->bhcqk', q, k).astype(F32) * scale
    d_new = (qpos[:, None] - (P + jnp.arange(S))[None, :]).astype(F32)
    s_new = jnp.where(d_new >= 0, s_new - slopes * d_new, -jnp.inf)
    pr = jax.nn.softmax(jnp.concatenate([s_past, s_new], axis=-1), axis=-1)
    att = (pr[:, :, 0] - lam * pr[:, :, 1]).astype(v.dtype)
    return (jnp.einsum('bhqk,bkhv->bqhv', att[..., :P], v_past)
            + jnp.einsum('bhqk,bkhv->bqhv', att[..., P:], v))

def peer_ffn(xn, lp):
    lead = xn.shape[:-1]
    x = xn.reshape(-1, D_MODEL)
    N = x.shape[0]
    q = (x @ lp['peer_wq']).reshape(N, PEER_HEADS, 2, PEER_DHALF)
    s = jnp.einsum('nhcd,ckd->nhck', q, lp['peer_subkeys']).astype(F32)
    v1, i1 = lax.top_k(s[:, :, 0], PEER_TOPK)
    v2, i2 = lax.top_k(s[:, :, 1], PEER_TOPK)
    cand = (v1[..., :, None] + v2[..., None, :]).reshape(N, PEER_HEADS, PEER_TOPK * PEER_TOPK)
    sc, ci = lax.top_k(cand, PEER_TOPK)
    e1 = jnp.take_along_axis(i1, ci // PEER_TOPK, axis=-1)
    e2 = jnp.take_along_axis(i2, ci % PEER_TOPK, axis=-1)
    idx = e1 * N_KEYS + e2
    gate = jax.nn.softmax(sc, axis=-1)
    nb = -(-N // PEER_BLOCK)
    npad = nb * PEER_BLOCK - N
    xr = jnp.pad(x, ((0, npad), (0, 0))).reshape(nb, PEER_BLOCK, D_MODEL)
    ir = jnp.pad(idx, ((0, npad), (0, 0), (0, 0))).reshape(nb, PEER_BLOCK, PEER_HEADS, PEER_TOPK)
    gr = jnp.pad(gate, ((0, npad), (0, 0), (0, 0))).reshape(nb, PEER_BLOCK, PEER_HEADS, PEER_TOPK)
    u_tab, v_tab = lp['peer_u'], lp['peer_v']

    def block(args):
        xb, ib, gb = args
        hid = jnp.einsum('td,thkd->thk', xb, u_tab[ib]).astype(F32)
        hid = jax.nn.gelu(hid, approximate=False) * gb
        return jnp.einsum('thk,thkd->td', hid.astype(xb.dtype), v_tab[ib])

    out = lax.map(block, (xr, ir, gr)).reshape(-1, D_MODEL)[:N]
    return out.reshape(*lead, D_MODEL)

def layer_forward(h, attn_core, shift0, S0, lp, lam_init):
    B, T, _ = h.shape
    xn = rms_norm(h, lp['norm1_g'])
    proj = xn @ lp['w_in']
    o1 = RW_PROJ
    o2 = o1 + DA_QK
    o3 = o2 + DA_QK
    o4 = o3 + DA_V
    o5 = o4 + D_MODEL
    p_rw, q, k, v, g_a, g_b = jnp.split(proj, [o1, o2, o3, o4, o5], axis=-1)
    y_rw, shift_last, S_fin = rwkv_branch(p_rw, shift0, S0, lp)
    q = rms_norm(q.reshape(B, T, DA_HEADS, 2, DA_DK), lp['da_qn_g'])
    k = rms_norm(k.reshape(B, T, DA_HEADS, 2, DA_DK), lp['da_kn_g'])
    v = v.reshape(B, T, DA_HEADS, DA_DV)
    lv = lp['da_lam'].astype(F32)
    lam = jnp.exp(jnp.sum(lv[0] * lv[1])) - jnp.exp(jnp.sum(lv[2] * lv[3])) + lam_init
    o = attn_core(q, k, v, lam)
    o = rms_norm(o, lp['da_subln_g']) * (1.0 - lam_init)
    y_da = o.reshape(B, T, DA_V) @ lp['w_da_br']
    mix = jax.nn.sigmoid(g_a) * y_rw + jax.nn.sigmoid(g_b) * y_da
    h = h + mix @ lp['w_out']
    h = h + peer_ffn(rms_norm(h, lp['norm2_g']), lp)
    return h, k, v, shift_last, S_fin

def setup_inputs(seed: int = 0) -> dict:
    key = jax.random.key(seed)
    ks = iter(jax.random.split(key, 48))
    nrm = lambda shape, scale: jax.random.normal(next(ks), shape, F32) * scale
    uni = lambda shape, lo, hi: jax.random.uniform(next(ks), shape, F32, lo, hi)
    n_pages = PAST_LEN // PAGE_SIZE
    n_used = DEC_BATCH * n_pages
    n_phys = n_used + max(1, n_used // 4)
    page_table = jax.random.permutation(next(ks), n_phys)[:n_used].reshape(DEC_BATCH, n_pages).astype(jnp.int32)
    return {
        'x_prompt': nrm((BATCH, SEQ, D_MODEL), 1.0),
        'x_sample': nrm((DEC_BATCH, DEC_SEQ, D_MODEL), 1.0),
        'cache_k': nrm((DEPTH, n_phys, PAGE_SIZE, DA_HEADS, 2, DA_DK), 1.0),
        'cache_v': nrm((DEPTH, n_phys, PAGE_SIZE, DA_HEADS, DA_DV), 1.0),
        'state_wkv': nrm((DEPTH, DEC_BATCH, RW_HEADS, RW_HEAD, RW_HEAD), 0.1),
        'state_shift': nrm((DEPTH, DEC_BATCH, RW_PROJ), 1.0),
        'page_table': page_table,
        'meta': nrm((N_META, D_MODEL), 1.0),
        'norm1_g': 1.0 + nrm((DEPTH, D_MODEL), 0.02),
        'w_in': nrm((DEPTH, D_MODEL, IN_WIDTH), D_MODEL ** -0.5),
        'rw_mu': uni((DEPTH, RW_PROJ), 0.0, 1.0),
        'rw_w0': uni((DEPTH, RW_DIM), -6.0, 1.0),
        'rw_w2': nrm((DEPTH, W_LORA, RW_DIM), 0.1 * W_LORA ** -0.5),
        'rw_a0': nrm((DEPTH, RW_DIM), 0.1),
        'rw_a2': nrm((DEPTH, A_LORA, RW_DIM), 0.1 * A_LORA ** -0.5),
        'rw_g2': nrm((DEPTH, G_LORA, RW_DIM), G_LORA ** -0.5),
        'rw_kk': 0.85 + nrm((DEPTH, RW_DIM), 0.02),
        'rw_ka': 1.0 + nrm((DEPTH, RW_DIM), 0.02),
        'rw_rk': nrm((DEPTH, RW_HEADS, RW_HEAD), 0.1),
        'rw_ln_g': 1.0 + nrm((DEPTH, RW_DIM), 0.02),
        'rw_ln_b': nrm((DEPTH, RW_DIM), 0.02),
        'w_rw_br': nrm((DEPTH, RW_DIM, D_MODEL), RW_DIM ** -0.5),
        'da_qn_g': 1.0 + nrm((DEPTH, DA_DK), 0.02),
        'da_kn_g': 1.0 + nrm((DEPTH, DA_DK), 0.02),
        'da_lam': nrm((DEPTH, 4, DA_DK), 0.1),
        'da_subln_g': 1.0 + nrm((DEPTH, DA_DV), 0.02),
        'w_da_br': nrm((DEPTH, DA_DIM, D_MODEL), DA_DIM ** -0.5),
        'w_out': nrm((DEPTH, D_MODEL, D_MODEL), D_MODEL ** -0.5),
        'norm2_g': 1.0 + nrm((DEPTH, D_MODEL), 0.02),
        'peer_wq': nrm((DEPTH, D_MODEL, PEER_HEADS * PEER_DQ), D_MODEL ** -0.5),
        'peer_subkeys': nrm((DEPTH, 2, N_KEYS, PEER_DHALF), PEER_DHALF ** -0.5),
        'peer_u': nrm((DEPTH, N_EXPERTS, D_MODEL), D_MODEL ** -0.5),
        'peer_v': nrm((DEPTH, N_EXPERTS, D_MODEL), (PEER_HEADS * PEER_TOPK) ** -0.5),
    }

def reference(x_prompt, x_sample, cache_k, cache_v, state_wkv, state_shift, page_table,
              meta, norm1_g, w_in, rw_mu, rw_w0, rw_w2, rw_a0, rw_a2, rw_g2, rw_kk, rw_ka, rw_rk,
              rw_ln_g, rw_ln_b, w_rw_br, da_qn_g, da_kn_g, da_lam, da_subln_g, w_da_br, w_out,
              norm2_g, peer_wq, peer_subkeys, peer_u, peer_v):
    B = x_prompt.shape[0]
    Bd = x_sample.shape[0]
    hp = jnp.concatenate([jnp.broadcast_to(meta.astype(x_prompt.dtype)[None], (B, N_META, D_MODEL)),
                          x_prompt], axis=1)
    hs = x_sample
    kp_l, vp_l, ks_l, vs_l, Sp_l, Ss_l, shp_l, shs_l = [], [], [], [], [], [], [], []
    for l in range(DEPTH):
        lp = dict(norm1_g=norm1_g[l], w_in=w_in[l], rw_mu=rw_mu[l], rw_w0=rw_w0[l], rw_w2=rw_w2[l],
                  rw_a0=rw_a0[l], rw_a2=rw_a2[l], rw_g2=rw_g2[l], rw_kk=rw_kk[l], rw_ka=rw_ka[l],
                  rw_rk=rw_rk[l], rw_ln_g=rw_ln_g[l], rw_ln_b=rw_ln_b[l], w_rw_br=w_rw_br[l],
                  da_qn_g=da_qn_g[l], da_kn_g=da_kn_g[l], da_lam=da_lam[l], da_subln_g=da_subln_g[l],
                  w_da_br=w_da_br[l], w_out=w_out[l], norm2_g=norm2_g[l], peer_wq=peer_wq[l],
                  peer_subkeys=peer_subkeys[l], peer_u=peer_u[l], peer_v=peer_v[l])
        lam_init = 0.8 - 0.6 * math.exp(-0.3 * l)
        hp, k_p, v_p, sh_p, S_p = layer_forward(
            hp, diff_attn_prompt, jnp.zeros((B, RW_PROJ), hp.dtype),
            jnp.zeros((B, RW_HEADS, RW_HEAD, RW_HEAD), F32), lp, lam_init)
        k_past = cache_k[l][page_table].reshape(Bd, -1, DA_HEADS, 2, DA_DK)
        v_past = cache_v[l][page_table].reshape(Bd, -1, DA_HEADS, DA_DV)
        attn_s = functools.partial(diff_attn_sample, k_past=k_past, v_past=v_past)
        hs, k_s, v_s, sh_s, S_s = layer_forward(hs, attn_s, state_shift[l], state_wkv[l], lp, lam_init)
        kp_l.append(k_p); vp_l.append(v_p); ks_l.append(k_s); vs_l.append(v_s)
        Sp_l.append(S_p); Ss_l.append(S_s); shp_l.append(sh_p); shs_l.append(sh_s)
    y_prompt = hp[:, N_META:]
    y_sample = hs
    return (y_prompt, y_sample, jnp.stack(kp_l), jnp.stack(vp_l), jnp.stack(ks_l), jnp.stack(vs_l),
            jnp.stack(Sp_l), jnp.stack(Ss_l), jnp.stack(shp_l), jnp.stack(shs_l))


_drawn_inputs = setup_inputs


def setup_inputs(seed=0):
    import zlib

    import numpy as np

    out = dict(_drawn_inputs(seed))
    spreads = {}
    factors = {'rw_w2': 8.0,
     'rw_ka': 2.67,
     'rw_ln_g': 29.494,
     'rw_ln_b': 29.041,
     'da_qn_g': 7.905,
     'da_kn_g': 3.009,
     'da_subln_g': 20.031,
     'norm2_g': 22.371,
     'rw_kk': 2.731,
     'rw_rk': 3.812}
    for name, (base, spread) in spreads.items():
        noise = np.random.default_rng([zlib.crc32(name.encode()), seed]).standard_normal(out[name].shape)
        drawn = base * np.exp(spread * noise) if base else spread * noise
        out[name] = __import__('jax').numpy.asarray(drawn.astype(out[name].dtype))
    for name, factor in factors.items():
        out[name] = (out[name] * factor).astype(out[name].dtype)
    return out
```

```python
import math
from contextlib import ExitStack

import concourse.bass as bass
from concourse import mybir

F32 = mybir.dt.float32
F32R = mybir.dt.float32r
U32 = mybir.dt.uint32
I32 = mybir.dt.int32
ALU = mybir.AluOpType
ACT = mybir.ActivationFunctionType
AX = mybir.AxisListType

P = 128
D = 1024
KD = D // P
META, SEQ, DEC = 16, 512, 8
NP_ = META + SEQ
T = NP_ + DEC
TQ = SEQ + DEC
TT = 5
RW_HEAD, RW_DIM, RW_PROJ = 64, 512, 1792
RB = RW_DIM // P
RWT = RW_PROJ // P
C = 64
PAD = C - META
NCH = (PAD + NP_) // C
TW = PAD + T
HA, DV = 4, 128
PAGE, NPAGE, PAST = 128, 8, 1024
HC = 2 * HA
PH, TOPK, KEYS = 8, 16, 128
SLOPE = [2.0 ** (-8.0 * (h + 1) / HA) for h in range(HA)]
LAM_INIT = 0.8 - 0.6 * math.exp(-0.3 * 0)
EPS, LN_EPS = 1e-6, 64e-5
MASKED = 1e30
LEVELS = [1, 2, 4, 8, 16, 32]

PARAMS = [("norm1_g", 8), ("norm2_g", 8), ("rw_mu", RWT), ("rw_w0", RB), ("rw_a0", RB), ("rw_kk", RB),
          ("rw_ka", RB), ("rw_rk", RB), ("rw_ln_g", RB), ("rw_ln_b", RB), ("da_subln_g", 1),
          ("da_qn_g", 1), ("da_kn_g", 1)]
PCOL = {}
for _name, _n in PARAMS:
    PCOL[_name] = sum(n for m, n in PARAMS[:len(PCOL)])
NPAR = sum(n for _, n in PARAMS)


class Stage:

    def __init__(self, nc, name):
        self.nc, self.name, self.ctx, self.sems = nc, name, ExitStack(), []

    def __enter__(self):
        self.ctx.__enter__()
        return self

    def __exit__(self, *e):
        self.ctx.__exit__(*e)
        for sem in self.sems:
            self.nc.sync.sem_clear(sem)

    def sb(self, name, shape, dt=F32):
        return self.ctx.enter_context(self.nc.sbuf_tensor(f"{self.name}_{name}", shape, dt))

    def ps(self, name, shape, dt=F32):
        return self.ctx.enter_context(self.nc.psum_tensor(f"{self.name}_{name}", shape, dt))

    def sem(self, name):
        self.sems.append(self.ctx.enter_context(self.nc.semaphore(f"{self.name}_{name}")))
        return self.sems[-1]

    def block(self):
        return self.ctx.enter_context(self.nc.Block())


class Chain:

    def __init__(self, eng, sem, i=None, per=0):
        self.eng, self.sem, self.n, self.i, self.per = eng, sem, 0, i, per

    def at(self, n):
        return n if self.i is None else self.i * self.per + n

    def __call__(self, ins):
        ins.then_inc(self.sem, 1)
        self.n += 1
        self.eng.wait_ge(self.sem, self.at(self.n))
        return self.n

    def end(self):
        assert self.i is None or self.n == self.per, (self.n, self.per)


def sc(nc):
    return nc.scalar.activation


def constants(nc, g, ins):
    c = {}
    for name, shape in (("ident", [P, P]), ("ones", [P, P]), ("bd", [P, P]), ("iota", [P, P]),
                        ("um", [P, C]), ("ui", [P, C]), ("lmt", [P, len(LEVELS), C]), ("m1", [P, C]),
                        ("ident2", [P, C]), ("par", [P, NPAR]), ("eps", [P, 2]), ("lam", [P, 2])):
        c[name] = g.sb(name, shape)
    with Stage(nc, "const") as s:
        rows = s.sb("rows", [P, P])
        lv = s.sb("lv", [P, 4, 64])
        pr = s.sb("pr", [P, 2, 64])
        ls = s.sb("ls", [P, 2])
        pt = s.ps("pt", [P, P])
        params, lams, made, step = s.sem("params"), s.sem("lams"), s.sem("made"), s.sem("step")
        turned, dots, exps = s.sem("turned"), s.sem("dots"), s.sem("exps")
        nload = len(PARAMS) + 2

        blk = s.block()

        @blk.sync
        def _(sp):
            for name, n in PARAMS:
                src = ins[name]
                r = PCOL[name]
                if name in ("da_qn_g", "da_kn_g"):
                    sp.dma_start(rows[r:r + 1, 0:64], src).then_inc(params, 16)
                    sp.dma_start(rows[r:r + 1, 64:128], src).then_inc(params, 16)
                elif name == "rw_rk":
                    sp.dma_start(rows[r:r + n, :], src.rearrange("o (m h) k -> (o m) (h k)", h=2)).then_inc(params, 16)
                else:
                    sp.dma_start(rows[r:r + n, :], src.rearrange("o (m p) -> (o m) p", p=P)).then_inc(params, 16)
            sp.dma_start(lv[:, :, :], ins["da_lam"].to_broadcast([P, 4, 64])).then_inc(lams, 16)


        @blk.gpsimd
        def _(pool):
            chain = Chain(pool, step)
            chain(nc.gpsimd.memset(c["ident"][:, :], 0.0))
            chain(nc.gpsimd.affine_select(out=c["ident"][:, :], in_=c["ident"][:, :], compare_op=ALU.not_equal,
                                          fill=1.0, base=0, pattern=[[-1, P]], channel_multiplier=1))
            chain(nc.gpsimd.iota(c["iota"][:, :], pattern=[[1, P]], base=0, channel_multiplier=0,
                                 allow_small_or_imprecise_dtypes=True))
            chain(nc.gpsimd.memset(c["ones"][:, :], 1.0))
            chain(nc.gpsimd.memset(c["bd"][:, :], 0.0))
            chain(nc.gpsimd.memset(c["lmt"][:, :, :], 0.0))
            chain(nc.gpsimd.memset(c["m1"][:, :], 0.0))
            one = c["ones"][0:64, 0:64]
            for b in (0, 64):
                q = slice(b, b + 64)
                one = c["ones"][q, 0:C]
                chain(nc.gpsimd.memset(c["bd"][q, q], 1.0))
                for m, op, st, cm in (("um", ALU.is_gt, 1, -1), ("ui", ALU.is_ge, 1, -1), ("ident2", ALU.is_equal, 1, -1)):
                    chain(nc.gpsimd.affine_select(out=c[m][q, :], in_=one, compare_op=op, fill=0.0, base=0,
                                                  pattern=[[st, C]], channel_multiplier=cm))
                for n, z in enumerate(LEVELS):
                    v = c["lmt"][q, n, :].rearrange("p (b o z) -> p b o z", o=2, z=z)[:, :, 1, :]
                    o = one.rearrange("p (b o z) -> p b o z", o=2, z=z)[:, :, 1, :]
                    nb = C // (2 * z)
                    chain(nc.gpsimd.affine_select(out=v, in_=o, compare_op=ALU.is_ge, fill=0.0, base=0,
                                                  pattern=[[-2 * z, nb], [0, z]], channel_multiplier=1))
                    chain(nc.gpsimd.affine_select(out=v, in_=v, compare_op=ALU.is_ge, fill=0.0, base=z - 1,
                                                  pattern=[[2 * z, nb], [0, z]], channel_multiplier=-1))
                v = c["m1"][q, :].rearrange("p (b o) -> p b o", o=2)[:, :, 0]
                o = one.rearrange("p (b o) -> p b o", o=2)[:, :, 0]
                chain(nc.gpsimd.affine_select(out=v, in_=o, compare_op=ALU.is_equal, fill=0.0, base=-1,
                                              pattern=[[-2, C // 2]], channel_multiplier=1))
            chain(nc.gpsimd.memset(c["eps"][:, 0:1], EPS))
            nc.gpsimd.memset(c["eps"][:, 1:2], LN_EPS).then_inc(made, 1)

        @blk.vector
        def _(dve):
            chain = Chain(dve, dots)
            dve.wait_ge(lams, 16)
            l4 = lv[:, :, :].rearrange("p (a b) k -> p a b k", b=2)
            chain(nc.vector.tensor_tensor(pr[:, :, :], l4[:, :, 0, :], l4[:, :, 1, :], ALU.mult))
            chain(nc.vector.tensor_reduce(ls[:, :], pr[:, :, :], AX.X, ALU.add))
            dve.wait_ge(exps, 1)
            chain(nc.vector.tensor_tensor(c["lam"][:, 0:1], ls[:, 0:1], ls[:, 1:2], ALU.subtract))
            chain(nc.vector.tensor_scalar(c["lam"][:, 0:1], c["lam"][:, 0:1], LAM_INIT, None, ALU.add))
            chain(nc.vector.tensor_scalar(c["lam"][:, 1:2], c["lam"][:, 0:1], -1.0, None, ALU.mult))
            dve.wait_ge(turned, 1)
            nc.vector.tensor_copy(c["par"][:, :], pt[:, 0:NPAR]).then_inc(dots, 1)

        @blk.scalar
        def _(act):
            act.wait_ge(dots, 2)
            sc(nc)(ls[:, :], ls[:, :], ACT.Exp).then_inc(exps, 1)

        @blk.tensor
        def _(pe):
            pe.wait_ge(params, 16 * nload)
            pe.wait_ge(made, 1)
            nc.tensor.transpose(pt[:, 0:NPAR], rows[0:NPAR, :], c["ident"][0:NPAR, 0:NPAR]).then_inc(turned, 1)
    return c


def load_tokens(nc, ins, c, xT):
    with Stage(nc, "load") as s:
        xt = s.sb("xt", [P, TT, D])
        pt = [s.ps(f"pt{b}", [P, 4, P]) for b in range(4)]
        rows, turned, copied = s.sem("rows"), s.sem("turned"), s.sem("copied")
        blk = s.block()
        xp, xs, me = ins["x_prompt"][0], ins["x_sample"][:, 0, :], ins["meta"]

        @blk.sync
        def _(sp):
            sp.dma_start(xt[0:META, 0, :], me).then_inc(rows, 16)
            sp.dma_start(xt[META:P, 0, :], xp[0:P - META, :]).then_inc(rows, 16)
            sp.dma_start(xt[:, 1:4, :], xp[P - META:4 * P - META, :].rearrange("(j p) d -> p j d", p=P)).then_inc(rows, 16)
            sp.dma_start(xt[0:META, 4, :], xp[4 * P - META:SEQ, :]).then_inc(rows, 16)
            sp.dma_start(xt[META:META + DEC, 4, :], xs).then_inc(rows, 16)

        @blk.tensor
        def _(pe):
            pe.wait_ge(rows, 5 * 16)
            for n in range(2 * TT):
                j, half = n // 2, n % 2
                w = min(P, T - P * j)
                if n >= 4:
                    pe.wait_ge(copied, n - 3)
                for q in range(4):
                    last = nc.tensor.transpose(pt[n % 4][:, q, 0:w], xt[0:w, j, (4 * half + q) * P:(4 * half + q + 1) * P],
                                               c["ident"][0:w, 0:w])
                last.then_inc(turned, 1)

        @blk.vector
        def _(dve):
            for n in range(2 * TT):
                j, half = n // 2, n % 2
                w = min(P, T - P * j)
                dve.wait_ge(turned, n + 1)
                nc.vector.tensor_copy(xT[:, 4 * half:4 * half + 4, j * P:j * P + w], pt[n % 4][:, :, 0:w]).then_inc(copied, 1)


def channel_norm(nc, name, c, src, x0, n, gcol, dst):
    h = n // 2
    with Stage(nc, name) as s:
        sq = s.sb("sq", [P, KD, n])
        rs = s.sb("rs", [P, n])
        ms = s.ps("ms", [P, 2, 512])
        squared, summed, rooted, inv = s.sem("squared"), s.sem("summed"), s.sem("rooted"), s.sem("inv")
        blk = s.block()

        @blk.scalar
        def _(act):
            for k in range(KD):
                sc(nc)(sq[:, k, :], src[:, k, x0:x0 + n], ACT.Square).then_inc(squared, 1)
            act.wait_ge(summed, 1)
            sc(nc)(rs[:, :].rearrange("p (a b) -> p a b", a=2), ms[:, :, 0:h], ACT.Sqrt, bias=c["eps"][:, 0:1],
                   scale=1.0 / D).then_inc(rooted, 1)

        @blk.tensor
        def _(pe):
            for k in range(KD):
                pe.wait_ge(squared, k + 1)
                for a in range(2):
                    last = nc.tensor.matmul(ms[:, a, 0:h], c["ones"][:, :], sq[:, k, a * h:a * h + h],
                                            start=(k == 0), stop=(k == KD - 1))
            last.then_inc(summed, 1)

        @blk.vector
        def _(dve):
            dve.wait_ge(rooted, 1)
            nc.vector.reciprocal(rs[:, :], rs[:, :]).then_inc(inv, 1)
            dve.wait_ge(inv, 1)
            for k in range(KD):
                nc.vector.scalar_tensor_tensor(out=dst[:, k, :], in0=src[:, k, x0:x0 + n],
                                               scalar=c["par"][:, gcol + k:gcol + k + 1], in1=rs[:, :],
                                               op0=ALU.mult, op1=ALU.mult)


def linear(nc, name, w, col0, tiles, x, x0, kc, n, engine, evacuate, extra=None):
    h = n // 2
    wv = w.rearrange("(c p) n -> p c n", p=P)
    with Stage(nc, name) as s:
        wt = [s.sb(f"w{b}", [P, kc, P]) for b in range(2)]
        acc = [s.ps(f"acc{b}", [P, 2, 512]) for b in range(2)]
        loaded = [s.sem(f"loaded{b}") for b in range(2)]
        done = [s.sem(f"done{b}") for b in range(2)]
        out = [s.sem(f"out{b}") for b in range(2)]
        tmp = extra(s) if extra else None
        blk = s.block()

        @blk.sync
        def _(sp):
            with sp.Fori(0, tiles // 2) as i:
                for b in range(2):
                    sp.wait_ge(done[b], i + 1)
                    sp.dma_start(wt[b][:, :, :], wv[:, :, bass.ds(i * (2 * P) + (col0 + b * P), P)]).then_inc(loaded[b], 16)

        @blk.tensor
        def _(pe):
            for b in range(2):
                pe.sem_inc(done[b], 1)
            with pe.Fori(0, tiles // 2) as i:
                for b in range(2):
                    pe.wait_ge(loaded[b], i * 16 + 16)
                    pe.wait_ge(out[b], i + 1)
                    for k in range(kc):
                        for a in range(2):
                            last = nc.tensor.matmul(acc[b][:, a, 0:h], wt[b][:, k, :], x[:, k, x0 + a * h:x0 + a * h + h],
                                                    start=(k == 0), stop=(k == kc - 1))
                    last.then_inc(done[b], 1)

        def take(eng):
            for b in range(2):
                eng.sem_inc(out[b], 1)
            with eng.Fori(0, tiles // 2) as i:
                for b in range(2):
                    eng.wait_ge(done[b], i + 2)
                    evacuate(eng, i, b, acc[b][:, :, 0:h], tmp).then_inc(out[b], 1)

        if engine == "scalar":
            blk.scalar(take)
        else:
            blk.vector(take)


def halves(ap):
    return ap.rearrange("p (a b) -> p a b", a=2)


def halves3(ap):
    return ap.rearrange("p o (a b) -> p (o a) b", a=2)


def project_values(nc, ins, xn, v_tok, outs, vnew):
    wv = ins["w_in"][0].rearrange("(c p) n -> p c n", p=P)
    v0 = RW_PROJ + 2 * 512
    with Stage(nc, "val") as s:
        w = s.sb("w", [P, KD, 512])
        acc = [s.ps(f"acc{b}", [P, 512]) for b in range(2)]
        loaded, done, out, stored = s.sem("loaded"), s.sem("done"), s.sem("out"), s.sem("stored")
        blk = s.block()

        @blk.sync
        def _(sp):
            sp.dma_start(w[:, :, :], wv[:, :, v0:v0 + 512]).then_inc(loaded, 16)
            sp.wait_ge(out, TT)
            vp = outs["v_prompt"][0, 0].rearrange("t h v -> t (h v)")
            sp.dma_start(vp[0:SEQ, :].rearrange("(j p) d -> p j d", p=P), v_tok[:, 0:4, :]).then_inc(stored, 16)
            sp.dma_start(vp[SEQ:NP_, :], v_tok[0:META, 4, :]).then_inc(stored, 16)
            sp.dma_start(outs["v_sample"][0, :, 0].rearrange("t h v -> t (h v)"), v_tok[META:META + DEC, 4, :]).then_inc(stored, 16)
            sp.dma_start(vnew, v_tok[META:META + DEC, 4, :]).then_inc(stored, 16)
            sp.wait_ge(stored, 64)

        @blk.tensor
        def _(pe):
            pe.wait_ge(loaded, 16)
            for j in range(TT):
                m = min(P, T - j * P)
                if j >= 2:
                    pe.wait_ge(out, j - 1)
                for k in range(KD):
                    last = nc.tensor.matmul(acc[j % 2][0:m, :], xn[:, k, j * P:j * P + m], w[:, k, :],
                                            start=(k == 0), stop=(k == KD - 1))
                last.then_inc(done, 1)

        @blk.scalar
        def _(act):
            for j in range(TT):
                m = min(P, T - j * P)
                act.wait_ge(done, j + 1)
                sc(nc)(v_tok[0:m, j, :], acc[j % 2][0:m, :], ACT.Copy).then_inc(out, 1)


def shift_mix(nc, ins, c, proj, outs):
    with Stage(nc, "shift") as s:
        shr = s.sb("shr", [DEC, RW_PROJ])
        sht = s.sb("sht", [P, RWT, DEC])
        last9 = s.sb("last9", [DEC + 1, RW_PROJ])
        d = s.sb("d", [P, RWT, T])
        pa = s.ps("pa", [P, RWT, DEC])
        pb = s.ps("pb", [DEC + 1, 4, 512])
        loaded, turned, step, tok, stored = s.sem("loaded"), s.sem("turned"), s.sem("step"), s.sem("tok"), s.sem("stored")
        blk = s.block()
        z = PAD

        @blk.sync
        def _(sp):
            sp.dma_start(shr[:, :], ins["state_shift"][0]).then_inc(loaded, 16)
            sp.wait_ge(tok, 1)
            sp.dma_start(outs["shift_prompt"][0], last9[0:1, :]).then_inc(stored, 16)
            sp.dma_start(outs["shift_sample"][0], last9[1:DEC + 1, :]).then_inc(stored, 16)
            sp.wait_ge(stored, 32)

        @blk.tensor
        def _(pe):
            for m in range(RWT):
                last = nc.tensor.transpose(pb[:, m // 4, (m % 4) * P:(m % 4 + 1) * P],
                                           proj[:, m, z + NP_ - 1:z + T], c["ident"][:, :])
            last.then_inc(turned, 1)
            pe.wait_ge(loaded, 16)
            for m in range(RWT):
                last = nc.tensor.transpose(pa[:, m, :], shr[:, m * P:(m + 1) * P], c["ident"][0:DEC, 0:DEC])
            last.then_inc(turned, 1)

        @blk.scalar
        def _(act):
            act.wait_ge(turned, 1)
            sc(nc)(last9[:, :], pb[:, :, :].rearrange("p a b -> p (a b)")[:, 0:RW_PROJ], ACT.Copy).then_inc(tok, 1)

        @blk.vector
        def _(dve):
            chain = Chain(dve, step)
            dve.wait_ge(turned, 2)
            chain(nc.vector.tensor_copy(sht[:, :, :], pa[:, :, :]))
            chain(nc.vector.tensor_tensor(d[:, :, 1:NP_], proj[:, 0:RWT, z:z + NP_ - 1], proj[:, 0:RWT, z + 1:z + NP_], ALU.subtract))
            chain(nc.vector.tensor_scalar(d[:, :, 0:1], proj[:, 0:RWT, z:z + 1], -1.0, None, ALU.mult))
            chain(nc.vector.tensor_tensor(d[:, :, NP_:T], sht[:, :, :], proj[:, 0:RWT, z + NP_:z + T], ALU.subtract))
            dve.wait_ge(tok, 1)
            for m in range(RWT):
                nc.vector.scalar_tensor_tensor(out=proj[:, m, z:z + T], in0=d[:, m, :],
                                               scalar=c["par"][:, PCOL["rw_mu"] + m:PCOL["rw_mu"] + m + 1],
                                               in1=proj[:, m, z:z + T], op0=ALU.mult, op1=ALU.add)


def rwkv_prepare(nc, ins, c, proj, rw):
    H = T // 2
    with Stage(nc, "prep") as s:
        w2 = s.sb("w2", [P, RW_DIM])
        g2 = s.sb("g2", [P, RW_DIM])
        tl = s.sb("tl", [P, T])
        t1 = s.sb("t1", [P, RB, T])
        mask = s.sb("mask", [P, TW])
        pp = [s.ps(f"pp{b}", [P, 2, 512]) for b in range(4)]
        loaded, low, made, sig = s.sem("loaded"), s.sem("low"), s.sem("made"), s.sem("sig")
        step, root, kkp, bon, kks, bons = s.sem("step"), s.sem("root"), s.sem("kkp"), s.sem("bon"), s.sem("kks"), s.sem("bons")
        blk = s.block()
        z = slice(PAD, TW)
        col = lambda n, m: c["par"][:, PCOL[n] + m:PCOL[n] + m + 1]

        @blk.sync
        def _(sp):
            sp.dma_start(w2[0:64, :], ins["rw_w2"][0]).then_inc(loaded, 16)
            sp.dma_start(w2[64:128, :], ins["rw_a2"][0]).then_inc(loaded, 16)
            sp.dma_start(g2[:, :], ins["rw_g2"][0]).then_inc(loaded, 16)

        @blk.tensor
        def _(pe):
            pe.wait_ge(loaded, 48)
            pe.wait_ge(low, 3)
            for n in range(12):
                q, m = n // 4, n % 4
                if n >= 4:
                    pe.wait_ge(sig, n - 3)
                for a in range(2):
                    o = pp[n % 4][:, a, 0:H]
                    ms = slice(m * P, (m + 1) * P)
                    ts = slice(a * H, a * H + H)
                    if q == 0:
                        last = nc.tensor.matmul(o, w2[0:64, ms], tl[0:64, ts], start=True, stop=True)
                    elif q == 1:
                        last = nc.tensor.matmul(o, w2[64:128, ms], tl[64:128, ts], start=True, stop=True)
                    else:
                        last = nc.tensor.matmul(o, g2[:, ms], proj[:, 13, PAD + a * H:PAD + a * H + H], start=True, stop=True)
                last.then_inc(made, 1)
            for n in range(8):
                pe.wait_ge(kkp if n < 4 else bon, n % 4 + 1)
                pe.wait_ge(sig, 9 + n) if n < 4 else pe.wait_ge(root, n - 3)
                for a in range(2):
                    last = nc.tensor.matmul(pp[n % 4][:, a, 0:H], c["bd"][:, :], t1[:, n % 4, a * H:a * H + H], start=True, stop=True)
                last.then_inc(kks if n < 4 else bons, 1)

        @blk.scalar
        def _(act):
            sc(nc)(tl[0:64, :], proj[0:64, 12, z], ACT.Tanh).then_inc(low, 1)
            sc(nc)(tl[64:128, :], proj[64:128, 12, z], ACT.Copy).then_inc(low, 1)
            sc(nc)(proj[:, 13, z], proj[:, 13, z], ACT.Sigmoid).then_inc(low, 1)
            for n in range(12):
                q, m = n // 4, n % 4
                act.wait_ge(made, n + 1)
                src = pp[n % 4][:, :, 0:H]
                if q == 0:
                    sc(nc)(halves(rw["lw"][:, m, z]), src, ACT.Sigmoid, bias=col("rw_w0", m)).then_inc(sig, 1)
                elif q == 1:
                    sc(nc)(halves(rw["b"][:, m, z]), src, ACT.Sigmoid, bias=col("rw_a0", m)).then_inc(sig, 1)
                else:
                    sc(nc)(halves(rw["g"][:, m, z]), src, ACT.Copy).then_inc(sig, 1)
            for m in range(4):
                act.wait_ge(kks, m + 1)
                sc(nc)(halves(rw["la"][:, m, z]), pp[m][:, :, 0:H], ACT.Sqrt).then_inc(root, 1)

        @blk.vector
        def _(dve):
            chain = Chain(dve, step)
            for a in ("lw", "b", "kk"):
                nc.vector.memset(rw[a][:, :, 0:PAD], 0.0)
            nc.vector.memset(proj[:, 0:12, 0:PAD], 0.0)
            chain(nc.vector.memset(mask[:, :], 1.0))
            chain(nc.vector.memset(mask[:, 0:NCH * C].rearrange("p (n c) -> p n c", c=C)[:, :, 0:1], 0.0))
            for m in range(4):
                chain(nc.vector.tensor_scalar(rw["kk"][:, m, z], proj[:, 4 + m, z], col("rw_kk", m), None, ALU.mult))
                nc.vector.tensor_tensor(t1[:, m, :], rw["kk"][:, m, z], rw["kk"][:, m, z], ALU.mult).then_inc(kkp, 1)
            dve.wait_ge(sig, 4)
            chain(nc.vector.tensor_scalar(rw["lw"][:, :, z], rw["lw"][:, :, z], -math.exp(-0.5), None, ALU.mult))
            for m in range(4):
                chain(nc.vector.tensor_tensor_scan(rw["L"][:, m, :], mask[:, :], rw["lw"][:, m, :], 0.0, ALU.mult, ALU.add))
            dve.wait_ge(sig, 8)
            dve.wait_ge(root, 4)
            chain(nc.vector.tensor_scalar(rw["la"][:, :, z], rw["la"][:, :, z], 1e-12, None, ALU.max))
            chain(nc.vector.reciprocal(rw["la"][:, :, z], rw["la"][:, :, z]))
            chain(nc.vector.tensor_tensor(rw["kk"][:, :, z], rw["kk"][:, :, z], rw["la"][:, :, z], ALU.mult))
            chain(nc.vector.tensor_tensor(rw["la"][:, :, :], rw["L"][:, :, :], rw["lw"][:, :, :], ALU.subtract))
            for m in range(4):
                chain(nc.vector.tensor_scalar(t1[:, m, :], rw["b"][:, m, z], -1.0, col("rw_ka", m), ALU.add, ALU.mult))
                chain(nc.vector.scalar_tensor_tensor(out=proj[:, 4 + m, z], in0=t1[:, m, :], scalar=1.0, in1=proj[:, 4 + m, z],
                                                     op0=ALU.add, op1=ALU.mult))
                chain(nc.vector.tensor_tensor(rw["b"][:, m, z], rw["b"][:, m, z], rw["kk"][:, m, z], ALU.mult))
                nc.vector.scalar_tensor_tensor(out=t1[:, m, :], in0=proj[:, m, z], scalar=col("rw_rk", m),
                                               in1=proj[:, 4 + m, z], op0=ALU.mult, op1=ALU.mult).then_inc(bon, 1)
            for m in range(4):
                dve.wait_ge(bons, m + 1)
                nc.vector.tensor_tensor(halves(rw["bonus"][:, m, :]), pp[m][:, :, 0:H], halves(proj[:, 8 + m, z]), ALU.mult)


def rwkv_chunks(nc, c, proj, rw, yT, outs):
    with Stage(nc, "chunk") as s:
        W = [P, RB, C]
        t = {n: s.sb(n, W) for n in ("eP", "eN", "eA", "at", "bt", "kt", "rt", "vc", "ykT", "N", "NT", "AkT", "RbT", "RkT",
                                     "X", "XT", "Y", "V", "Bt", "Kt", "W0", "U", "S")}
        lev = s.sb("lev", [P, len(LEVELS), RB, C])
        pc = s.sb("pc", [P, RB, 1])
        pfull = [s.ps(f"p{n}", [P, 2 * RB, C]) for n in range(8)]
        p = [x[:, 0:RB, :] for x in pfull]
        spare = pfull[7][0:32, RB, 0:1]
        srow = s.sb("srow", [P, RB, C])
        step, scaled, expd, prod, dsem = s.sem("step"), s.sem("scaled"), s.sem("expd"), s.sem("prod"), s.sem("dsem")
        stored, turned, final, live = s.sem("stored"), s.sem("turned"), s.sem("final"), s.sem("live")
        blk = s.block()

        def heads(pe, pairs):
            for out, terms in pairs:
                for m in range(RB):
                    for e in range(2):
                        q = slice(64 * e, 64 * e + 64)
                        for n, (l, r) in enumerate(terms):
                            rr = r[q, 0:64] if r is c["ident2"] else r[q, m, :]
                            last = nc.tensor.matmul(out[q, m, :], l[q, m, :], rr, start=(n == 0), stop=(n == len(terms) - 1))
            return last

        @blk.scalar
        def _(act):
            with act.Fori(0, NCH) as i:
                sl = bass.ds(i * C, C)
                act.wait_ge(prod, i * PE_STEPS + 1)
                sc(nc)(t["eP"][:, :, :], rw["L"][:, :, sl], ACT.Exp).then_inc(expd, 1)
                sc(nc)(t["eN"][:, :, :], rw["L"][:, :, sl], ACT.Exp, scale=-1.0).then_inc(expd, 1)
                sc(nc)(t["eA"][:, :, :], rw["la"][:, :, sl], ACT.Exp).then_inc(expd, 1)
                sc(nc)(t["vc"][:, :, :], proj[:, 8:12, sl], ACT.Copy).then_inc(expd, 1)

        @blk.tensor
        def _(pe):
            pe.sem_inc(prod, 1)
            with pe.Fori(0, NCH) as i:
                def seen(n):
                    pe.wait_ge(dsem, i * DVE_STEPS + n)
                    nc.tensor.matmul(spare, c["ones"][:, 0:32], c["ones"][:, 0:1], start=True, stop=True)


                pe.wait_ge(expd, i * 4 + 4)
                seen(1)
                heads(pe, [(p[0], [(t["at"], t["bt"])]), (p[1], [(t["bt"], t["at"])]), (p[2], [(t["kt"], t["at"])]),
                           (p[3], [(t["bt"], t["rt"])]), (p[4], [(t["kt"], t["rt"])]), (p[5], [(t["vc"], c["ident2"])]),
                           (p[6], [(t["bt"], c["ident2"])]), (p[7], [(t["kt"], c["ident2"])])]).then_inc(prod, 1)
                seen(2)
                for n in range(1, len(LEVELS)):
                    heads(pe, [(p[0], [(lev[:, n], t["X"])])]).then_inc(prod, 1)
                    seen(1 + 2 * n)
                    if n < len(LEVELS) - 1:
                        heads(pe, [(p[1], [(t["XT"], t["Y"])])])
                    heads(pe, [(p[2], [(t["Y"], t["XT"])])]).then_inc(prod, 1)
                    if n == 1:
                        heads(pe, [(p[3], [(t["at"], t["S"]), (t["AkT"], t["V"])])]).then_inc(prod, 1)
                        seen(2 + 2 * n)
                    else:
                        seen(2 + 2 * n)
                heads(pe, [(p[4], [(t["XT"], t["W0"])])]).then_inc(prod, 1)
                seen(1 + 2 * len(LEVELS))
                heads(pe, [(p[5], [(t["S"], t["rt"]), (t["U"], t["RbT"]), (t["V"], t["RkT"])]),
                           (p[6], [(t["Bt"], t["U"]), (t["Kt"], t["V"])])]).then_inc(prod, 1)
                seen(DVE_STEPS)
            heads(pe, [(p[7], [(t["S"], c["ident2"])])]).then_inc(turned, 1)

        @blk.vector
        def _(dve):
            nc.vector.memset(t["S"][:, :, :], 0.0).then_inc(live, 1)
            dve.wait_ge(live, 1)
            with dve.Fori(0, NCH) as i:
                sl = bass.ds(i * C, C)
                chain = Chain(dve, step, i, CHAIN_STEPS)
                last = lambda ins: ins.then_inc(dsem, 1)
                made = lambda n: dve.wait_ge(prod, i * PE_STEPS + n + 1)
                bc = lambda m: m.unsqueeze(1).to_broadcast(W)
                dve.wait_ge(expd, i * 4 + 4)
                chain(nc.vector.tensor_tensor(t["bt"][:, :, :], rw["b"][:, :, sl], t["eN"][:, :, :], ALU.mult))
                chain(nc.vector.tensor_tensor(t["kt"][:, :, :], proj[:, 4:8, sl], t["eN"][:, :, :], ALU.mult))
                chain(nc.vector.tensor_tensor(t["rt"][:, :, :], proj[:, 0:4, sl], t["eP"][:, :, :], ALU.mult))
                chain(nc.vector.tensor_copy(pc[:, :, :], t["eP"][:, :, C - 1:C]))
                last(nc.vector.scalar_tensor_tensor(out=t["at"][:, :, :], in0=rw["kk"][:, :, sl], scalar=-1.0,
                                                    in1=t["eA"][:, :, :], op0=ALU.mult, op1=ALU.mult))
                made(1)
                chain(nc.vector.tensor_tensor(t["N"][:, :, :], p[0][:, :, :], bc(c["m1"][:, :]), ALU.mult))
                for n in range(len(LEVELS)):
                    chain(nc.vector.tensor_tensor(lev[:, n, :, :], p[1][:, :, :], bc(c["lmt"][:, n, :]), ALU.mult))
                chain(nc.vector.tensor_tensor(t["X"][:, :, :], t["N"][:, :, :], bc(c["ident2"][:, 0:C]), ALU.add))
                chain(nc.vector.tensor_tensor(t["XT"][:, :, :], lev[:, 0, :, :], bc(c["ident2"][:, 0:C]), ALU.add))
                chain(nc.vector.tensor_tensor(t["AkT"][:, :, :], p[2][:, :, :], bc(c["um"][:, :]), ALU.mult))
                chain(nc.vector.tensor_tensor(t["RbT"][:, :, :], p[3][:, :, :], bc(c["ui"][:, :]), ALU.mult))
                chain(nc.vector.tensor_tensor(t["RkT"][:, :, :], p[4][:, :, :], bc(c["ui"][:, :]), ALU.mult))
                chain(nc.vector.tensor_copy(t["V"][:, :, :], p[5][:, :, :]))
                chain(nc.vector.tensor_copy(t["Bt"][:, :, :], p[6][:, :, :]))
                last(nc.vector.tensor_copy(t["Kt"][:, :, :], p[7][:, :, :]))
                dve.wait_ge(dsem, i * DVE_STEPS + 2)
                k = 1
                for n in range(1, len(LEVELS)):
                    k += 1
                    made(k)
                    last(nc.vector.tensor_copy(t["Y"][:, :, :], p[0][:, :, :]))
                    k += 1
                    made(k)
                    if n < len(LEVELS) - 1:
                        chain(nc.vector.tensor_tensor(t["X"][:, :, :], p[1][:, :, :], t["X"][:, :, :], ALU.add))
                    if n == 1:
                        chain(nc.vector.tensor_tensor(t["XT"][:, :, :], p[2][:, :, :], t["XT"][:, :, :], ALU.add))
                        k += 1
                        made(k)
                        last(nc.vector.tensor_copy(t["W0"][:, :, :], p[3][:, :, :]))
                        dve.wait_ge(dsem, i * DVE_STEPS + 2 + 2 * n)
                    else:
                        last(nc.vector.tensor_tensor(t["XT"][:, :, :], p[2][:, :, :], t["XT"][:, :, :], ALU.add))
                        dve.wait_ge(dsem, i * DVE_STEPS + 2 + 2 * n)
                k += 1
                made(k)
                last(nc.vector.tensor_copy(t["U"][:, :, :], p[4][:, :, :]))
                k += 1
                made(k)
                assert k == PE_STEPS
                chain(nc.vector.tensor_copy(yT[:, :, sl], p[5][:, :, :]))
                chain(nc.vector.tensor_tensor(t["S"][:, :, :], p[6][:, :, :], t["S"][:, :, :], ALU.add))
                chain.end()
                last(nc.vector.tensor_tensor(t["S"][:, :, :], t["S"][:, :, :], pc[:, :, :].to_broadcast(W), ALU.mult))
                dve.wait_ge(dsem, i * DVE_STEPS + DVE_STEPS)
            dve.wait_ge(turned, 1)
            nc.vector.tensor_copy(srow[:, :, :], p[7][:, :, :]).then_inc(final, 1)

        @blk.sync
        def _(sp):
            sp.wait_ge(final, 1)
            for e in range(2):
                dst = outs["wkv_prompt"][0, 0].rearrange("(m e) v k -> e v m k", e=2)
                sp.dma_start(dst[e], srow[64 * e:64 * e + 64, :, :]).then_inc(stored, 16)
            sp.wait_ge(stored, 32)


PE_STEPS = 1 + 2 * (len(LEVELS) - 1) + 1 + 2
DVE_STEPS = 2 + 2 * (len(LEVELS) - 1) + 2
CHAIN_STEPS = 4 + 1 + len(LEVELS) + 2 + 3 + 2 + (len(LEVELS) - 2) + 1 + 2


def rwkv_sample(nc, c, proj, rw, yT, ins, outs, scr):
    RH, N = 8, RW_HEAD
    with Stage(nc, "step") as s:
        names = ["w", "k", "a", "b", "r", "v"]
        vt = s.sb("vt", [P, 6, RB, DEC])
        vr = s.sb("vr", [DEC, 6, RW_DIM])
        vec = s.sb("vec", [64, 6, N])
        HV = N // 2
        room = lambda a: rw[a][0:64, :, :].rearrange("p m t -> p (m t)")[:, 0:HV * N].rearrange("p (v k) -> p v k", k=N)
        S0, S1 = room("L"), room("la")
        t1 = s.sb("t1", [64, HV, N])
        sa = s.sb("sa", [64, N])
        y = s.sb("y", [64, N])
        yr = s.sb("yr", [DEC, RW_DIM])
        pt = s.ps("pt", [DEC, 6, 512])
        py = s.ps("py", [P, RB, DEC])
        step, dec, turned, rows, state, there, back = (s.sem(n) for n in ("step", "dec", "turned", "rows", "state", "there", "back"))
        again, stored, yturn = s.sem("again"), s.sem("stored"), s.sem("yturn")
        gath = s.sem("gath")
        blk = s.block()
        z = slice(PAD + NP_, TW)

        @blk.sync
        def _(sp):
            st_in = ins["state_wkv"][0].rearrange("b h v k -> (b h) v k")
            st_out = outs["wkv_sample"][0].rearrange("b h v k -> (b h) v k")
            sp.dma_start(S0[:, :, :], st_in[:, 0:HV, :]).then_inc(state, 16)
            sp.wait_ge(rows, 6)
            sp.dma_start(scr["vec"].rearrange("q b n -> b q n"), vr[:, :, :]).then_inc(there, 16)
            sp.wait_ge(there, 16)
            sp.dma_start(vec[:, :, :], scr["vec"].rearrange("q b (h k) -> (b h) q k", k=N)).then_inc(back, 16)
            sp.wait_ge(gath, 1)
            sp.dma_start(st_out[:, 0:HV, :], S1[:, :, :]).then_inc(stored, 16)
            sp.dma_start(S0[:, :, :], st_in[:, HV:N, :]).then_inc(state, 16)
            sp.wait_ge(gath, 2)
            sp.dma_start(scr["y"].rearrange("b (h k) -> (b h) k", k=N), y[:, :]).then_inc(there, 16)
            sp.dma_start(st_out[:, HV:N, :], S1[:, :, :]).then_inc(stored, 16)
            sp.wait_ge(there, 32)
            sp.dma_start(yr[:, :], scr["y"]).then_inc(again, 16)
            sp.wait_ge(stored, 32)

        @blk.scalar
        def _(act):
            sc(nc)(vt[:, 0, :, :], rw["lw"][:, :, z], ACT.Exp).then_inc(dec, 1)
            act.wait_ge(turned, 1)
            for q in range(6):
                sc(nc)(vr[:, q, :], pt[:, q, :], ACT.Copy).then_inc(rows, 1)

        @blk.tensor
        def _(pe):
            pe.wait_ge(dec, 1)
            pe.wait_ge(step, 5)
            for q in range(6):
                for m in range(RB):
                    last = nc.tensor.transpose(pt[:, q, m * P:(m + 1) * P], vt[:, q, m, :], c["ident"][:, :])
            last.then_inc(turned, 1)
            pe.wait_ge(again, 16)
            for m in range(RB):
                last = nc.tensor.transpose(py[:, m, :], yr[:, m * P:(m + 1) * P], c["ident"][0:DEC, 0:DEC])
            last.then_inc(yturn, 1)

        @blk.vector
        def _(dve):
            chain = Chain(dve, step)
            W = [64, HV, N]
            over_v = lambda q: vec[:, q, :].unsqueeze(1).to_broadcast(W)
            over_k = lambda v: v.unsqueeze(2).to_broadcast(W)
            chain(nc.vector.tensor_copy(vt[:, 1, :, :], proj[:, 4:8, z]))
            chain(nc.vector.tensor_scalar(vt[:, 2, :, :], rw["kk"][:, :, z], -1.0, None, ALU.mult))
            chain(nc.vector.tensor_copy(vt[:, 3, :, :], rw["b"][:, :, z]))
            chain(nc.vector.tensor_copy(vt[:, 4, :, :], proj[:, 0:4, z]))
            chain(nc.vector.tensor_copy(vt[:, 5, :, :], proj[:, 8:12, z]))
            dve.wait_ge(back, 16)
            for hv in range(2):
                vs = slice(hv * HV, (hv + 1) * HV)
                dve.wait_ge(state, 16 * (hv + 1))
                chain(nc.vector.tensor_tensor(t1[:, :, :], S0[:, :, :], over_v(2), ALU.mult))
                chain(nc.vector.tensor_reduce(sa[:, vs], t1[:, :, :], AX.X, ALU.add))
                if hv:
                    dve.wait_ge(stored, 16)
                chain(nc.vector.tensor_tensor(S1[:, :, :], S0[:, :, :], over_v(0), ALU.mult))
                chain(nc.vector.tensor_tensor(t1[:, :, :], over_k(sa[:, vs]), over_v(3), ALU.mult))
                chain(nc.vector.tensor_tensor(S1[:, :, :], S1[:, :, :], t1[:, :, :], ALU.add))
                chain(nc.vector.tensor_tensor(t1[:, :, :], over_k(vec[:, 5, vs]), over_v(1), ALU.mult))
                chain(nc.vector.tensor_tensor(S1[:, :, :], S1[:, :, :], t1[:, :, :], ALU.add))
                chain(nc.vector.tensor_tensor(t1[:, :, :], S1[:, :, :], over_v(4), ALU.mult))
                nc.vector.tensor_reduce(y[:, vs], t1[:, :, :], AX.X, ALU.add).then_inc(gath, 1)
                dve.wait_ge(gath, hv + 1)
            dve.wait_ge(yturn, 1)
            nc.vector.tensor_copy(yT[:, :, z], py[:, :, :])


def rwkv_output(nc, c, rw, yT, yo):
    H = TQ // 2
    with Stage(nc, "rwout") as s:
        d = s.sb("d", [P, RB, TQ])
        sq = s.sb("sq", [P, RB, TQ])
        pm = [s.ps(f"pm{m}", [P, 2, 512]) for m in range(4)]
        mean, cent, var, root, step = s.sem("mean"), s.sem("cent"), s.sem("var"), s.sem("root"), s.sem("step")
        blk = s.block()
        z = slice(PAD + META, TW)
        col = lambda n, m: c["par"][:, PCOL[n] + m:PCOL[n] + m + 1]

        @blk.tensor
        def _(pe):
            for m in range(4):
                for a in range(2):
                    last = nc.tensor.matmul(pm[m][:, a, 0:H], c["bd"][:, :], yT[:, m, PAD + META + a * H:PAD + META + a * H + H],
                                            start=True, stop=True)
                last.then_inc(mean, 1)
            for m in range(4):
                pe.wait_ge(cent, m + 1)
                for a in range(2):
                    last = nc.tensor.matmul(pm[m][:, a, 0:H], c["bd"][:, :], sq[:, m, a * H:a * H + H], start=True, stop=True)
                last.then_inc(var, 1)

        @blk.scalar
        def _(act):
            for m in range(4):
                act.wait_ge(var, m + 1)
                sc(nc)(halves(sq[:, m, :]), pm[m][:, :, 0:H], ACT.Sqrt, bias=c["eps"][:, 1:2], scale=1.0 / RW_HEAD).then_inc(root, 1)

        @blk.vector
        def _(dve):
            chain = Chain(dve, step)
            for m in range(4):
                dve.wait_ge(mean, m + 1)
                chain(nc.vector.scalar_tensor_tensor(out=halves(d[:, m, :]), in0=pm[m][:, :, 0:H], scalar=-1.0 / RW_HEAD,
                                                     in1=halves(yT[:, m, z]), op0=ALU.mult, op1=ALU.add))
                nc.vector.tensor_tensor(sq[:, m, :], d[:, m, :], d[:, m, :], ALU.mult).then_inc(cent, 1)
            for m in range(4):
                dve.wait_ge(root, m + 1)
                chain(nc.vector.reciprocal(sq[:, m, :], sq[:, m, :]))
                chain(nc.vector.scalar_tensor_tensor(out=d[:, m, :], in0=d[:, m, :], scalar=col("rw_ln_g", m), in1=sq[:, m, :],
                                                     op0=ALU.mult, op1=ALU.mult))
                chain(nc.vector.scalar_tensor_tensor(out=d[:, m, :], in0=d[:, m, :], scalar=col("rw_ln_b", m),
                                                     in1=rw["bonus"][:, m, META:T], op0=ALU.add, op1=ALU.add))
                chain(nc.vector.tensor_tensor(yo[:, m, :], d[:, m, :], rw["g"][:, m, z], ALU.mult))


def qk_norm(nc, c, proj, outs):
    H = T // 2
    with Stage(nc, "qk") as s:
        sq = s.sb("sq", [P, 8, T])
        krow = s.sb("krow", [P, TT, 512])
        pm = [s.ps(f"pm{n}", [P, 2, 512]) for n in range(2)]
        pk = [s.ps(f"pk{n}", [P, 512]) for n in range(2)]
        squared, summed, root, step, keys, turned, copied, stored, inv = (
            s.sem(n) for n in ("squared", "summed", "root", "step", "keys", "turned", "copied", "stored", "inv"))
        blk = s.block()
        z = slice(PAD, TW)

        @blk.scalar
        def _(act):
            for n in range(8):
                sc(nc)(sq[:, n, :], proj[:, 14 + n, z], ACT.Square).then_inc(squared, 1)
            for n in range(8):
                act.wait_ge(summed, n + 1)
                sc(nc)(halves(sq[:, n, :]), pm[n % 2][:, :, 0:H], ACT.Sqrt, bias=c["eps"][:, 0:1], scale=1.0 / 64).then_inc(root, 1)

        @blk.tensor
        def _(pe):
            for n in range(8):
                pe.wait_ge(squared, n + 1)
                if n >= 2:
                    pe.wait_ge(root, n - 1)
                for a in range(2):
                    last = nc.tensor.matmul(pm[n % 2][:, a, 0:H], c["bd"][:, :], sq[:, n, a * H:a * H + H], start=True, stop=True)
                last.then_inc(summed, 1)
            pe.wait_ge(keys, 4)
            for j in range(TT):
                w = min(P, T - j * P)
                if j >= 2:
                    pe.wait_ge(copied, j - 1)
                for h in range(HA):
                    last = nc.tensor.transpose(pk[j % 2][0:w, h * P:(h + 1) * P], proj[:, 18 + h, PAD + j * P:PAD + j * P + w],
                                               c["ident"][:, :])
                last.then_inc(turned, 1)

        @blk.vector
        def _(dve):
            chain = Chain(dve, step)
            for n in range(8):
                g = PCOL["da_qn_g" if n < 4 else "da_kn_g"]
                dve.wait_ge(root, n + 1)
                chain(nc.vector.reciprocal(sq[:, n, :], sq[:, n, :]))
                last = nc.vector.scalar_tensor_tensor(out=proj[:, 14 + n, z], in0=proj[:, 14 + n, z], scalar=c["par"][:, g:g + 1],
                                                      in1=sq[:, n, :], op0=ALU.mult, op1=ALU.mult)
                if n < 4:
                    chain(last)
                    chain(nc.vector.tensor_scalar(proj[:, 14 + n, z], proj[:, 14 + n, z], 0.125, None, ALU.mult))
                else:
                    last.then_inc(keys, 1)
            for j in range(TT):
                w = min(P, T - j * P)
                dve.wait_ge(turned, j + 1)
                nc.vector.tensor_copy(krow[0:w, j, :], pk[j % 2][0:w, :]).then_inc(copied, 1)

        @blk.sync
        def _(sp):
            sp.wait_ge(copied, TT)
            kp = outs["k_prompt"][0, 0].rearrange("t h c d -> t (h c d)")
            sp.dma_start(kp[0:SEQ, :].rearrange("(j p) d -> p j d", p=P), krow[:, 0:4, :]).then_inc(stored, 16)
            sp.dma_start(kp[SEQ:NP_, :], krow[0:META, 4, :]).then_inc(stored, 16)
            sp.dma_start(outs["k_sample"][0, :, 0].rearrange("t h c d -> t (h c d)"), krow[META:META + DEC, 4, :]).then_inc(stored, 16)
            sp.wait_ge(stored, 48)


def attend_prompt(nc, c, proj, v_tok, oT):
    WM = NP_
    with Stage(nc, "att") as s:
        dist = s.sb("dist", [P, WM])
        S = [s.sb(f"S{e}", [P, WM]) for e in range(2)]
        A = s.sb("A", [P, WM])
        AT = s.sb("AT", [P, TT, P])
        st = s.sb("st", [P, 2, 4])
        pS = [s.ps(f"pS{e}", [P, 1024]) for e in range(2)]
        pT = s.ps("pT", [P, 8, P])
        pO = s.ps("pO", [P, 512])
        built, scored, biased, expd, mixed, turned, copied, summed, taken, step = (
            s.sem(n) for n in ("built", "scored", "biased", "expd", "mixed", "turned", "copied", "summed", "taken", "step"))
        blk = s.block()
        steps = [(h, i) for h in range(HA) for i in range(4)]
        width = lambda i: META + P * (i + 1)
        blocks = lambda i: [(j, P if j <= i else META) for j in range(i + 2)]

        @blk.gpsimd
        def _(pool):
            nc.gpsimd.iota(dist[:, :], pattern=[[-1, WM]], base=META + 3 * P, channel_multiplier=1,
                           allow_small_or_imprecise_dtypes=True).then_inc(built, 1)
            pool.wait_ge(built, 1)
            nc.gpsimd.affine_select(out=dist[:, :], in_=dist[:, :], compare_op=ALU.is_ge, fill=MASKED, base=META + 3 * P,
                                    pattern=[[-1, WM]], channel_multiplier=1).then_inc(built, 1)

        @blk.tensor
        def _(pe):
            def scores(n):
                h, i = steps[n]
                for e in range(2):
                    q = slice(64 * e, 64 * e + 64)
                    if n:
                        pe.wait_ge(biased, 2 * (n - 1) + e + 1)
                    x0 = PAD + META + i * P
                    for a, b in ((0, min(width(i), 512)), (512, width(i))):
                        if b > a:
                            last = nc.tensor.matmul(pS[e][:, a:b], proj[q, 14 + h, x0:x0 + P], proj[q, 18 + h, PAD + a:PAD + b],
                                                    start=True, stop=True)
                    last.then_inc(scored, 1)

            scores(0)
            for n, (h, i) in enumerate(steps):
                pe.wait_ge(mixed, n + 1)
                for j, w in blocks(i):
                    last = nc.tensor.transpose(pT[0:w, j, :], A[:, j * P:j * P + w], c["ident"][:, :])
                last.then_inc(turned, 1)
                if n + 1 < len(steps):
                    scores(n + 1)
                pe.wait_ge(copied, n + 1)
                if n:
                    pe.wait_ge(taken, n)
                for j, w in blocks(i):
                    last = nc.tensor.matmul(pO[:, 0:P], v_tok[0:w, j, h * DV:(h + 1) * DV], AT[0:w, j, :],
                                            start=(j == 0), stop=(j == i + 1))
                last.then_inc(summed, 1)

        @blk.scalar
        def _(act):
            for n, (h, i) in enumerate(steps):
                for e in range(2):
                    act.wait_ge(biased, 2 * n + e + 1)
                    sc(nc)(S[e][:, 0:width(i)], S[e][:, 0:width(i)], ACT.Exp, bias=st[:, e, 0:1],
                           accum_out=st[:, e, 1:2]).then_inc(expd, 1)
                act.wait_ge(turned, n + 1)
                if n:
                    act.wait_ge(summed, n)
                sc(nc)(AT[:, 0:i + 1, :], pT[:, 0:i + 1, :], ACT.Copy)
                sc(nc)(AT[0:META, i + 1, :], pT[0:META, i + 1, :], ACT.Copy).then_inc(copied, 1)
                act.wait_ge(summed, n + 1)
                sc(nc)(oT[:, h, i * P:(i + 1) * P], pO[:, 0:P], ACT.Copy).then_inc(taken, 1)

        @blk.vector
        def _(dve):
            chain = Chain(dve, step)
            dve.wait_ge(built, 2)
            for n, (h, i) in enumerate(steps):
                w = width(i)
                if n:
                    dve.wait_ge(mixed, n)
                for e in range(2):
                    dve.wait_ge(scored, 2 * n + e + 1)
                    chain(nc.vector.scalar_tensor_tensor(out=S[e][:, 0:w], in0=dist[:, WM - w:WM], scalar=-SLOPE[h],
                                                         in1=pS[e][:, 0:w], op0=ALU.mult, op1=ALU.add))
                    nc.vector.tensor_reduce(st[:, e, 0:1], S[e][:, 0:w], AX.X, ALU.max, negate=True).then_inc(biased, 1)
                dve.wait_ge(expd, 2 * n + 2)
                chain(nc.vector.reciprocal(st[:, :, 2:3], st[:, :, 1:2]))
                chain(nc.vector.tensor_tensor(st[:, 1, 3:4], st[:, 1, 2:3], c["lam"][:, 1:2], ALU.mult))
                if n:
                    dve.wait_ge(turned, n)
                chain(nc.vector.tensor_scalar(A[:, 0:w], S[1][:, 0:w], st[:, 1, 3:4], None, ALU.mult))
                nc.vector.scalar_tensor_tensor(out=A[:, 0:w], in0=S[0][:, 0:w], scalar=st[:, 0, 2:3], in1=A[:, 0:w],
                                               op0=ALU.mult, op1=ALU.add).then_inc(mixed, 1)


def attend_sample(nc, ins, c, proj, oT, vnew):
    zs = PAD + NP_
    with Stage(nc, "dec") as s:
        K = [s.sb(f"K{b}", [P, NPAGE, 512]) for b in range(2)]
        V = [s.sb(f"V{b}", [P, NPAGE, 512]) for b in range(2)]
        vn = [s.sb(f"vn{b}", [1, 512]) for b in range(2)]
        Q = s.sb("Q", [P, DEC, 512])
        pages = s.sb("pages", [1, DEC * NPAGE], I32)
        bias = s.sb("bias", [P, NPAGE, 2, HA])
        Sc = s.sb("Sc", [P, NPAGE, 2, HA])
        rows = s.sb("rows", [HC, PAST + 1])
        new = s.sb("new", [HC, DEC])
        qk = s.sb("qk", [P, DEC, 2, HA])
        comb0 = s.sb("comb0", [HC, HA])
        comb = s.sb("comb", [HC, HA])
        st = s.sb("st", [HC, 3])
        at = s.sb("at", [P, NPAGE, HA])
        atn = s.sb("atn", [1, HA])
        orow = Q[0:HA, :, :]
        pQ = [s.ps(f"pQ{b}", [P, 512]) for b in range(2)]
        pN = s.ps("pN", [P, 512])
        pR = s.ps("pR", [HC, PAST])
        pA = s.ps("pA", [P, 16 * NPAGE, HA])[:, 0:NPAGE, :]
        pA1 = s.ps("pA1", [1, 512])
        pO = s.ps("pO", [HA, 512])
        names = ("ptab", "vtab", "step", "pstep", "prods", "newd", "newc", "qrep", "qcop", "sdone", "turned", "laid",
                 "maxed", "expd", "combd", "backt", "bcop", "summed", "kept", "gathered", "dstep", "astep")
        (ptab, vtab, step, pstep, prods, newd, newc, qrep, qcop, sdone, turned, laid,
         maxed, expd, combd, backt, bcop, summed, kept, gathered, dstep, astep) = (s.sem(n) for n in names)
        kin, vin, kfree, vfree = ([s.sem(f"{n}{b}") for b in range(2)] for n in ("kin", "vin", "kfree", "vfree"))
        blk = s.block()
        ck = ins["cache_k"][0].rearrange("n p h c d -> n p (h c d)")
        cv = ins["cache_v"][0].rearrange("n p h v -> n p (h v)")
        n_phys = ck.shape[0]

        def sequences(eng, first, middle, last):
            first(0, 0)
            with eng.Fori(0, DEC // 2 - 1) as i:
                middle(i, 1)
                middle(i, 2)
            middle(DEC // 2 - 1, 1)
            last(DEC // 2 - 1, 1)

        @blk.sync
        def _(sp):
            sp.dma_start(pages[:, :], ins["page_table"].rearrange("b n -> (b n)").unsqueeze(0)).then_inc(ptab, 16)
            sp.wait_ge(ptab, 16)
            with sp.Fori(0, DEC // 2) as i:
                for b in range(2):
                    sp.wait_ge(kfree[b], i + 1)
                    for pg in range(NPAGE):
                        page = sp.value_load(pages[0:1, bass.ds(i * (2 * NPAGE) + (b * NPAGE + pg), 1)], min_val=0, max_val=n_phys - 1)
                        sp.dma_start(K[b][:, pg, :], ck[bass.ds(page, 1)].rearrange("o p x -> p (o x)")).then_inc(kin[b], 16)

        @blk.gpsimd
        def _(pool):
            chain = Chain(pool, pstep)
            chain(nc.gpsimd.iota(bias[:, :, :, :], pattern=[[-PAGE, NPAGE], [0, HC]], base=PAST, channel_multiplier=-1,
                                 allow_small_or_imprecise_dtypes=True))
            chain(nc.gpsimd.memset(comb0[:, :], 0.0))
            chain(nc.gpsimd.affine_select(out=comb0[:, :], in_=comb0[:, :], compare_op=ALU.not_equal, fill=1.0, base=0,
                                          pattern=[[-1, HA]], channel_multiplier=1))
            chain(nc.gpsimd.affine_select(out=comb0[:, :], in_=comb0[:, :], compare_op=ALU.not_equal, fill=2.0, base=-HA,
                                          pattern=[[-1, HA]], channel_multiplier=1))
            pool.wait_ge(ptab, 16)
            with pool.Fori(0, DEC // 2) as i:
                for b in range(2):
                    pool.wait_ge(vfree[b], i + 1)
                    for pg in range(NPAGE):
                        page = pool.value_load(pages[0:1, bass.ds(i * (2 * NPAGE) + (b * NPAGE + pg), 1)], min_val=0, max_val=n_phys - 1)
                        pool.dma_start(V[b][:, pg, :], cv[bass.ds(page, 1)].rearrange("o p x -> p (o x)")).then_inc(vin[b], 16)
                    pool.dma_start(vn[b][:, :], vnew[bass.ds(i * 2 + b, 1), :]).then_inc(vin[b], 16)

        @blk.tensor
        def _(pe):
            for b in range(2):
                pe.sem_inc(vfree[b], 1)
            for b in range(DEC):
                if b >= 2:
                    pe.wait_ge(qcop, b - 1)
                for h in range(HA):
                    q = proj[:, 14 + h, zs + b:zs + b + 1].to_broadcast([P, P])
                    last = nc.tensor.matmul(pQ[b % 2][:, h * P:(h + 1) * P], q, c["ident"][:, :], start=True, stop=True)
                last.then_inc(qrep, 1)
            pe.wait_ge(prods, 1)
            for b in range(DEC):
                last = nc.tensor.matmul(pN[0:HC, b:b + 1], qk[:, b, :, :].rearrange("p e h -> p (e h)"), c["ones"][:, 0:1],
                                        start=True, stop=True)
            last.then_inc(newd, 1)

            def turn(i, off):
                pe.wait_ge(sdone, i * 2 + (off + 1))
                for pg in range(NPAGE):
                    last = nc.tensor.transpose(pR[:, pg * P:(pg + 1) * P], Sc[:, pg, :, :].rearrange("p e h -> p (e h)"), c["ident"][:, :])
                last.then_inc(turned, 1)

            def combine(i, off):
                pe.wait_ge(combd, i * 2 + (off + 1))
                for pg in range(NPAGE):
                    nc.tensor.matmul(pA[:, pg, :], rows[:, pg * P:(pg + 1) * P], comb[:, :], start=True, stop=True)
                nc.tensor.matmul(pA1[:, 0:HA], rows[:, PAST:PAST + 1], comb[:, :], start=True, stop=True).then_inc(backt, 1)

            def values(i, off):
                b = off % 2
                pe.wait_ge(bcop, i * 2 + (off + 1))
                pe.wait_ge(kept, i * 2 + (off + 1))
                pe.wait_ge(vin[b], (i + (off // 2 + 1)) * (16 * (NPAGE + 1)))
                for pg in range(NPAGE):
                    nc.tensor.matmul(pO[:, :], at[:, pg, :], V[b][:, pg, :], start=(pg == 0), stop=False)
                nc.tensor.matmul(pO[:, :], atn[:, :], vn[b][:, :], start=False, stop=True).then_inc(summed, 1)

            def middle(i, off):
                combine(i, off - 1)
                turn(i, off)
                values(i, off - 1)

            def last_one(i, off):
                combine(i, off)
                values(i, off)

            pe.sem_inc(kept, 1)
            sequences(pe, turn, middle, last_one)
            pe.wait_ge(kept, DEC + 1)
            for b in range(DEC):
                for h in range(HA):
                    last = nc.tensor.matmul(pN[:, h * DEC + b:h * DEC + b + 1], orow[:, b, h * DV:(h + 1) * DV],
                                            c["ident"][0:HA, h:h + 1], start=True, stop=True)
            last.then_inc(gathered, 1)

        @blk.scalar
        def _(act):
            for b in range(DEC):
                act.wait_ge(qrep, b + 1)
                sc(nc)(Q[:, b, :], pQ[b % 2][:, :], ACT.Copy).then_inc(qcop, 1)
            act.wait_ge(newc, 1)

            def lay(i, off):
                act.wait_ge(turned, i * 2 + (off + 1))
                sc(nc)(rows[:, 0:PAST], pR[:, :], ACT.Copy).then_inc(laid, 1)
                sc(nc)(rows[:, PAST:PAST + 1], new[:, bass.ds(i * 2 + off, 1)], ACT.Copy).then_inc(laid, 1)

            def exponent(i, off):
                act.wait_ge(maxed, i * 2 + (off + 1))
                sc(nc)(rows[:, :], rows[:, :], ACT.Exp, bias=st[:, 0:1], accum_out=st[:, 1:2]).then_inc(expd, 1)

            def weights(i, off):
                act.wait_ge(backt, i * 2 + (off + 1))
                sc(nc)(at[:, :, :], pA[:, :, :], ACT.Copy).then_inc(astep, 1)
                act.wait_ge(astep, i * 2 + (off + 1))
                sc(nc)(atn[:, :], pA1[:, 0:HA], ACT.Copy).then_inc(bcop, 1)

            def keep(i, off):
                b = off % 2
                act.wait_ge(summed, i * 2 + (off + 1))
                sc(nc)(orow[:, bass.ds(i * 2 + off, 1), :], pO[:, :].unsqueeze(1), ACT.Copy).then_inc(kept, 1)
                act.sem_inc(vfree[b], 1)

            def first(i, off):
                lay(i, off)
                exponent(i, off)

            def middle(i, off):
                weights(i, off - 1)
                lay(i, off)
                exponent(i, off)
                keep(i, off - 1)

            def last_one(i, off):
                weights(i, off)
                keep(i, off)

            sequences(act, first, middle, last_one)

        @blk.vector
        def _(dve):
            chain = Chain(dve, step)
            for e in range(2):
                chain(nc.vector.memset(qk[64 * (1 - e):64 * (1 - e) + 64, :, e, :], 0.0))
                q = slice(64 * e, 64 * e + 64)
                chain(nc.vector.tensor_tensor(qk[q, :, e, :].rearrange("p b h -> p h b"), proj[q, 14:18, zs:zs + DEC],
                                              proj[q, 18:22, zs:zs + DEC], ALU.mult))
            dve.wait_ge(pstep, 4)
            for h in range(HA):
                chain(nc.vector.tensor_scalar(bias[:, :, :, h], bias[:, :, :, h], -SLOPE[h], None, ALU.mult))
            chain(nc.vector.tensor_scalar(comb[:, :], comb0[:, :], 2.0, None, ALU.is_equal))
            chain(nc.vector.tensor_scalar(comb0[:, :], comb0[:, :], 1.0, None, ALU.is_equal))
            nc.vector.scalar_tensor_tensor(out=comb0[:, :], in0=comb[:, :], scalar=c["lam"][0:HC, 1:2], in1=comb0[:, :],
                                           op0=ALU.mult, op1=ALU.add).then_inc(prods, 1)
            dve.wait_ge(newd, 1)
            nc.vector.tensor_copy(new[:, :], pN[0:HC, 0:DEC]).then_inc(newc, 1)
            dve.wait_ge(newc, 1)
            dve.wait_ge(prods, 1)
            for b in range(2):
                dve.sem_inc(kfree[b], 1)
            dve.wait_ge(qcop, DEC)

            def product(i, off):
                b = off % 2
                dve.wait_ge(kin[b], (i + (off // 2 + 1)) * (16 * NPAGE))
                nc.vector.tensor_tensor(K[b][:, :, :], K[b][:, :, :],
                                        Q[:, bass.ds(i * 2 + off, 1), :].to_broadcast([P, NPAGE, 512]), ALU.mult).then_inc(dstep, 1)

            def reduce(i, off, n):
                b = off % 2
                dve.wait_ge(dstep, i * 6 + n)
                nc.vector.tensor_reduce(Sc[:, :, :, :].rearrange("p g e h -> p g h e"),
                                        K[b][:, :, :].rearrange("p g (h e d) -> p g h e d", h=HA, e=2), AX.X, ALU.add).then_inc(dstep, 1)

            def bias_add(i, off, n):
                b = off % 2
                dve.wait_ge(dstep, i * 6 + n)
                dve.sem_inc(kfree[b], 1)
                nc.vector.tensor_tensor(Sc[:, :, :, :], Sc[:, :, :, :], bias[:, :, :, :], ALU.add).then_inc(sdone, 1)

            def maximum(i, off):
                dve.wait_ge(laid, (i * 2 + (off + 1)) * 2)
                nc.vector.tensor_reduce(st[:, 0:1], rows[:, :], AX.X, ALU.max, negate=True).then_inc(maxed, 1)

            def scale(i, off, n):
                dve.wait_ge(expd, i * 2 + (off + 1))
                nc.vector.reciprocal(st[:, 2:3], st[:, 1:2]).then_inc(dstep, 1)
                dve.wait_ge(dstep, i * 6 + n)
                nc.vector.tensor_scalar(comb[:, :], comb0[:, :], st[:, 2:3], None, ALU.mult).then_inc(combd, 1)

            def first(i, off):
                product(i, off)
                reduce(i, off, 1)
                bias_add(i, off, 2)

            def middle(i, off):
                n = 2 + 3 * (off - 1)
                product(i, off)
                maximum(i, off - 1)
                reduce(i, off, n + 1)
                scale(i, off - 1, n + 3)
                bias_add(i, off, n + 2)

            def last_one(i, off):
                maximum(i, off)
                scale(i, off, 2 + 3 + 1)

            sequences(dve, first, middle, last_one)
            dve.wait_ge(gathered, 1)
            nc.vector.tensor_copy(oT[:, :, SEQ:TQ], pN[:, 0:HA * DEC].rearrange("p (h b) -> p h b", h=HA)).then_inc(vtab, 1)


def head_norm(nc, c, oT):
    H = TQ // 2
    with Stage(nc, "subln") as s:
        sq = s.sb("sq", [P, HA, TQ])
        pm = [s.ps(f"pm{h}", [P, 2, 512]) for h in range(HA)]
        squared, summed, root, step = (s.sem(n) for n in ("squared", "summed", "root", "step"))
        blk = s.block()
        g = PCOL["da_subln_g"]

        @blk.scalar
        def _(act):
            for h in range(HA):
                sc(nc)(sq[:, h, :], oT[:, h, :], ACT.Square).then_inc(squared, 1)
            for h in range(HA):
                act.wait_ge(summed, h + 1)
                sc(nc)(halves(sq[:, h, :]), pm[h][:, :, 0:H], ACT.Sqrt, bias=c["eps"][:, 0:1], scale=1.0 / DV).then_inc(root, 1)

        @blk.tensor
        def _(pe):
            for h in range(HA):
                pe.wait_ge(squared, h + 1)
                for a in range(2):
                    last = nc.tensor.matmul(pm[h][:, a, 0:H], c["ones"][:, :], sq[:, h, a * H:a * H + H], start=True, stop=True)
                last.then_inc(summed, 1)

        @blk.vector
        def _(dve):
            chain = Chain(dve, step)
            for h in range(HA):
                dve.wait_ge(root, h + 1)
                chain(nc.vector.reciprocal(sq[:, h, :], sq[:, h, :]))
                chain(nc.vector.scalar_tensor_tensor(out=oT[:, h, :], in0=oT[:, h, :], scalar=c["par"][:, g:g + 1], in1=sq[:, h, :],
                                                     op0=ALU.mult, op1=ALU.mult))
                chain(nc.vector.tensor_scalar(oT[:, h, :], oT[:, h, :], 1.0 - LAM_INIT, None, ALU.mult))


def split_columns(nc, x, hi, lo):
    with Stage(nc, "split") as s:
        cut = s.sem("cut")
        blk = s.block()

        @blk.scalar
        def _(act):
            for k in range(KD):
                sc(nc)(hi[:, k, :], x[:, k, :], ACT.Copy).then_inc(cut, 1)

        @blk.vector
        def _(dve):
            for k in range(KD):
                dve.wait_ge(cut, k + 1)
                nc.vector.tensor_tensor(lo[:, k, :], x[:, k, :], hi[:, k, :].bitcast(F32), ALU.subtract)


SPREAD = [(0, P), (P, P), (2 * P, P), (3 * P, P + DEC)]
TS = 2
TB = 8


def peer_choose(nc, ins, c, xn, eT):
    w = TQ // TT
    h2 = TQ // 2
    wv = ins["peer_wq"][0].rearrange("(c p) n -> p c n", p=P)
    with Stage(nc, "pick") as s:
        wt = [s.sb(f"w{b}", [P, KD, P]) for b in range(2)]
        kr = s.sb("kr", [P, 2, P])
        kT = s.sb("kT", [P, 2, P])
        qT = s.sb("qT", [P, 2, TQ])
        S = [s.sb(f"S{g}", [P, TT * 2, KEYS])[0:w] for g in range(2)]
        S2 = [s.sb(f"S2{b}", [P, KEYS])[0:w] for b in range(2)]
        v = [s.sb(f"v{g}", [P, TT, 2, TOPK])[0:w] for g in range(2)]
        ix = s.sb("ix", [P, TT, 2, TOPK], U32)[0:w]
        ixf = [s.sb(f"ixf{g}", [P, TT, 2, TOPK])[0:w] for g in range(2)]
        cand = [s.sb(f"cand{g}", [P, TT, TOPK, TOPK])[0:w] for g in range(2)]
        cand2 = [s.sb(f"cand2{b}", [P, TOPK * TOPK])[0:w] for b in range(2)]
        best = s.sb("best", [P, TT, PH, TOPK])[0:w]
        ci = s.sb("ci", [P, TT, TOPK], U32)[0:w]
        r = s.sb("r", [P, 2, TT, TOPK], U32)[0:w]
        rf = s.sb("rf", [P, 2, TT, TOPK])[0:w]
        one = [s.sb(f"one{e}", [P, TT, TOPK, TOPK])[0:w] for e in range(2)]
        ex = s.sb("ex", [P, TT, 3, PH, TOPK])[0:w]
        z = s.sb("z", [P, TT, PH])[0:w]
        acc = s.ps("acc", [P, 4, 512])
        pS = s.ps("pS", [P, 12, KEYS])
        pk = s.ps("pk", [P, 512])
        (keys, kturn, kcop, scored, copied, step, halved, paired, matched, looked, shifted, expd, chosen, turned, taken) = (
            s.sem(n) for n in ("keys", "kturn", "kcop", "scored", "copied", "step", "halved", "paired", "matched", "looked",
                               "shifted", "expd", "chosen", "turned", "taken"))
        loaded, done, queried = ([s.sem(f"{n}{e}") for e in range(2)] for n in ("loaded", "done", "queried"))
        blk = s.block()
        NEG = -3.0e38

        @blk.sync
        def _(sp):
            sp.dma_start(kr[:, :, :], ins["peer_subkeys"][0].rearrange("c k d -> k c d")).then_inc(keys, 16)
            with sp.Fori(0, PH) as i:
                for e in range(2):
                    sp.wait_ge(done[e], i + 1)
                    sp.dma_start(wt[e][:, :, :], wv[:, :, bass.ds(i * (2 * P) + e * P, P)]).then_inc(loaded[e], 16)

        @blk.tensor
        def _(pe):
            for e in range(2):
                pe.sem_inc(done[e], 1)
            pe.wait_ge(keys, 16)
            for e in range(2):
                last = nc.tensor.transpose(pk[:, e * P:(e + 1) * P], kr[:, e, :], c["ident"][:, :])
            last.then_inc(kturn, 1)
            pe.wait_ge(kcop, 1)
            with pe.Fori(0, PH) as i:
                for e in range(2):
                    pe.wait_ge(loaded[e], i * 16 + 16)
                    pe.wait_ge(queried[e], i + 1)
                    for k in range(KD):
                        for a in range(2):
                            last = nc.tensor.matmul(acc[:, 2 * e + a, 0:h2], wt[e][:, k, :], xn[:, k, a * h2:a * h2 + h2],
                                                    start=(k == 0), stop=(k == KD - 1))
                    last.then_inc(done[e], 1)
                for e in range(2):
                    pe.wait_ge(queried[e], i + 2)
                    if e == 0:
                        pe.wait_ge(copied, i + 1)
                    for j in range(TT):
                        last = nc.tensor.matmul(pS[0:w, 2 * j + e, :], qT[:, e, j * w:(j + 1) * w], kT[:, e, :],
                                                start=True, stop=True)
                last.then_inc(scored, 1)
            pe.wait_ge(chosen, 1)
            slots = acc[:, :, :].rearrange("p a (s c) -> p (a s) c", c=P)
            for q in range(3):
                for j in range(TT):
                    last = nc.tensor.transpose(slots[:, q * TT + j, 0:w], ex[:, j, q, :, :].rearrange("p h k -> p (h k)"),
                                               c["ident"][0:w, 0:w])
            last.then_inc(turned, 1)

        @blk.scalar
        def _(act):
            act.wait_ge(kturn, 1)
            sc(nc)(kT[:, :, :], pk[:, 0:2 * P].rearrange("p (e k) -> p e k", e=2), ACT.Copy).then_inc(kcop, 1)
            for e in range(2):
                act.sem_inc(queried[e], 1)
            act.sem_inc(copied, 1)
            act.sem_inc(scored, 1)
            with act.Fori(0, PH // 2) as i:
                for g in range(2):
                    act.wait_ge(scored, i * 2 + (g + 1))
                    for e in range(2):
                        act.wait_ge(done[e], i * 2 + (g + 2))
                        sc(nc)(halves3(qT[:, e:e + 1, :]), acc[:, 2 * e:2 * e + 2, 0:h2], ACT.Copy).then_inc(queried[e], 1)
                    act.wait_ge(scored, i * 2 + (g + 2))
                    act.wait_ge(halved, i * 2 + (g + 1))
                    sc(nc)(S[g][:, :, :], pS[0:w, 0:2 * TT, :], ACT.Copy).then_inc(copied, 1)
            act.wait_ge(shifted, 1)
            sc(nc)(ex[:, :, 2, :, :], ex[:, :, 2, :, :], ACT.Exp).then_inc(expd, 1)
            act.wait_ge(turned, 1)
            slots = acc[:, :, :].rearrange("p a (s c) -> p (a s) c", c=P)
            for q in range(3):
                sc(nc)(eT[:, q, :].rearrange("p (j t) -> p j t", j=TT), slots[:, q * TT:(q + 1) * TT, 0:w], ACT.Copy).then_inc(taken, 1)

        @blk.gpsimd
        def _(pool):
            def pairs(i, off):
                g = off % 2
                pool.wait_ge(halved, i * 2 + (off + 3))
                nc.gpsimd.tensor_tensor(cand[g][:, :, :, :], v[g][:, :, 0, :].unsqueeze(3).to_broadcast([w, TT, TOPK, TOPK]),
                                        v[g][:, :, 1, :].unsqueeze(2).to_broadcast([w, TT, TOPK, TOPK]), ALU.add).then_inc(paired, 1)

            def look(i, off):
                g = off % 2
                for e in range(2):
                    pool.wait_ge(matched, i * 4 + (off * 2 + e + 1))
                    nc.gpsimd.tensor_tensor(one[e][:, :, :, :], one[e][:, :, :, :],
                                            ixf[g][:, :, e, :].unsqueeze(2).to_broadcast([w, TT, TOPK, TOPK]),
                                            ALU.mult).then_inc(looked, 1)

            pairs(0, 0)
            with pool.Fori(0, PH // 2 - 1) as i:
                for off in (1, 2):
                    pairs(i, off)
                    look(i, off - 1)
            pairs(PH // 2 - 1, 1)
            look(PH // 2 - 1, 0)
            look(PH // 2 - 1, 1)

        @blk.vector
        def _(dve):
            chain = Chain(dve, step)
            dve.sem_inc(halved, 2)

            def top16(jobs):
                ops = [(lambda val, idx, src, rest: nc.vector.max(val[:, 0:8], src)),
                       (lambda val, idx, src, rest: nc.vector.max_index(idx[:, 0:8], val[:, 0:8], src)),
                       (lambda val, idx, src, rest: nc.vector.match_replace(rest, val[:, 0:8], src, NEG)),
                       (lambda val, idx, src, rest: nc.vector.max(val[:, 8:16], rest)),
                       (lambda val, idx, src, rest: nc.vector.max_index(idx[:, 8:16], val[:, 8:16], rest))]
                for op in ops:
                    for job in jobs:
                        op(*job).then_inc(step, 1)
                        chain.n += 1
                        dve.wait_ge(step, chain.n - len(jobs) + 1)
                dve.wait_ge(step, chain.n)

            def best_of_halves(h):
                g = h % 2
                dve.wait_ge(copied, h + 2)
                for j in range(TT):
                    top16([(v[g][:, j, e, :], ix[:, j, e, :], S[g][:, 2 * j + e, :], S2[e][:, :]) for e in range(2)])

            def indices(h):
                nc.vector.tensor_copy(ixf[h % 2][:, :, :, :], ix[:, :, :, :]).then_inc(halved, 1)
                dve.wait_ge(halved, h + 3)

            def key_indices(h):
                for e in range(2):
                    dve.wait_ge(looked, 2 * h + e + 1)
                    chain(nc.vector.tensor_reduce(ex[:, :, e, h, :], one[e][:, :, :, :], AX.X, ALU.add))

            best_of_halves(0)
            indices(0)
            for h in range(PH):
                g = h % 2
                if h + 1 < PH:
                    best_of_halves(h + 1)
                if h:
                    key_indices(h - 1)
                if h + 1 < PH:
                    indices(h + 1)
                dve.wait_ge(paired, h + 1)
                for js in ((0, 1), (2, 3), (4,)):
                    top16([(best[:, j, h, :], ci[:, j, :], cand[g][:, j, :, :].rearrange("p a b -> p (a b)"), cand2[j % 2][:, :])
                           for j in js])
                chain(nc.vector.tensor_scalar(r[:, 0, :, :], ci[:, :, :], 4, None, ALU.logical_shift_right))
                chain(nc.vector.tensor_scalar(r[:, 1, :, :], ci[:, :, :], TOPK - 1, None, ALU.bitwise_and))
                chain(nc.vector.tensor_copy(rf[:, :, :, :], r[:, :, :, :]))
                iota = c["iota"][0:w, 0:TOPK].unsqueeze(1).to_broadcast([w, TT * TOPK, TOPK])
                for e in range(2):
                    pick = rf[:, e, :, :].rearrange("p j a -> p (j a)").unsqueeze(2).to_broadcast([w, TT * TOPK, TOPK])
                    nc.vector.tensor_tensor(one[e][:, :, :, :].rearrange("p j a b -> p (j a) b"), pick, iota,
                                            ALU.is_equal).then_inc(matched, 1)
            nc.vector.tensor_tensor(ex[:, :, 2, :, :], best[:, :, :, :], best[:, :, :, 0:1].to_broadcast([w, TT, PH, TOPK]),
                                    ALU.subtract).then_inc(shifted, 1)
            key_indices(PH - 1)
            dve.wait_ge(expd, 1)
            chain(nc.vector.tensor_reduce(z[:, :, :], ex[:, :, 2, :, :], AX.X, ALU.add))
            chain(nc.vector.reciprocal(z[:, :, :], z[:, :, :]))
            nc.vector.tensor_tensor(ex[:, :, 2, :, :], ex[:, :, 2, :, :], z[:, :, :].unsqueeze(3).to_broadcast([w, TT, PH, TOPK]),
                                    ALU.mult).then_inc(chosen, 1)


def peer_spread(nc, c, eT, mscr):
    NG = TB // TS
    with Stage(nc, "spread") as s:
        M = [s.sb(f"M{b}", [P, KEYS, P + DEC]) for b in range(2)]
        et = s.sb("et", [P, 3, TB])
        e1 = s.sb("e1", [P, 1, TB])
        e1used = s.sb("e1used", [P, NG])
        A = [s.sb(f"A{g}", [P, TS, KEYS]) for g in range(NG)]
        B = [s.sb(f"B{g}", [P, TS, KEYS]) for g in range(NG)]
        pm = [s.ps(f"pm{g}", [P, 4, KEYS])[:, 0:TS, :] for g in range(NG)]
        estep, e1step, hot, first_hot, ready = (s.sem(n) for n in ("estep", "e1step", "hot", "first_hot", "ready"))
        done, out = ([s.sem(f"{n}{g}") for g in range(NG)] for n in ("done", "out"))
        stored = [s.sem(f"stored{b}") for b in range(2)]
        blk = s.block()

        @blk.sync
        def _(sp):
            for n, (t0, w) in enumerate(SPREAD):
                sp.wait_ge(ready, n + 1)
                sp.dma_start(mscr[:, :, t0:t0 + w], M[n % 2][:, :, 0:w]).then_inc(stored[n % 2], 16)
            for b in range(2):
                sp.wait_ge(stored[b], 16 * len(SPREAD) // 2)

        @blk.tensor
        def _(pe):
            for g in range(NG):
                pe.sem_inc(done[g], 1)
            with pe.Fori(0, TQ // TB) as i:
                for g in range(NG):
                    pe.wait_ge(hot, i * NG + (g + 2))
                    if g % 2:
                        pe.wait_ge(first_hot, i * (NG // 2) + (g // 2 + 2))
                    pe.wait_ge(out[g], i + 1)
                    for t in range(TS):
                        last = nc.tensor.matmul(pm[g][:, t, :], A[g][:, t, :], B[g][:, t, :], start=True, stop=True)
                    last.then_inc(done[g], 1)

        @blk.scalar
        def _(act):
            for g in range(NG):
                act.sem_inc(out[g], 1)
            for n, (t0, w) in enumerate(SPREAD):
                if n >= 2:
                    act.wait_ge(stored[n % 2], 16 * (n // 2))
                with act.Fori(t0 // TB, (t0 + w) // TB) as i:
                    for g in range(NG):
                        act.wait_ge(done[g], i + 2)
                        at = bass.ds(i * TB + (g * TS - t0), TS)
                        sc(nc)(M[n % 2][:, :, at].rearrange("p e t -> p t e"), pm[g][:, :, :], ACT.Copy).then_inc(out[g], 1)
                for g in range(NG):
                    act.wait_ge(out[g], (t0 + w) // TB + 1)
                act.sem_inc(ready, 1)

        @blk.gpsimd
        def _(pool):
            pool.sem_inc(first_hot, 1)
            with pool.Fori(0, TQ // TB) as i:
                pool.wait_ge(first_hot, i * (NG // 2) + 1)
                nc.gpsimd.tensor_copy(e1[:, :, :], eT[:, 0:1, bass.ds(i * TB, TB)]).then_inc(e1step, 1)
                for g in range(1, NG, 2):
                    if g == 1:
                        pool.wait_ge(e1step, i + 1)
                    pool.wait_ge(done[g], i + 1)
                    nc.gpsimd.tensor_tensor(e1used[:, g:g + 1], c["iota"][:, 0:1], c["iota"][:, 0:1], ALU.add)
                    for t in range(TS):
                        q = g * TS + t
                        last = nc.gpsimd.tensor_scalar(A[g][:, t, :], c["iota"][:, :], e1[:, 0, q:q + 1], None, ALU.is_equal)
                    last.then_inc(first_hot, 1)

        @blk.vector
        def _(dve):
            dve.sem_inc(hot, 1)
            with dve.Fori(0, TQ // TB) as i:
                dve.wait_ge(hot, i * NG + 1)
                nc.vector.tensor_copy(et[:, :, :], eT[:, :, bass.ds(i * TB, TB)]).then_inc(estep, 1)
                dve.wait_ge(estep, i + 1)
                for g in range(NG):
                    dve.wait_ge(done[g], i + 1)
                    for t in range(TS):
                        q = g * TS + t
                        if g % 2 == 0:
                            nc.vector.tensor_scalar(A[g][:, t, :], c["iota"][:, :], et[:, 0, q:q + 1], None, ALU.is_equal)
                        last = nc.vector.tensor_scalar(B[g][:, t, :], c["iota"][:, :], et[:, 1, q:q + 1], et[:, 2, q:q + 1],
                                                       ALU.is_equal, ALU.mult)
                    last.then_inc(hot, 1)


def peer_experts(nc, ins, c, xh, xl, mscr, acc):
    H = TQ // 2
    NQ = KEYS // 2
    uv = ins["peer_u"][0].rearrange("(a b) d -> a b d", b=KEYS)
    vv = ins["peer_v"][0].rearrange("(a b) d -> a b d", b=KEYS)
    with Stage(nc, "experts") as s:
        U = [s.sb(f"U{b}", [P, 2, D]) for b in range(2)]
        V = [s.sb(f"V{b}", [P, 2, D]) for b in range(2)]
        M = [s.sb(f"M{b}", [P, 2, TQ]) for b in range(2)]
        UH = [s.sb(f"UH{e}", [P, KD, P], F32R) for e in range(2)]
        UL = [s.sb(f"UL{e}", [P, KD, P], F32R) for e in range(2)]
        VH = [s.sb(f"VH{b}", [P, 2, D], F32R) for b in range(2)]
        VL = [s.sb(f"VL{b}", [P, 2, D], F32R) for b in range(2)]
        G = [s.sb(f"G{e}", [P, TQ]) for e in range(2)]
        GH = [s.sb(f"GH{b}", [P, 2, TQ], F32R) for b in range(2)]
        GL = [s.sb(f"GL{b}", [P, 2, TQ], F32R) for b in range(2)]
        pU = [s.ps(f"pU{a}", [P, 4, P]) for a in range(2)]
        pH = [s.ps(f"pH{a}", [P, 512]) for a in range(2)]
        pV = [s.ps(f"pV{a}", [P, 512]) for a in range(4)]
        u_in, v_in, m_in = ([s.sem(f"{n}{b}") for b in range(2)] for n in ("u_in", "v_in", "m_in"))
        turned, u_hi, u_lo, hidden, gelued, gated, g_hi, g_lo, v_hi, v_lo, summed, added = (
            s.sem(n) for n in ("turned", "u_hi", "u_lo", "hidden", "gelued", "gated", "g_hi", "g_lo", "v_hi", "v_lo",
                               "summed", "added"))
        blk = s.block()

        class Pair:

            def __init__(self, off, i=None):
                self.off, self.i, self.b = off, i, off % 2

            def count(self, per, n):
                return per * self.off + n if self.i is None else self.i * (2 * per) + (per * self.off + n)

            def loads(self):
                return 16 * (self.off // 2 + 1) if self.i is None else self.i * 16 + 16 * (self.off // 2 + 1)

            def after(self, n):
                return self.i is not None or self.off >= n

        def schedule(eng, first, body, tail):
            first()
            with eng.Fori(0, NQ // 2 - 1) as i:
                for off in range(2):
                    body(Pair(off, i), Pair(off + 1, i), Pair(off + 2, i))
            tail()

        def load(sp, q):
            k = q.b
            at = bass.ds(q.count(2, 0), 2)
            if q.after(2):
                sp.wait_ge(turned, q.count(4, -4))
            sp.dma_start(U[k][:, :, :], uv[:, at, :]).then_inc(u_in[k], 16)
            if q.after(2):
                sp.wait_ge(gated, q.count(2, -2))
            sp.dma_start(M[k][:, :, :], mscr[:, at, :]).then_inc(m_in[k], 16)
            if q.after(2):
                sp.wait_ge(v_lo, q.count(1, -1))
            sp.dma_start(V[k][:, :, :], vv[:, at, :]).then_inc(v_in[k], 16)

        @blk.sync
        def _(sp):
            schedule(sp, lambda: (load(sp, Pair(0)), load(sp, Pair(1))), lambda p, q, r: load(sp, r), lambda: None)

        def turn(pe, q, st):
            e, a = st // 2, st % 2
            if st == 0:
                pe.wait_ge(u_in[q.b], q.loads())
            if q.after(1) or st >= 2:
                pe.wait_ge(u_lo, q.count(4, st - 1))
            for k in range(4):
                last = nc.tensor.transpose(pU[a][:, k, :], U[q.b][:, e, (4 * a + k) * P:(4 * a + k + 1) * P], c["ident"][:, :])
            last.then_inc(turned, 1)

        def product_u(pe, q):
            for e in range(2):
                pe.wait_ge(u_lo, q.count(4, 2 * e + 2))
                for a in range(2):
                    if q.after(1) or e:
                        pe.wait_ge(gelued, q.count(4, 2 * e + a - 1))
                    ts = slice(a * H, (a + 1) * H)
                    for k in range(KD):
                        for n, (u, x) in enumerate(((UH, xh), (UH, xl), (UL, xh))):
                            last = nc.tensor.matmul(pH[a][:, 0:H], u[e][:, k, :], x[:, k, ts], start=(k == 0 and n == 0),
                                                    stop=(k == KD - 1 and n == 2))
                    last.then_inc(hidden, 1)

        def product_v(pe, q, n):
            k, a = n // 2, n % 2
            if n == 0:
                pe.wait_ge(v_lo, q.count(1, 1))
                pe.wait_ge(g_lo, q.count(2, 2))
            pe.wait_ge(added, q.count(16, n + 1))
            ts = slice(a * H, (a + 1) * H)
            terms = [(v[q.b][:, e, k * P:(k + 1) * P], g[q.b][:, e, ts]) for e in range(2) for v, g in ((VH, GH), (VH, GL), (VL, GH))]
            for t, (l, r) in enumerate(terms):
                last = nc.tensor.matmul(pV[n % 4][:, 0:H], l, r, start=(t == 0), stop=(t == 5))
            last.then_inc(summed, 1)

        @blk.tensor
        def _(pe):
            def first():
                for st in range(4):
                    turn(pe, Pair(0), st)
                product_u(pe, Pair(0))
                for st in range(4):
                    turn(pe, Pair(1), st)

            def body(p, q, r):
                product_u(pe, q)
                for n in range(16):
                    if n % 4 == 0:
                        turn(pe, r, n // 4)
                    product_v(pe, p, n)

            def tail():
                product_u(pe, Pair(NQ - 1))
                for p in (NQ - 2, NQ - 1):
                    for n in range(16):
                        product_v(pe, Pair(p), n)

            schedule(pe, first, body, tail)

        def cut_u(act, q, st):
            e, a = st // 2, st % 2
            act.wait_ge(turned, q.count(4, st + 1))
            if q.after(1):
                act.wait_ge(hidden, q.count(4, 2 * e - 2))
            sc(nc)(UH[e][:, 4 * a:4 * a + 4, :], pU[a][:, :, :], ACT.Copy).then_inc(u_hi, 1)

        def cut_v(act, q):
            act.wait_ge(v_in[q.b], q.loads())
            if q.after(2):
                act.wait_ge(summed, q.count(16, -16))
            sc(nc)(VH[q.b][:, :, :], V[q.b][:, :, :], ACT.Copy).then_inc(v_hi, 1)

        def gelu(act, q, e):
            for a in range(2):
                act.wait_ge(hidden, q.count(4, 2 * e + a + 1))
                if q.after(1):
                    act.wait_ge(g_lo, q.count(2, e - 1))
                sc(nc)(G[e][:, a * H:(a + 1) * H], pH[a][:, 0:H], ACT.Gelu).then_inc(gelued, 1)

        def cut_g(act, q, e):
            act.wait_ge(gated, q.count(2, e + 1))
            if q.after(2):
                act.wait_ge(summed, q.count(16, -16))
            sc(nc)(GH[q.b][:, e, :], G[e][:, :], ACT.Copy).then_inc(g_hi, 1)

        @blk.scalar
        def _(act):
            def hidden_values(q):
                gelu(act, q, 0)
                cut_v(act, q)
                cut_g(act, q, 0)
                gelu(act, q, 1)

            def first():
                for st in range(4):
                    cut_u(act, Pair(0), st)
                hidden_values(Pair(0))
                cut_g(act, Pair(0), 1)
                for st in range(4):
                    cut_u(act, Pair(1), st)

            def body(p, q, r):
                hidden_values(q)
                cut_u(act, r, 0)
                cut_g(act, q, 1)
                for st in range(1, 4):
                    cut_u(act, r, st)

            def tail():
                hidden_values(Pair(NQ - 1))
                cut_g(act, Pair(NQ - 1), 1)

            schedule(act, first, body, tail)

        def rest_g(pool, q, e):
            pool.wait_ge(g_hi, q.count(2, e + 1))
            nc.gpsimd.tensor_tensor(GL[q.b][:, e, :], G[e][:, :], GH[q.b][:, e, :].bitcast(F32), ALU.subtract).then_inc(g_lo, 1)

        def rest_v(pool, q):
            pool.wait_ge(v_hi, q.count(1, 1))
            nc.gpsimd.tensor_tensor(VL[q.b][:, :, :], V[q.b][:, :, :], VH[q.b][:, :, :].bitcast(F32), ALU.subtract).then_inc(v_lo, 1)

        @blk.gpsimd
        def _(pool):
            def all_of(q):
                rest_v(pool, q)
                rest_g(pool, q, 0)
                rest_g(pool, q, 1)

            schedule(pool, lambda: all_of(Pair(0)), lambda p, q, r: all_of(q), lambda: all_of(Pair(NQ - 1)))

        def rest_u(dve, q, st):
            e, a = st // 2, st % 2
            dve.wait_ge(u_hi, q.count(4, st + 1))
            nc.vector.tensor_tensor(UL[e][:, 4 * a:4 * a + 4, :], pU[a][:, :, :], UH[e][:, 4 * a:4 * a + 4, :].bitcast(F32),
                                    ALU.subtract).then_inc(u_lo, 1)

        def gate(dve, q, e):
            dve.wait_ge(m_in[q.b], q.loads())
            dve.wait_ge(gelued, q.count(4, 2 * e + 2))
            nc.vector.tensor_tensor(G[e][:, :], G[e][:, :], M[q.b][:, e, :], ALU.mult).then_inc(gated, 1)

        def add(dve, q, n):
            k, a = n // 2, n % 2
            dve.wait_ge(summed, q.count(16, n + 1))
            nc.vector.tensor_tensor(acc[:, k, a * H:(a + 1) * H], pV[n % 4][:, 0:H], acc[:, k, a * H:(a + 1) * H],
                                    ALU.add).then_inc(added, 1)

        @blk.vector
        def _(dve):
            def first():
                dve.sem_inc(added, 4)
                for st in range(4):
                    rest_u(dve, Pair(0), st)
                for e in range(2):
                    gate(dve, Pair(0), e)
                for st in range(4):
                    rest_u(dve, Pair(1), st)

            def body(p, q, r):
                for e in range(2):
                    gate(dve, q, e)
                for n in range(16):
                    if n % 4 == 0:
                        rest_u(dve, r, n // 4)
                    add(dve, p, n)

            def tail():
                for e in range(2):
                    gate(dve, Pair(NQ - 1), e)
                for p in (NQ - 2, NQ - 1):
                    for n in range(16):
                        add(dve, Pair(p), n)

            schedule(dve, first, body, tail)


def store_rows(nc, c, acc, outs):
    with Stage(nc, "store") as s:
        rows = [s.sb(f"rows{b}", [P, D]) for b in range(2)]
        pt = [s.ps(f"pt{b}", [P, 4, P]) for b in range(4)]
        turned, copied, stored = s.sem("turned"), s.sem("copied"), [s.sem(f"stored{b}") for b in range(2)]
        blk = s.block()

        @blk.tensor
        def _(pe):
            for n in range(2 * TT):
                j, half = n // 2, n % 2
                w = min(P, TQ - j * P)
                if n >= 4:
                    pe.wait_ge(copied, n - 3)
                for q in range(4):
                    last = nc.tensor.transpose(pt[n % 4][0:w, q, :], acc[:, 4 * half + q, j * P:j * P + w], c["ident"][:, :])
                last.then_inc(turned, 1)

        @blk.vector
        def _(dve):
            for n in range(2 * TT):
                j, half = n // 2, n % 2
                w = min(P, TQ - j * P)
                dve.wait_ge(turned, n + 1)
                if j >= 2:
                    dve.wait_ge(stored[j % 2], 16 * (j // 2))
                nc.vector.tensor_copy(rows[j % 2][0:w, 512 * half:512 * half + 512].rearrange("p (q d) -> p q d", q=4),
                                      pt[n % 4][0:w, :, :]).then_inc(copied, 1)

        @blk.sync
        def _(sp):
            for j in range(TT):
                sp.wait_ge(copied, 2 * j + 2)
                if j < 4:
                    dst = outs["y_prompt"][0, j * P:(j + 1) * P, :]
                    sp.dma_start(dst, rows[j % 2][:, :]).then_inc(stored[j % 2], 16)
                else:
                    sp.dma_start(outs["y_sample"][:, 0, :], rows[j % 2][0:DEC, :]).then_inc(stored[j % 2], 16)
            sp.wait_ge(stored[0], 48)
            sp.wait_ge(stored[1], 32)


def hybrid_step(nc, ins, outs, scr):
    def act_copy(dst):
        return lambda eng, i, b, p, tmp: sc(nc)(halves3(dst(i * 2 + b)), p, ACT.Copy)

    with ExitStack() as whole:
        def open_in(ctx):
            g = Stage(nc, "keep")
            ctx.enter_context(g)
            return g

        g = open_in(whole)
        c = constants(nc, g, ins)
        xT = g.sb("xT", [P, KD, T])
        xn = g.sb("xn", [P, KD, T])
        mixed = xn[:, :, 0:TQ]
        acc = xT[:, :, META:T]
        with ExitStack() as inner:
            b = open_in(inner)
            yo = b.sb("yo", [P, RB, TQ])
            oT = b.sb("oT", [P, HA, TQ])
            with ExitStack() as mixers:
                m = open_in(mixers)
                proj = m.sb("proj", [P, RWT + 2 * HA, TW])
                load_tokens(nc, ins, c, xT)
                channel_norm(nc, "norm1", c, xT, 0, T, PCOL["norm1_g"], xn)
                linear(nc, "inp", ins["w_in"][0], 0, RWT + 2 * HA, xn, 0, KD, T, "scalar",
                       act_copy(lambda n: proj[:, bass.ds(n, 1), PAD:TW]))
                shift_mix(nc, ins, c, proj, outs)
                with ExitStack() as rwkv:
                    r = open_in(rwkv)
                    rw = {n: r.sb(n, [P, RB, TW]) for n in ("lw", "L", "la", "kk", "b", "g")}
                    rw["bonus"] = r.sb("bonus", [P, RB, T])
                    yT = r.sb("yT", [P, RB, TW])
                    rwkv_prepare(nc, ins, c, proj, rw)
                    rwkv_chunks(nc, c, proj, rw, yT, outs)
                    rwkv_sample(nc, c, proj, rw, yT, ins, outs, scr)
                    rwkv_output(nc, c, rw, yT, yo)
                v_tok = m.sb("v_tok", [P, TT, 512])
                project_values(nc, ins, xn, v_tok, outs, scr["v"])
                qk_norm(nc, c, proj, outs)
                attend_prompt(nc, c, proj, v_tok, oT)
                attend_sample(nc, ins, c, proj, oT, scr["v"])
            head_norm(nc, c, oT)
            gates = b.sb("gates", [P, 2 * KD, TQ])
            linear(nc, "gate", ins["w_in"][0], RW_PROJ + 3 * 512, 2 * KD, xn, META, KD, TQ, "scalar",
                   lambda eng, i, b, p, tmp: sc(nc)(halves3(gates[:, bass.ds(i * 2 + b, 1), :]), p, ACT.Sigmoid))
            linear(nc, "rwbr", ins["w_rw_br"][0], 0, KD, yo, 0, RB, TQ, "vector",
                   lambda eng, i, b, p, tmp: nc.vector.tensor_tensor(halves3(mixed[:, bass.ds(i * 2 + b, 1), :]), p,
                                                                     halves3(gates[:, bass.ds(i * 2 + b, 1), :]), ALU.mult))

            def add_branch(eng, i, b, p, tmp):
                t, sem = tmp
                gate = halves3(gates[:, bass.ds(i * 2 + (KD + b), 1), :])
                nc.vector.tensor_tensor(t[b][:, :, :], p, gate, ALU.mult).then_inc(sem, 1)
                eng.wait_ge(sem, i * 2 + b + 1)
                dst = halves3(mixed[:, bass.ds(i * 2 + b, 1), :])
                return nc.vector.tensor_tensor(dst, t[b][:, :, :], dst, ALU.add)

            linear(nc, "dabr", ins["w_da_br"][0], 0, KD, oT, 0, HA, TQ, "vector", add_branch,
                   extra=lambda s: ([s.sb(f"t{b}", [P, 2, TQ // 2]) for b in range(2)], s.sem("gated")))

        def add_residual(eng, i, b, p, tmp):
            return nc.vector.tensor_tensor(halves3(acc[:, bass.ds(i * 2 + b, 1), :]), p,
                                           halves3(xT[:, bass.ds(i * 2 + b, 1), META:T]), ALU.add)

        linear(nc, "out", ins["w_out"][0], 0, KD, mixed, 0, KD, TQ, "vector", add_residual)
        channel_norm(nc, "norm2", c, acc, 0, TQ, PCOL["norm2_g"], mixed)
        with ExitStack() as inner:
            b = open_in(inner)
            eT = b.sb("eT", [P, 3, TQ])
            peer_choose(nc, ins, c, mixed, eT)
            peer_spread(nc, c, eT, scr["gates"])
        with ExitStack() as inner:
            b = open_in(inner)
            xh = b.sb("xh", [P, KD, TQ], F32R)
            xl = b.sb("xl", [P, KD, TQ], F32R)
            split_columns(nc, mixed, xh, xl)
            peer_experts(nc, ins, c, xh, xl, scr["gates"], acc)
        store_rows(nc, c, acc, outs)


_INS = ["x_prompt", "x_sample", "cache_k", "cache_v", "state_wkv", "state_shift", "page_table", "meta", "norm1_g", "w_in",
        "rw_mu", "rw_w0", "rw_w2", "rw_a0", "rw_a2", "rw_g2", "rw_kk", "rw_ka", "rw_rk", "rw_ln_g", "rw_ln_b", "w_rw_br",
        "da_qn_g", "da_kn_g", "da_lam", "da_subln_g", "w_da_br", "w_out", "norm2_g", "peer_wq", "peer_subkeys", "peer_u",
        "peer_v"]
_OUTS = {"y_prompt": (1, SEQ, D), "y_sample": (DEC, 1, D), "k_prompt": (1, 1, NP_, HA, 2, 64), "v_prompt": (1, 1, NP_, HA, DV),
         "k_sample": (1, DEC, 1, HA, 2, 64), "v_sample": (1, DEC, 1, HA, DV), "wkv_prompt": (1, 1, 8, 64, 64),
         "wkv_sample": (1, DEC, 8, 64, 64), "shift_prompt": (1, 1, RW_PROJ), "shift_sample": (1, DEC, RW_PROJ)}
_SCRATCH = {"vec": (6, DEC, RW_DIM), "y": (DEC, RW_DIM), "v": (DEC, 512),
            "gates": (KEYS, KEYS, TQ)}


def kernel(**inputs):
    import numpy as _np
    import concourse.bacc as _bacc
    from concourse import mybir as _mybir
    from concourse.bass_utils import run_bass_kernel_spmd as _run

    nc = _bacc.Bacc("TRN2", target_bir_lowering=False, num_devices=1)
    arrays, ins, outs, scr = {}, {}, {}, {}
    for name in _INS:
        a = _np.ascontiguousarray(inputs[name])
        arrays[f"in_{name}"] = a
        ins[name] = nc.dram_tensor(f"in_{name}", a.shape, _mybir.dt.from_np(a.dtype), kind="ExternalInput").ap()
    for name, shape in _OUTS.items():
        outs[name] = nc.dram_tensor(f"out_{name}", shape, F32, kind="ExternalOutput").ap()
    for name, shape in _SCRATCH.items():
        scr[name] = nc.dram_tensor(f"scratch_{name}", shape, F32, kind="Internal").ap()
    hybrid_step(nc, ins, outs, scr)
    r = _run(nc, [arrays], core_ids=[0])
    return tuple(r.results[0][f"out_{name}"] for name in _OUTS)
```

```python
import math
from contextlib import ExitStack

import concourse.bass as bass
from concourse import mybir

F32 = mybir.dt.float32
F32R = mybir.dt.float32r
U32 = mybir.dt.uint32
I32 = mybir.dt.int32
ALU = mybir.AluOpType
ACT = mybir.ActivationFunctionType
AX = mybir.AxisListType

P = 128
D = 1024
KD = D // P
META, SEQ, DEC = 16, 512, 8
NP_ = META + SEQ
T = NP_ + DEC
TQ = SEQ + DEC
TT = 5
RW_HEAD, RW_DIM, RW_PROJ = 64, 512, 1792
RB = RW_DIM // P
RWT = RW_PROJ // P
C = 64
PAD = C - META
NCH = (PAD + NP_) // C
TW = PAD + T
HA, DV = 4, 128
PAGE, NPAGE, PAST = 128, 8, 1024
HC = 2 * HA
PH, TOPK, KEYS = 8, 16, 128
SLOPE = [2.0 ** (-8.0 * (h + 1) / HA) for h in range(HA)]
LAM_INIT = 0.8 - 0.6 * math.exp(-0.3 * 0)
EPS, LN_EPS = 1e-6, 64e-5
MASKED = 1e30
LEVELS = [1, 2, 4, 8, 16, 32]

PARAMS = [("norm1_g", 8), ("norm2_g", 8), ("rw_mu", RWT), ("rw_w0", RB), ("rw_a0", RB), ("rw_kk", RB),
          ("rw_ka", RB), ("rw_rk", RB), ("rw_ln_g", RB), ("rw_ln_b", RB), ("da_subln_g", 1),
          ("da_qn_g", 1), ("da_kn_g", 1)]
PCOL = {}
for _name, _n in PARAMS:
    PCOL[_name] = sum(n for m, n in PARAMS[:len(PCOL)])
NPAR = sum(n for _, n in PARAMS)


class Stage:

    def __init__(self, nc, name):
        self.nc, self.name, self.ctx, self.sems = nc, name, ExitStack(), []

    def __enter__(self):
        self.ctx.__enter__()
        return self

    def __exit__(self, *e):
        self.ctx.__exit__(*e)
        for sem in self.sems:
            self.nc.sync.sem_clear(sem)

    def sb(self, name, shape, dt=F32):
        return self.ctx.enter_context(self.nc.sbuf_tensor(f"{self.name}_{name}", shape, dt))

    def ps(self, name, shape, dt=F32):
        return self.ctx.enter_context(self.nc.psum_tensor(f"{self.name}_{name}", shape, dt))

    def sem(self, name):
        self.sems.append(self.ctx.enter_context(self.nc.semaphore(f"{self.name}_{name}")))
        return self.sems[-1]

    def block(self):
        return self.ctx.enter_context(self.nc.Block())


class Chain:

    def __init__(self, eng, sem, i=None, per=0):
        self.eng, self.sem, self.n, self.i, self.per = eng, sem, 0, i, per

    def at(self, n):
        return n if self.i is None else self.i * self.per + n

    def __call__(self, ins):
        ins.then_inc(self.sem, 1)
        self.n += 1
        self.eng.wait_ge(self.sem, self.at(self.n))
        return self.n

    def end(self):
        assert self.i is None or self.n == self.per, (self.n, self.per)


def sc(nc):
    return nc.scalar.activation


def constants(nc, g, ins):
    c = {}
    for name, shape in (("ident", [P, P]), ("ones", [P, P]), ("bd", [P, P]), ("iota", [P, P]),
                        ("um", [P, C]), ("ui", [P, C]), ("lmt", [P, len(LEVELS), C]), ("m1", [P, C]),
                        ("ident2", [P, C]), ("par", [P, NPAR]), ("eps", [P, 2]), ("lam", [P, 2])):
        c[name] = g.sb(name, shape)
    with Stage(nc, "const") as s:
        rows = s.sb("rows", [P, P])
        lv = s.sb("lv", [P, 4, 64])
        pr = s.sb("pr", [P, 2, 64])
        ls = s.sb("ls", [P, 2])
        pt = s.ps("pt", [P, P])
        params, lams, made, step = s.sem("params"), s.sem("lams"), s.sem("made"), s.sem("step")
        turned, dots, exps = s.sem("turned"), s.sem("dots"), s.sem("exps")
        nload = len(PARAMS) + 2

        blk = s.block()

        @blk.sync
        def _(sp):
            for name, n in PARAMS:
                src = ins[name]
                r = PCOL[name]
                if name in ("da_qn_g", "da_kn_g"):
                    sp.dma_start(rows[r:r + 1, 0:64], src).then_inc(params, 16)
                    sp.dma_start(rows[r:r + 1, 64:128], src).then_inc(params, 16)
                elif name == "rw_rk":
                    sp.dma_start(rows[r:r + n, :], src.rearrange("o (m h) k -> (o m) (h k)", h=2)).then_inc(params, 16)
                else:
                    sp.dma_start(rows[r:r + n, :], src.rearrange("o (m p) -> (o m) p", p=P)).then_inc(params, 16)
            sp.dma_start(lv[:, :, :], ins["da_lam"].to_broadcast([P, 4, 64])).then_inc(lams, 16)

        @blk.gpsimd
        def _(pool):
            chain = Chain(pool, step)
            chain(nc.gpsimd.memset(c["ident"][:, :], 0.0))
            chain(nc.gpsimd.affine_select(out=c["ident"][:, :], in_=c["ident"][:, :], compare_op=ALU.not_equal,
                                          fill=1.0, base=0, pattern=[[-1, P]], channel_multiplier=1))
            chain(nc.gpsimd.iota(c["iota"][:, :], pattern=[[1, P]], base=0, channel_multiplier=0,
                                 allow_small_or_imprecise_dtypes=True))
            chain(nc.gpsimd.memset(c["ones"][:, :], 1.0))
            chain(nc.gpsimd.memset(c["bd"][:, :], 0.0))
            chain(nc.gpsimd.memset(c["lmt"][:, :, :], 0.0))
            chain(nc.gpsimd.memset(c["m1"][:, :], 0.0))
            for b in (0, 64):
                q = slice(b, b + 64)
                one = c["ones"][q, 0:C]
                chain(nc.gpsimd.memset(c["bd"][q, q], 1.0))
                for m, op, st, cm in (("um", ALU.is_gt, 1, -1), ("ui", ALU.is_ge, 1, -1), ("ident2", ALU.is_equal, 1, -1)):
                    chain(nc.gpsimd.affine_select(out=c[m][q, :], in_=one, compare_op=op, fill=0.0, base=0,
                                                  pattern=[[st, C]], channel_multiplier=cm))
                for n, z in enumerate(LEVELS):
                    v = c["lmt"][q, n, :].rearrange("p (b o z) -> p b o z", o=2, z=z)[:, :, 1, :]
                    o = one.rearrange("p (b o z) -> p b o z", o=2, z=z)[:, :, 1, :]
                    nb = C // (2 * z)
                    chain(nc.gpsimd.affine_select(out=v, in_=o, compare_op=ALU.is_ge, fill=0.0, base=0,
                                                  pattern=[[-2 * z, nb], [0, z]], channel_multiplier=1))
                    chain(nc.gpsimd.affine_select(out=v, in_=v, compare_op=ALU.is_ge, fill=0.0, base=z - 1,
                                                  pattern=[[2 * z, nb], [0, z]], channel_multiplier=-1))
                v = c["m1"][q, :].rearrange("p (b o) -> p b o", o=2)[:, :, 0]
                o = one.rearrange("p (b o) -> p b o", o=2)[:, :, 0]
                chain(nc.gpsimd.affine_select(out=v, in_=o, compare_op=ALU.is_equal, fill=0.0, base=-1,
                                              pattern=[[-2, C // 2]], channel_multiplier=1))
            chain(nc.gpsimd.memset(c["eps"][:, 0:1], EPS))
            nc.gpsimd.memset(c["eps"][:, 1:2], LN_EPS).then_inc(made, 1)

        @blk.vector
        def _(dve):
            chain = Chain(dve, dots)
            dve.wait_ge(lams, 16)
            l4 = lv[:, :, :].rearrange("p (a b) k -> p a b k", b=2)
            chain(nc.vector.tensor_tensor(pr[:, :, :], l4[:, :, 0, :], l4[:, :, 1, :], ALU.mult))
            chain(nc.vector.tensor_reduce(ls[:, :], pr[:, :, :], AX.X, ALU.add))
            dve.wait_ge(exps, 1)
            chain(nc.vector.tensor_tensor(c["lam"][:, 0:1], ls[:, 0:1], ls[:, 1:2], ALU.subtract))
            chain(nc.vector.tensor_scalar(c["lam"][:, 0:1], c["lam"][:, 0:1], LAM_INIT, None, ALU.add))
            chain(nc.vector.tensor_scalar(c["lam"][:, 1:2], c["lam"][:, 0:1], -1.0, None, ALU.mult))
            dve.wait_ge(turned, 1)
            nc.vector.tensor_copy(c["par"][:, :], pt[:, 0:NPAR]).then_inc(dots, 1)

        @blk.scalar
        def _(act):
            act.wait_ge(dots, 2)
            sc(nc)(ls[:, :], ls[:, :], ACT.Exp).then_inc(exps, 1)

        @blk.tensor
        def _(pe):
            pe.wait_ge(params, 16 * nload)
            pe.wait_ge(made, 1)
            nc.tensor.transpose(pt[:, 0:NPAR], rows[0:NPAR, :], c["ident"][0:NPAR, 0:NPAR]).then_inc(turned, 1)
    return c


def load_tokens(nc, ins, c, xT):
    with Stage(nc, "load") as s:
        xt = s.sb("xt", [P, TT, D])
        pt = [s.ps(f"pt{b}", [P, 4, P]) for b in range(4)]
        rows, turned, copied = s.sem("rows"), s.sem("turned"), s.sem("copied")
        blk = s.block()
        xp, xs, me = ins["x_prompt"][0], ins["x_sample"][:, 0, :], ins["meta"]

        @blk.sync
        def _(sp):
            sp.dma_start(xt[0:META, 0, :], me).then_inc(rows, 16)
            sp.dma_start(xt[META:P, 0, :], xp[0:P - META, :]).then_inc(rows, 16)
            sp.dma_start(xt[:, 1:4, :], xp[P - META:4 * P - META, :].rearrange("(j p) d -> p j d", p=P)).then_inc(rows, 16)
            sp.dma_start(xt[0:META, 4, :], xp[4 * P - META:SEQ, :]).then_inc(rows, 16)
            sp.dma_start(xt[META:META + DEC, 4, :], xs).then_inc(rows, 16)

        @blk.tensor
        def _(pe):
            pe.wait_ge(rows, 5 * 16)
            for n in range(2 * TT):
                j, half = n // 2, n % 2
                w = min(P, T - P * j)
                if n >= 4:
                    pe.wait_ge(copied, n - 3)
                for q in range(4):
                    last = nc.tensor.transpose(pt[n % 4][:, q, 0:w], xt[0:w, j, (4 * half + q) * P:(4 * half + q + 1) * P],
                                               c["ident"][0:w, 0:w])
                last.then_inc(turned, 1)

        @blk.vector
        def _(dve):
            for n in range(2 * TT):
                j, half = n // 2, n % 2
                w = min(P, T - P * j)
                dve.wait_ge(turned, n + 1)
                nc.vector.tensor_copy(xT[:, 4 * half:4 * half + 4, j * P:j * P + w], pt[n % 4][:, :, 0:w]).then_inc(copied, 1)


def channel_norm(nc, name, c, src, x0, n, gcol, dst):
    h = n // 2
    with Stage(nc, name) as s:
        sq = s.sb("sq", [P, KD, n])
        rs = s.sb("rs", [P, n])
        ms = s.ps("ms", [P, 2, 512])
        squared, summed, rooted, inv = s.sem("squared"), s.sem("summed"), s.sem("rooted"), s.sem("inv")
        blk = s.block()

        @blk.scalar
        def _(act):
            for k in range(KD):
                sc(nc)(sq[:, k, :], src[:, k, x0:x0 + n], ACT.Square).then_inc(squared, 1)
            act.wait_ge(summed, 1)
            sc(nc)(rs[:, :].rearrange("p (a b) -> p a b", a=2), ms[:, :, 0:h], ACT.Sqrt, bias=c["eps"][:, 0:1],
                   scale=1.0 / D).then_inc(rooted, 1)

        @blk.tensor
        def _(pe):
            for k in range(KD):
                pe.wait_ge(squared, k + 1)
                for a in range(2):
                    last = nc.tensor.matmul(ms[:, a, 0:h], c["ones"][:, :], sq[:, k, a * h:a * h + h],
                                            start=(k == 0), stop=(k == KD - 1))
            last.then_inc(summed, 1)

        @blk.vector
        def _(dve):
            dve.wait_ge(rooted, 1)
            nc.vector.reciprocal(rs[:, :], rs[:, :]).then_inc(inv, 1)
            dve.wait_ge(inv, 1)
            for k in range(KD):
                nc.vector.scalar_tensor_tensor(out=dst[:, k, :], in0=src[:, k, x0:x0 + n],
                                               scalar=c["par"][:, gcol + k:gcol + k + 1], in1=rs[:, :],
                                               op0=ALU.mult, op1=ALU.mult)


def linear(nc, name, w, col0, tiles, x, x0, kc, n, engine, evacuate, extra=None):
    h = n // 2
    wv = w.rearrange("(c p) n -> p c n", p=P)
    with Stage(nc, name) as s:
        wt, wh, wl = ([s.sb(f"{m}{b}", [P, kc, P], dt) for b in range(2)] for m, dt in (("w", F32), ("wh", F32R), ("wl", F32R)))
        xh, xl = (s.sb(m, [P, kc, n], F32R) for m in ("xh", "xl"))
        acc = [s.ps(f"acc{b}", [P, 2, 512]) for b in range(2)]
        loaded, highs, lows, done, out = ([s.sem(f"{m}{b}") for b in range(2)] for m in ("loaded", "highs", "lows", "done", "out"))
        xhigh, xlow = s.sem("xhigh"), s.sem("xlow")
        tmp = extra(s) if extra else None
        blk = s.block()

        @blk.sync
        def _(sp):
            with sp.Fori(0, tiles // 2) as i:
                for b in range(2):
                    sp.wait_ge(lows[b], i + 1)
                    sp.dma_start(wt[b][:, :, :], wv[:, :, bass.ds(i * (2 * P) + (col0 + b * P), P)]).then_inc(loaded[b], 16)

        @blk.gpsimd
        def _(pool):
            for b in range(2):
                pool.sem_inc(lows[b], 1)
            with pool.Fori(0, tiles // 2) as i:
                for b in range(2):
                    pool.wait_ge(highs[b], i + 1)
                    nc.gpsimd.tensor_tensor(wl[b][:, :, :], wt[b][:, :, :], wh[b][:, :, :].bitcast(F32), ALU.subtract).then_inc(lows[b], 1)

        @blk.tensor
        def _(pe):
            for b in range(2):
                pe.sem_inc(done[b], 1)
            pe.wait_ge(xlow, kc)
            with pe.Fori(0, tiles // 2) as i:
                for b in range(2):
                    pe.wait_ge(lows[b], i + 2)
                    pe.wait_ge(out[b], i + 1)
                    for k in range(kc):
                        for m, (l, r) in enumerate(((wh, xh), (wh, xl), (wl, xh))):
                            for a in range(2):
                                last = nc.tensor.matmul(acc[b][:, a, 0:h], l[b][:, k, :], r[:, k, a * h:a * h + h],
                                                        start=(k == 0 and m == 0), stop=(k == kc - 1 and m == 2))
                    last.then_inc(done[b], 1)

        def split(eng, copy):
            with eng.Fori(0, tiles // 2) as i:
                for b in range(2):
                    eng.wait_ge(loaded[b], i * 16 + 16)
                    eng.wait_ge(done[b], i + 1)
                    copy(wh[b][:, :, :], wt[b][:, :, :]).then_inc(highs[b], 1)

        def take(eng):
            for b in range(2):
                eng.sem_inc(out[b], 1)
            with eng.Fori(0, tiles // 2) as i:
                for b in range(2):
                    eng.wait_ge(done[b], i + 2)
                    evacuate(eng, i, b, acc[b][:, :, 0:h], tmp).then_inc(out[b], 1)

        @blk.scalar
        def _(act):
            for k in range(kc):
                sc(nc)(xh[:, k, :], x[:, k, x0:x0 + n], ACT.Copy).then_inc(xhigh, 1)
            if engine == "scalar":
                take(act)
            else:
                split(act, lambda dst, src: sc(nc)(dst, src, ACT.Copy))

        @blk.vector
        def _(dve):
            for k in range(kc):
                dve.wait_ge(xhigh, k + 1)
                nc.vector.tensor_tensor(xl[:, k, :], x[:, k, x0:x0 + n], xh[:, k, :].bitcast(F32), ALU.subtract).then_inc(xlow, 1)
            if engine == "scalar":
                split(dve, nc.vector.tensor_copy)
            else:
                take(dve)


def halves(ap):
    return ap.rearrange("p (a b) -> p a b", a=2)


def halves3(ap):
    return ap.rearrange("p o (a b) -> p (o a) b", a=2)


def shift_mix(nc, ins, c, proj, outs):
    with Stage(nc, "shift") as s:
        shr = s.sb("shr", [DEC, RW_PROJ])
        sht = s.sb("sht", [P, RWT, DEC])
        last9 = s.sb("last9", [DEC + 1, RW_PROJ])
        d = s.sb("d", [P, RWT, T])
        pa = s.ps("pa", [P, RWT, DEC])
        pb = s.ps("pb", [DEC + 1, 4, 512])
        loaded, turned, step, tok, stored = s.sem("loaded"), s.sem("turned"), s.sem("step"), s.sem("tok"), s.sem("stored")
        blk = s.block()
        z = PAD

        @blk.sync
        def _(sp):
            sp.dma_start(shr[:, :], ins["state_shift"][0]).then_inc(loaded, 16)
            sp.wait_ge(tok, 1)
            sp.dma_start(outs["shift_prompt"][0], last9[0:1, :]).then_inc(stored, 16)
            sp.dma_start(outs["shift_sample"][0], last9[1:DEC + 1, :]).then_inc(stored, 16)
            sp.wait_ge(stored, 32)

        @blk.tensor
        def _(pe):
            for m in range(RWT):
                last = nc.tensor.transpose(pb[:, m // 4, (m % 4) * P:(m % 4 + 1) * P],
                                           proj[:, m, z + NP_ - 1:z + T], c["ident"][:, :])
            last.then_inc(turned, 1)
            pe.wait_ge(loaded, 16)
            for m in range(RWT):
                last = nc.tensor.transpose(pa[:, m, :], shr[:, m * P:(m + 1) * P], c["ident"][0:DEC, 0:DEC])
            last.then_inc(turned, 1)

        @blk.scalar
        def _(act):
            act.wait_ge(turned, 1)
            sc(nc)(last9[:, :], pb[:, :, :].rearrange("p a b -> p (a b)")[:, 0:RW_PROJ], ACT.Copy).then_inc(tok, 1)

        @blk.vector
        def _(dve):
            chain = Chain(dve, step)
            dve.wait_ge(turned, 2)
            chain(nc.vector.tensor_copy(sht[:, :, :], pa[:, :, :]))
            chain(nc.vector.tensor_tensor(d[:, :, 1:NP_], proj[:, 0:RWT, z:z + NP_ - 1], proj[:, 0:RWT, z + 1:z + NP_], ALU.subtract))
            chain(nc.vector.tensor_scalar(d[:, :, 0:1], proj[:, 0:RWT, z:z + 1], -1.0, None, ALU.mult))
            chain(nc.vector.tensor_tensor(d[:, :, NP_:T], sht[:, :, :], proj[:, 0:RWT, z + NP_:z + T], ALU.subtract))
            dve.wait_ge(tok, 1)
            for m in range(RWT):
                nc.vector.scalar_tensor_tensor(out=proj[:, m, z:z + T], in0=d[:, m, :],
                                               scalar=c["par"][:, PCOL["rw_mu"] + m:PCOL["rw_mu"] + m + 1],
                                               in1=proj[:, m, z:z + T], op0=ALU.mult, op1=ALU.add)


def rwkv_prepare(nc, ins, c, proj, rw):
    H = T // 2
    with Stage(nc, "prep") as s:
        w2 = s.sb("w2", [P, RW_DIM])
        g2 = s.sb("g2", [P, RW_DIM])
        tl = s.sb("tl", [P, T])
        t1 = s.sb("t1", [P, RB, T])
        mask = s.sb("mask", [P, TW])
        pp = [s.ps(f"pp{b}", [P, 2, 512]) for b in range(4)]
        loaded, low, made, sig = s.sem("loaded"), s.sem("low"), s.sem("made"), s.sem("sig")
        step, root, kkp, bon, kks, bons = s.sem("step"), s.sem("root"), s.sem("kkp"), s.sem("bon"), s.sem("kks"), s.sem("bons")
        blk = s.block()
        z = slice(PAD, TW)
        col = lambda n, m: c["par"][:, PCOL[n] + m:PCOL[n] + m + 1]

        @blk.sync
        def _(sp):
            sp.dma_start(w2[0:64, :], ins["rw_w2"][0]).then_inc(loaded, 16)
            sp.dma_start(w2[64:128, :], ins["rw_a2"][0]).then_inc(loaded, 16)
            sp.dma_start(g2[:, :], ins["rw_g2"][0]).then_inc(loaded, 16)

        @blk.tensor
        def _(pe):
            pe.wait_ge(loaded, 48)
            pe.wait_ge(low, 3)
            for n in range(12):
                q, m = n // 4, n % 4
                if n >= 4:
                    pe.wait_ge(sig, n - 3)
                for a in range(2):
                    o = pp[n % 4][:, a, 0:H]
                    ms = slice(m * P, (m + 1) * P)
                    ts = slice(a * H, a * H + H)
                    if q == 0:
                        last = nc.tensor.matmul(o, w2[0:64, ms], tl[0:64, ts], start=True, stop=True)
                    elif q == 1:
                        last = nc.tensor.matmul(o, w2[64:128, ms], tl[64:128, ts], start=True, stop=True)
                    else:
                        last = nc.tensor.matmul(o, g2[:, ms], proj[:, 13, PAD + a * H:PAD + a * H + H], start=True, stop=True)
                last.then_inc(made, 1)
            for n in range(8):
                pe.wait_ge(kkp if n < 4 else bon, n % 4 + 1)
                pe.wait_ge(sig, 9 + n) if n < 4 else pe.wait_ge(root, n - 3)
                for a in range(2):
                    last = nc.tensor.matmul(pp[n % 4][:, a, 0:H], c["bd"][:, :], t1[:, n % 4, a * H:a * H + H], start=True, stop=True)
                last.then_inc(kks if n < 4 else bons, 1)

        @blk.scalar
        def _(act):
            sc(nc)(tl[0:64, :], proj[0:64, 12, z], ACT.Tanh).then_inc(low, 1)
            sc(nc)(tl[64:128, :], proj[64:128, 12, z], ACT.Copy).then_inc(low, 1)
            sc(nc)(proj[:, 13, z], proj[:, 13, z], ACT.Sigmoid).then_inc(low, 1)
            for n in range(12):
                q, m = n // 4, n % 4
                act.wait_ge(made, n + 1)
                src = pp[n % 4][:, :, 0:H]
                if q == 0:
                    sc(nc)(halves(rw["lw"][:, m, z]), src, ACT.Sigmoid, bias=col("rw_w0", m)).then_inc(sig, 1)
                elif q == 1:
                    sc(nc)(halves(rw["b"][:, m, z]), src, ACT.Sigmoid, bias=col("rw_a0", m)).then_inc(sig, 1)
                else:
                    sc(nc)(halves(rw["g"][:, m, z]), src, ACT.Copy).then_inc(sig, 1)
            for m in range(4):
                act.wait_ge(kks, m + 1)
                sc(nc)(halves(rw["la"][:, m, z]), pp[m][:, :, 0:H], ACT.Sqrt).then_inc(root, 1)

        @blk.vector
        def _(dve):
            chain = Chain(dve, step)
            for a in ("lw", "b", "kk"):
                nc.vector.memset(rw[a][:, :, 0:PAD], 0.0)
            nc.vector.memset(proj[:, 0:12, 0:PAD], 0.0)
            chain(nc.vector.memset(mask[:, :], 1.0))
            chain(nc.vector.memset(mask[:, 0:NCH * C].rearrange("p (n c) -> p n c", c=C)[:, :, 0:1], 0.0))
            for m in range(4):
                chain(nc.vector.tensor_scalar(rw["kk"][:, m, z], proj[:, 4 + m, z], col("rw_kk", m), None, ALU.mult))
                nc.vector.tensor_tensor(t1[:, m, :], rw["kk"][:, m, z], rw["kk"][:, m, z], ALU.mult).then_inc(kkp, 1)
            dve.wait_ge(sig, 4)
            chain(nc.vector.tensor_scalar(rw["lw"][:, :, z], rw["lw"][:, :, z], -math.exp(-0.5), None, ALU.mult))
            for m in range(4):
                chain(nc.vector.tensor_tensor_scan(rw["L"][:, m, :], mask[:, :], rw["lw"][:, m, :], 0.0, ALU.mult, ALU.add))
            dve.wait_ge(sig, 8)
            dve.wait_ge(root, 4)
            chain(nc.vector.tensor_scalar(rw["la"][:, :, z], rw["la"][:, :, z], 1e-12, None, ALU.max))
            chain(nc.vector.reciprocal(rw["la"][:, :, z], rw["la"][:, :, z]))
            chain(nc.vector.tensor_tensor(rw["kk"][:, :, z], rw["kk"][:, :, z], rw["la"][:, :, z], ALU.mult))
            chain(nc.vector.tensor_tensor(rw["la"][:, :, :], rw["L"][:, :, :], rw["lw"][:, :, :], ALU.subtract))
            for m in range(4):
                chain(nc.vector.tensor_scalar(t1[:, m, :], rw["b"][:, m, z], -1.0, col("rw_ka", m), ALU.add, ALU.mult))
                chain(nc.vector.scalar_tensor_tensor(out=proj[:, 4 + m, z], in0=t1[:, m, :], scalar=1.0, in1=proj[:, 4 + m, z],
                                                     op0=ALU.add, op1=ALU.mult))
                chain(nc.vector.tensor_tensor(rw["b"][:, m, z], rw["b"][:, m, z], rw["kk"][:, m, z], ALU.mult))
                nc.vector.scalar_tensor_tensor(out=t1[:, m, :], in0=proj[:, m, z], scalar=col("rw_rk", m),
                                               in1=proj[:, 4 + m, z], op0=ALU.mult, op1=ALU.mult).then_inc(bon, 1)
            for m in range(4):
                dve.wait_ge(bons, m + 1)
                nc.vector.tensor_tensor(halves(rw["bonus"][:, m, :]), pp[m][:, :, 0:H], halves(proj[:, 8 + m, z]), ALU.mult)


def rwkv_chunks(nc, c, proj, rw, yT, outs, scratch):
    NL = len(LEVELS)
    G = 3
    assert NCH % G == 0
    with Stage(nc, "chunk") as s:
        W = [P, RB, C]
        flat = [x.rearrange("p m t -> p (m t)") for x in scratch] + [proj[:, m, 0:TW] for m in (12, 13)]
        free = [x[:, n * RB * C:(n + 1) * RB * C].rearrange("p (m t) -> p m t", m=RB)
                for x in flat for n in range(x.shape[1] // (RB * C))]
        free += [rw["lw"][:, :, n * C:(n + 1) * C] for n in range(NCH)]

        def buf(name):
            return free.pop() if free else s.sb(name, W)[:, :, :]

        eP, eN, eA, W0, U, S = (s.sb(n, W) for n in ("eP", "eN", "eA", "W0", "U", "S"))
        srow = W0
        at, bt, kt, rt, vc, AkT, RbT, RkT, XT, V, Bt, Kt = (
            [buf(f"{n}{k}") for k in range(G)] for n in ("at", "bt", "kt", "rt", "vc", "AkT", "RbT", "RkT", "XT", "V", "Bt", "Kt"))
        X, Y = kt, bt
        lev = [[buf(f"lev{k}{n}") for n in range(NL - 1)] for k in range(G)]
        pc = [s.sb(f"pc{k}", [P, RB, 1]) for k in range(G)]
        banks = [s.ps(f"p{n}", [P, 2 * RB, C]) for n in range(8)]
        p = [banks[n // 2][:, (n % 2) * RB:(n % 2 + 1) * RB, :] for n in range(16)]
        first = [0, 8, 0]
        low = [8, 12, 0]
        expd, prodb, turned, final, stored, group, stated = (
            s.sem(n) for n in ("expd", "prodb", "turned", "final", "stored", "group", "stated"))
        dsem, prod, asem = ([s.sem(f"{n}{k}") for k in range(G)] for n in ("dsem", "prod", "asem"))
        SCALED, MASKED_ = 5, 5 + 2 + (NL - 1) + 2 + 4
        D = MASKED_ + 3 * (NL - 1) - 1
        PR = 1 + 2 * (NL - 1)
        DB, PB = 7, 4
        blk = s.block()

        def heads(out, *terms):
            for m in range(RB):
                for e in range(2):
                    q = slice(64 * e, 64 * e + 64)
                    for n, (l, r) in enumerate(terms):
                        rr = r[q, 0:64] if r is c["ident2"] else r[q, m, :]
                        last = nc.tensor.matmul(out[q, m, :], l[q, m, :], rr, start=(n == 0), stop=(n == len(terms) - 1))
            return last

        def chunk(i, k):
            return bass.ds(i * (G * C) + k * C, C)

        @blk.scalar
        def _(act):
            with act.Fori(0, NCH // G) as i:
                act.wait_ge(group, i + 1)
                for k in range(G):
                    sl = chunk(i, k)
                    if k:
                        act.wait_ge(dsem[k - 1], i * D + SCALED)
                    sc(nc)(eP[:, :, :], rw["L"][:, :, sl], ACT.Exp).then_inc(expd, 1)
                    sc(nc)(eN[:, :, :], rw["L"][:, :, sl], ACT.Exp, scale=-1.0).then_inc(expd, 1)
                    sc(nc)(eA[:, :, :], rw["la"][:, :, sl], ACT.Exp).then_inc(expd, 1)
                    sc(nc)(vc[k][:, :, :], proj[:, 8:12, sl], ACT.Copy).then_inc(expd, 1)
                for k in range(G):
                    act.wait_ge(prod[k], i * PR + 1)
                    for n, dst in enumerate((Bt, Kt)):
                        sc(nc)(dst[k][:, :, :], p[first[k] + 6 + n], ACT.Copy).then_inc(asem[k], 1)

        @blk.tensor
        def _(pe):
            def seen(out, *waits):
                for sem, n in waits:
                    pe.wait_ge(sem, n)
                    nc.tensor.matmul(out[0:32, 0, 0:1], c["ones"][:, 0:32], c["ones"][:, 0:1], start=True, stop=True)

            with pe.Fori(0, NCH // G) as i:
                made = lambda k, n: (dsem[k], i * D + n)
                for k in range(G):
                    o = first[k]
                    if k == 2:
                        seen(p[o], made(0, MASKED_), (asem[0], i * 2 + 2))
                    seen(p[o], made(k, SCALED))
                    for n, (l, r) in enumerate(((at[k], bt[k]), (bt[k], at[k]), (kt[k], at[k]), (bt[k], rt[k]), (kt[k], rt[k]),
                                                (vc[k], c["ident2"]), (bt[k], c["ident2"]), (kt[k], c["ident2"]))):
                        last = heads(p[o + n], (l, r))
                    last.then_inc(prod[k], 1)
                for n in range(1, NL):
                    before = MASKED_ + 3 * (n - 1)
                    for k in range(G):
                        o = low[k]
                        if n == 1 and k == 0:
                            seen(p[o], made(1, MASKED_))
                        seen(p[o], made(k, before))
                        if n == 1 and k == 1:
                            seen(p[o], (asem[1], i * 2 + 2))
                        heads(p[o], (lev[k][n - 1], X[k])).then_inc(prod[k], 1)
                    for k in range(G):
                        o = low[k]
                        seen(p[o + 2], made(k, before + 1))
                        last = heads(p[o + 2], (Y[k], XT[k]))
                        if n < NL - 1:
                            last = heads(p[o + 3], (XT[k], Y[k]))
                        last.then_inc(prod[k], 1)
                w0, u = p[4], p[6]
                seen(w0, (asem[2], i * 2 + 2))
                for k in range(G):
                    state = lambda n: (stated, i * (G * DB) + (k * DB + n + 1))
                    seen(w0, state(0))
                    heads(w0, (AkT[k], V[k]), (at[k], S)).then_inc(prodb, 1)
                    heads(p[9], (Kt[k], V[k]))
                    heads(p[8], (S, rt[k]), (V[k], RkT[k])).then_inc(prodb, 1)
                    if k == 0:
                        for kk in range(G):
                            seen(u, made(kk, D))
                    seen(u, state(1))
                    heads(u, (XT[k], W0)).then_inc(prodb, 1)
                    seen(p[10], state(4))
                    heads(p[11], (Bt[k], U))
                    heads(p[10], (U, RbT[k])).then_inc(prodb, 1)
            pe.wait_ge(stated, NCH * DB + 1)
            heads(p[6], (S, c["ident2"])).then_inc(turned, 1)

        @blk.vector
        def _(dve):
            nc.vector.memset(S[:, :, :], 0.0).then_inc(stated, 1)
            dve.sem_inc(group, 1)
            bc = lambda m: m.unsqueeze(1).to_broadcast(W)
            tt = nc.vector.tensor_tensor
            with dve.Fori(0, NCH // G) as i:
                for k in range(G):
                    sl = chunk(i, k)
                    dve.wait_ge(expd, i * (4 * G) + (4 * k + 4))
                    tt(bt[k], rw["b"][:, :, sl], eN[:, :, :], ALU.mult).then_inc(dsem[k], 1)
                    tt(kt[k], proj[:, 4:8, sl], eN[:, :, :], ALU.mult).then_inc(dsem[k], 1)
                    tt(rt[k], proj[:, 0:4, sl], eP[:, :, :], ALU.mult).then_inc(dsem[k], 1)
                    nc.vector.tensor_copy(pc[k][:, :, :], eP[:, :, C - 1:C]).then_inc(dsem[k], 1)
                    nc.vector.scalar_tensor_tensor(out=at[k], in0=rw["kk"][:, :, sl], scalar=-1.0, in1=eA[:, :, :],
                                                   op0=ALU.mult, op1=ALU.mult).then_inc(dsem[k], 1)
                for k in range(G):
                    o = first[k]
                    dve.wait_ge(prod[k], i * PR + 1)
                    tt(X[k], p[o], bc(c["m1"][:, :]), ALU.mult).then_inc(dsem[k], 1)
                    tt(XT[k], p[o + 1], bc(c["lmt"][:, 0, :]), ALU.mult).then_inc(dsem[k], 1)
                    for n in range(1, NL):
                        tt(lev[k][n - 1], p[o + 1], bc(c["lmt"][:, n, :]), ALU.mult).then_inc(dsem[k], 1)
                    dve.wait_ge(dsem[k], i * D + SCALED + NL + 1)
                    tt(X[k], X[k], bc(c["ident2"][:, 0:C]), ALU.add).then_inc(dsem[k], 1)
                    tt(XT[k], XT[k], bc(c["ident2"][:, 0:C]), ALU.add).then_inc(dsem[k], 1)
                    tt(AkT[k], p[o + 2], bc(c["um"][:, :]), ALU.mult).then_inc(dsem[k], 1)
                    tt(RbT[k], p[o + 3], bc(c["ui"][:, :]), ALU.mult).then_inc(dsem[k], 1)
                    tt(RkT[k], p[o + 4], bc(c["ui"][:, :]), ALU.mult).then_inc(dsem[k], 1)
                    nc.vector.tensor_copy(V[k], p[o + 5]).then_inc(dsem[k], 1)
                for n in range(1, NL):
                    for k in range(G):
                        dve.wait_ge(prod[k], i * PR + 2 * n)
                        nc.vector.tensor_copy(Y[k], p[low[k]]).then_inc(dsem[k], 1)
                    for k in range(G):
                        dve.wait_ge(prod[k], i * PR + 2 * n + 1)
                        tt(XT[k], p[low[k] + 2], XT[k], ALU.add).then_inc(dsem[k], 1)
                        if n < NL - 1:
                            tt(X[k], p[low[k] + 3], X[k], ALU.add).then_inc(dsem[k], 1)
                for k in range(G):
                    made = lambda n: dve.wait_ge(prodb, i * (G * PB) + (k * PB + n))
                    made(1)
                    nc.vector.tensor_copy(W0[:, :, :], p[4]).then_inc(stated, 1)
                    made(2)
                    tt(S[:, :, :], p[9], S[:, :, :], ALU.add).then_inc(stated, 1)
                    nc.vector.tensor_copy(yT[:, :, chunk(i, k)], p[8]).then_inc(stated, 1)
                    made(3)
                    nc.vector.tensor_copy(U[:, :, :], p[6]).then_inc(stated, 1)
                    made(4)
                    tt(S[:, :, :], p[11], S[:, :, :], ALU.add).then_inc(stated, 1)
                    tt(yT[:, :, chunk(i, k)], p[10], yT[:, :, chunk(i, k)], ALU.add).then_inc(stated, 1)
                    dve.wait_ge(stated, i * (G * DB) + (k * DB + 6))
                    tt(S[:, :, :], S[:, :, :], pc[k][:, :, :].to_broadcast(W), ALU.mult).then_inc(stated, 1)
                dve.wait_ge(stated, i * (G * DB) + (G * DB + 1))
                dve.sem_inc(group, 1)
            dve.wait_ge(turned, 1)
            nc.vector.tensor_copy(srow[:, :, :], p[6]).then_inc(final, 1)

        @blk.sync
        def _(sp):
            sp.wait_ge(final, 1)
            for e in range(2):
                dst = outs["wkv_prompt"][0, 0].rearrange("(m e) v k -> e v m k", e=2)
                sp.dma_start(dst[e], srow[64 * e:64 * e + 64, :, :]).then_inc(stored, 16)
            sp.wait_ge(stored, 32)


def rwkv_sample(nc, c, proj, rw, yT, ins, outs, scr):
    N = RW_HEAD
    with Stage(nc, "step") as s:
        vt = s.sb("vt", [P, 6, RB, DEC])
        vr = s.sb("vr", [DEC, 6, RW_DIM])
        vec = s.sb("vec", [P, 5, N])
        HV = N // 2
        value = s.sb("value", [P, HV])
        room = lambda a: rw[a][:, :, :].rearrange("p m t -> p (m t)")[:, 0:HV * N].rearrange("p (v k) -> p v k", k=N)
        S0, S1 = room("L"), room("la")
        t1 = s.sb("t1", [P, HV, N])
        sa = s.sb("sa", [P, HV])
        y = s.sb("y", [P, HV])
        yr = s.sb("yr", [DEC, RW_DIM])
        pt = s.ps("pt", [DEC, 6, 512])
        py = s.ps("py", [P, RB, DEC])
        step, dec, turned, rows, state, there, back = (s.sem(n) for n in ("step", "dec", "turned", "rows", "state", "there", "back"))
        again, stored, yturn = s.sem("again"), s.sem("stored"), s.sem("yturn")
        gath = s.sem("gath")
        blk = s.block()
        z = slice(PAD + NP_, TW)

        @blk.sync
        def _(sp):
            st_in = ins["state_wkv"][0].rearrange("b h v k -> (b h) v k")
            st_out = outs["wkv_sample"][0].rearrange("b h v k -> (b h) v k")
            halves_of = [(slice(64 * e, 64 * e + 64), slice(HV * e, HV * e + HV)) for e in range(2)]
            y_out = scr["y"].rearrange("b (h k) -> (b h) k", k=N)
            for q, vs in halves_of:
                sp.dma_start(S0[q, :, :], st_in[:, vs, :]).then_inc(state, 16)
            sp.wait_ge(rows, 6)
            sp.dma_start(scr["vec"].rearrange("q b n -> b q n"), vr[:, :, :]).then_inc(there, 16)
            sp.wait_ge(there, 16)
            for q, vs in halves_of:
                sp.dma_start(vec[q, :, :], scr["vec"][0:5].rearrange("q b (h k) -> (b h) q k", k=N)).then_inc(back, 16)
                sp.dma_start(value[q, :], scr["vec"][5].rearrange("b (h k) -> (b h) k", k=N)[:, vs]).then_inc(back, 16)
            sp.wait_ge(gath, 1)
            for q, vs in halves_of:
                sp.dma_start(y_out[:, vs], y[q, :]).then_inc(there, 16)
            for q, vs in halves_of:
                sp.dma_start(st_out[:, vs, :], S1[q, :, :]).then_inc(stored, 16)
            sp.wait_ge(there, 48)
            sp.dma_start(yr[:, :], scr["y"]).then_inc(again, 16)
            sp.wait_ge(stored, 32)

        @blk.scalar
        def _(act):
            sc(nc)(vt[:, 0, :, :], rw["lw"][:, :, z], ACT.Exp).then_inc(dec, 1)
            act.wait_ge(turned, 1)
            for q in range(6):
                sc(nc)(vr[:, q, :], pt[:, q, :], ACT.Copy).then_inc(rows, 1)

        @blk.tensor
        def _(pe):
            pe.wait_ge(dec, 1)
            pe.wait_ge(step, 5)
            for q in range(6):
                for m in range(RB):
                    last = nc.tensor.transpose(pt[:, q, m * P:(m + 1) * P], vt[:, q, m, :], c["ident"][:, :])
            last.then_inc(turned, 1)
            pe.wait_ge(again, 16)
            for m in range(RB):
                last = nc.tensor.transpose(py[:, m, :], yr[:, m * P:(m + 1) * P], c["ident"][0:DEC, 0:DEC])
            last.then_inc(yturn, 1)

        @blk.vector
        def _(dve):
            chain = Chain(dve, step)
            W = [P, HV, N]
            over_v = lambda q: vec[:, q, :].unsqueeze(1).to_broadcast(W)
            over_k = lambda v: v.unsqueeze(2).to_broadcast(W)
            chain(nc.vector.tensor_copy(vt[:, 1, :, :], proj[:, 4:8, z]))
            chain(nc.vector.tensor_scalar(vt[:, 2, :, :], rw["kk"][:, :, z], -1.0, None, ALU.mult))
            chain(nc.vector.tensor_copy(vt[:, 3, :, :], rw["b"][:, :, z]))
            chain(nc.vector.tensor_copy(vt[:, 4, :, :], proj[:, 0:4, z]))
            chain(nc.vector.tensor_copy(vt[:, 5, :, :], proj[:, 8:12, z]))
            dve.wait_ge(back, 64)
            dve.wait_ge(state, 32)
            chain(nc.vector.tensor_tensor(t1[:, :, :], S0[:, :, :], over_v(2), ALU.mult))
            chain(nc.vector.tensor_reduce(sa[:, :], t1[:, :, :], AX.X, ALU.add))
            chain(nc.vector.tensor_tensor(S1[:, :, :], S0[:, :, :], over_v(0), ALU.mult))
            chain(nc.vector.tensor_tensor(t1[:, :, :], over_k(sa[:, :]), over_v(3), ALU.mult))
            chain(nc.vector.tensor_tensor(S1[:, :, :], S1[:, :, :], t1[:, :, :], ALU.add))
            chain(nc.vector.tensor_tensor(t1[:, :, :], over_k(value[:, :]), over_v(1), ALU.mult))
            chain(nc.vector.tensor_tensor(S1[:, :, :], S1[:, :, :], t1[:, :, :], ALU.add))
            chain(nc.vector.tensor_tensor(t1[:, :, :], S1[:, :, :], over_v(4), ALU.mult))
            nc.vector.tensor_reduce(y[:, :], t1[:, :, :], AX.X, ALU.add).then_inc(gath, 1)
            dve.wait_ge(yturn, 1)
            nc.vector.tensor_copy(yT[:, :, z], py[:, :, :])


def rwkv_output(nc, c, rw, yT, yo):
    H = TQ // 2
    with Stage(nc, "rwout") as s:
        d = s.sb("d", [P, RB, TQ])
        sq = s.sb("sq", [P, RB, TQ])
        pm = [s.ps(f"pm{m}", [P, 2, 512]) for m in range(4)]
        mean, cent, var, root, step = s.sem("mean"), s.sem("cent"), s.sem("var"), s.sem("root"), s.sem("step")
        blk = s.block()
        z = slice(PAD + META, TW)
        col = lambda n, m: c["par"][:, PCOL[n] + m:PCOL[n] + m + 1]

        @blk.tensor
        def _(pe):
            for m in range(4):
                for a in range(2):
                    last = nc.tensor.matmul(pm[m][:, a, 0:H], c["bd"][:, :], yT[:, m, PAD + META + a * H:PAD + META + a * H + H],
                                            start=True, stop=True)
                last.then_inc(mean, 1)
            for m in range(4):
                pe.wait_ge(cent, m + 1)
                for a in range(2):
                    last = nc.tensor.matmul(pm[m][:, a, 0:H], c["bd"][:, :], sq[:, m, a * H:a * H + H], start=True, stop=True)
                last.then_inc(var, 1)

        @blk.scalar
        def _(act):
            for m in range(4):
                act.wait_ge(var, m + 1)
                sc(nc)(halves(sq[:, m, :]), pm[m][:, :, 0:H], ACT.Sqrt, bias=c["eps"][:, 1:2], scale=1.0 / RW_HEAD).then_inc(root, 1)

        @blk.vector
        def _(dve):
            chain = Chain(dve, step)
            for m in range(4):
                dve.wait_ge(mean, m + 1)
                chain(nc.vector.scalar_tensor_tensor(out=halves(d[:, m, :]), in0=pm[m][:, :, 0:H], scalar=-1.0 / RW_HEAD,
                                                     in1=halves(yT[:, m, z]), op0=ALU.mult, op1=ALU.add))
                nc.vector.tensor_tensor(sq[:, m, :], d[:, m, :], d[:, m, :], ALU.mult).then_inc(cent, 1)
            for m in range(4):
                dve.wait_ge(root, m + 1)
                chain(nc.vector.reciprocal(sq[:, m, :], sq[:, m, :]))
                chain(nc.vector.scalar_tensor_tensor(out=d[:, m, :], in0=d[:, m, :], scalar=col("rw_ln_g", m), in1=sq[:, m, :],
                                                     op0=ALU.mult, op1=ALU.mult))
                chain(nc.vector.scalar_tensor_tensor(out=d[:, m, :], in0=d[:, m, :], scalar=col("rw_ln_b", m),
                                                     in1=rw["bonus"][:, m, META:T], op0=ALU.add, op1=ALU.add))
                chain(nc.vector.tensor_tensor(yo[:, m, :], d[:, m, :], rw["g"][:, m, z], ALU.mult))


def attention_inputs(nc, ins, c, proj, xn, v_tok, outs, vnew):
    H = T // 2
    wv = ins["w_in"][0].rearrange("(c p) n -> p c n", p=P)
    v0 = RW_PROJ + 2 * 512
    with Stage(nc, "qkv") as s:
        w = s.sb("w", [P, KD, 512])
        sq = s.sb("sq", [P, 8, T])
        krow = s.sb("krow", [P, TT, 512])
        pm = [s.ps(f"pm{n}", [P, 2, 512]) for n in range(2)]
        pk = [s.ps(f"pk{n}", [P, 512]) for n in range(2)]
        acc = [s.ps(f"acc{b}", [P, 512]) for b in range(2)]
        squared, summed, root, step, keys, turned, copied, stored = (
            s.sem(n) for n in ("squared", "summed", "root", "step", "keys", "turned", "copied", "stored"))
        loaded, done, out = s.sem("loaded"), s.sem("done"), s.sem("out")
        blk = s.block()
        z = slice(PAD, TW)
        tokens = [min(P, T - j * P) for j in range(TT)]

        @blk.scalar
        def _(act):
            for n in range(8):
                sc(nc)(sq[:, n, :], proj[:, 14 + n, z], ACT.Square).then_inc(squared, 1)

            def values(j):
                act.wait_ge(done, j + 1)
                sc(nc)(v_tok[0:tokens[j], j, :], acc[j % 2][0:tokens[j], :], ACT.Copy).then_inc(out, 1)

            for n in range(8):
                act.wait_ge(summed, n + 1)
                sc(nc)(halves(sq[:, n, :]), pm[n % 2][:, :, 0:H], ACT.Sqrt, bias=c["eps"][:, 0:1], scale=1.0 / 64).then_inc(root, 1)
                if n % 2 and n > 2:
                    values(n // 2 - 1)
            values(3)
            values(4)

        @blk.tensor
        def _(pe):
            def values(j):
                if j == 0:
                    pe.wait_ge(loaded, 16)
                if j >= 2:
                    pe.wait_ge(out, j - 1)
                for k in range(KD):
                    last = nc.tensor.matmul(acc[j % 2][0:tokens[j], :], xn[:, k, j * P:j * P + tokens[j]], w[:, k, :],
                                            start=(k == 0), stop=(k == KD - 1))
                last.then_inc(done, 1)

            for n in range(8):
                pe.wait_ge(squared, n + 1)
                if n >= 2:
                    pe.wait_ge(root, n - 1)
                for a in range(2):
                    last = nc.tensor.matmul(pm[n % 2][:, a, 0:H], c["bd"][:, :], sq[:, n, a * H:a * H + H], start=True, stop=True)
                last.then_inc(summed, 1)
                if n % 2:
                    values(n // 2)
            values(4)
            pe.wait_ge(keys, 4)
            for j, m in enumerate(tokens):
                if j >= 2:
                    pe.wait_ge(copied, j - 1)
                for h in range(HA):
                    last = nc.tensor.transpose(pk[j % 2][0:m, h * P:(h + 1) * P], proj[:, 18 + h, PAD + j * P:PAD + j * P + m],
                                               c["ident"][:, :])
                last.then_inc(turned, 1)

        @blk.vector
        def _(dve):
            chain = Chain(dve, step)
            for n in range(8):
                g = PCOL["da_qn_g" if n < 4 else "da_kn_g"]
                dve.wait_ge(root, n + 1)
                chain(nc.vector.reciprocal(sq[:, n, :], sq[:, n, :]))
                last = nc.vector.scalar_tensor_tensor(out=proj[:, 14 + n, z], in0=proj[:, 14 + n, z], scalar=c["par"][:, g:g + 1],
                                                      in1=sq[:, n, :], op0=ALU.mult, op1=ALU.mult)
                if n < 4:
                    chain(last)
                    chain(nc.vector.tensor_scalar(proj[:, 14 + n, z], proj[:, 14 + n, z], 0.125, None, ALU.mult))
                else:
                    last.then_inc(keys, 1)
            for j, m in enumerate(tokens):
                dve.wait_ge(turned, j + 1)
                nc.vector.tensor_copy(krow[0:m, j, :], pk[j % 2][0:m, :]).then_inc(copied, 1)

        @blk.sync
        def _(sp):
            def rows(prompt, sample, x):
                sp.dma_start(prompt[0:SEQ, :].rearrange("(j p) d -> p j d", p=P), x[:, 0:4, :]).then_inc(stored, 16)
                sp.dma_start(prompt[SEQ:NP_, :], x[0:META, 4, :]).then_inc(stored, 16)
                sp.dma_start(sample, x[META:META + DEC, 4, :]).then_inc(stored, 16)

            sp.dma_start(w[:, :, :], wv[:, :, v0:v0 + 512]).then_inc(loaded, 16)
            sp.wait_ge(out, TT)
            rows(outs["v_prompt"][0, 0].rearrange("t h v -> t (h v)"), outs["v_sample"][0, :, 0].rearrange("t h v -> t (h v)"), v_tok)
            sp.dma_start(vnew, v_tok[META:META + DEC, 4, :]).then_inc(stored, 16)
            sp.wait_ge(copied, TT)
            rows(outs["k_prompt"][0, 0].rearrange("t h c d -> t (h c d)"),
                 outs["k_sample"][0, :, 0].rearrange("t h c d -> t (h c d)"), krow)
            sp.wait_ge(stored, 16 * 7)


def load_pages(eng, cache, pages, at, dst, sem):
    for pg in range(NPAGE):
        page = eng.value_load(pages[0:1, bass.ds(at + pg, 1)], min_val=0, max_val=cache.shape[0] - 1)
        eng.dma_start(dst[:, pg, :], cache[bass.ds(page, 1)].rearrange("o p x -> p (o x)")).then_inc(sem, 16)


def attend_prompt(nc, ins, c, proj, v_tok, oT, past):
    WM = NP_
    with Stage(nc, "att") as s:
        dist = s.sb("dist", [P, WM])
        S = [[s.sb(f"S{b}{e}", [P, WM]) for e in range(2)] for b in range(2)]
        A = s.sb("A", [P, WM])
        AT = s.sb("AT", [P, TT, P])
        st = [s.sb(f"st{b}", [P, 2, 4]) for b in range(2)]
        pS = [s.ps(f"pS{e}", [P, 1024]) for e in range(2)]
        pT = s.ps("pT", [P, 8, P])
        pO = s.ps("pO", [P, 512])
        built, scored, biased, expd, mixed, turned, copied, summed, taken, step = (
            s.sem(n) for n in ("built", "scored", "biased", "expd", "mixed", "turned", "copied", "summed", "taken", "step"))
        blk = s.block()
        ptab, fetched = s.sem("ptab"), s.sem("fetched")
        steps = [(h, i) for h in range(HA) for i in range(4)]
        width = lambda i: META + P * (i + 1)
        blocks = lambda i: [(j, P if j <= i else META) for j in range(i + 2)]

        @blk.sync
        def _(sp):
            sp.dma_start(past["pages"][:, :], ins["page_table"].rearrange("b n -> (b n)").unsqueeze(0)).then_inc(ptab, 16)
            sp.wait_ge(ptab, 16)
            for b in range(2):
                load_pages(sp, past["ck"], past["pages"], b * NPAGE, past["K"][b], fetched)
            sp.wait_ge(fetched, 16 * 2 * NPAGE)

        @blk.gpsimd
        def _(pool):
            nc.gpsimd.iota(dist[:, :], pattern=[[-1, WM]], base=META + 3 * P, channel_multiplier=1,
                           allow_small_or_imprecise_dtypes=True).then_inc(built, 1)
            pool.wait_ge(built, 1)
            nc.gpsimd.affine_select(out=dist[:, :], in_=dist[:, :], compare_op=ALU.is_ge, fill=MASKED, base=META + 3 * P,
                                    pattern=[[-1, WM]], channel_multiplier=1).then_inc(built, 1)

        @blk.tensor
        def _(pe):
            def scores(n):
                h, i = steps[n]
                for e in range(2):
                    q = slice(64 * e, 64 * e + 64)
                    if n:
                        pe.wait_ge(biased, 2 * (n - 1) + e + 1)
                    x0 = PAD + META + i * P
                    for a, b in ((0, min(width(i), 512)), (512, width(i))):
                        if b > a:
                            last = nc.tensor.matmul(pS[e][:, a:b], proj[q, 14 + h, x0:x0 + P], proj[q, 18 + h, PAD + a:PAD + b],
                                                    start=True, stop=True)
                    last.then_inc(scored, 1)

            scores(0)
            scores(1)
            for n, (h, i) in enumerate(steps):
                if n + 2 < len(steps):
                    scores(n + 2)
                pe.wait_ge(mixed, n + 1)
                for j, w in blocks(i):
                    last = nc.tensor.transpose(pT[0:w, j, :], A[:, j * P:j * P + w], c["ident"][:, :])
                last.then_inc(turned, 1)
                pe.wait_ge(copied, n + 1)
                if n:
                    pe.wait_ge(taken, n)
                for j, w in blocks(i):
                    last = nc.tensor.matmul(pO[:, 0:P], v_tok[0:w, j, h * DV:(h + 1) * DV], AT[0:w, j, :],
                                            start=(j == 0), stop=(j == i + 1))
                last.then_inc(summed, 1)

        @blk.scalar
        def _(act):
            def exponents(n):
                w = width(steps[n][1])
                for e in range(2):
                    act.wait_ge(biased, 2 * n + e + 1)
                    x = S[n % 2][e][:, 0:w]
                    sc(nc)(x, x, ACT.Exp, bias=st[n % 2][:, e, 0:1], accum_out=st[n % 2][:, e, 1:2]).then_inc(expd, 1)

            def result(n):
                h, i = steps[n]
                act.wait_ge(summed, n + 1)
                sc(nc)(oT[:, h, i * P:(i + 1) * P], pO[:, 0:P], ACT.Copy).then_inc(taken, 1)

            exponents(0)
            exponents(1)
            for n, (h, i) in enumerate(steps):
                act.wait_ge(turned, n + 1)
                sc(nc)(AT[:, 0:i + 1, :], pT[:, 0:i + 1, :], ACT.Copy)
                sc(nc)(AT[0:META, i + 1, :], pT[0:META, i + 1, :], ACT.Copy).then_inc(copied, 1)
                if n + 2 < len(steps):
                    exponents(n + 2)
                result(n)

        @blk.vector
        def _(dve):
            chain = Chain(dve, step)
            dve.wait_ge(built, 2)

            def bias_and_maximum(n):
                h, i = steps[n]
                w, b = width(i), n % 2
                if n >= 2:
                    dve.wait_ge(mixed, n - 1)
                for e in range(2):
                    dve.wait_ge(scored, 2 * n + e + 1)
                    chain(nc.vector.scalar_tensor_tensor(out=S[b][e][:, 0:w], in0=dist[:, WM - w:WM], scalar=-SLOPE[h],
                                                         in1=pS[e][:, 0:w], op0=ALU.mult, op1=ALU.add))
                    nc.vector.tensor_reduce(st[b][:, e, 0:1], S[b][e][:, 0:w], AX.X, ALU.max, negate=True).then_inc(biased, 1)

            bias_and_maximum(0)
            bias_and_maximum(1)
            for n, (h, i) in enumerate(steps):
                w, x, q = width(i), S[n % 2], st[n % 2]
                dve.wait_ge(expd, 2 * n + 2)
                chain(nc.vector.reciprocal(q[:, :, 2:3], q[:, :, 1:2]))
                chain(nc.vector.tensor_tensor(q[:, 1, 3:4], q[:, 1, 2:3], c["lam"][:, 1:2], ALU.mult))
                if n:
                    dve.wait_ge(turned, n)
                chain(nc.vector.tensor_scalar(A[:, 0:w], x[1][:, 0:w], q[:, 1, 3:4], None, ALU.mult))
                nc.vector.scalar_tensor_tensor(out=A[:, 0:w], in0=x[0][:, 0:w], scalar=q[:, 0, 2:3], in1=A[:, 0:w],
                                               op0=ALU.mult, op1=ALU.add).then_inc(mixed, 1)
                if n + 2 < len(steps):
                    bias_and_maximum(n + 2)


def attend_sample(nc, c, proj, oT, past, vnew):
    zs = PAD + NP_
    with Stage(nc, "dec") as s:
        K, V, vn, pages = (past[n] for n in ("K", "V", "vn", "pages"))
        Q = s.sb("Q", [P, DEC, 512])
        bias = s.sb("bias", [P, NPAGE, 2, HA])
        Sc = s.sb("Sc", [P, NPAGE, 2, HA])
        rows = s.sb("rows", [HC, PAST + 1])
        new = s.sb("new", [HC, DEC])
        qk = s.sb("qk", [P, DEC, 2, HA])
        comb0 = s.sb("comb0", [HC, HA])
        comb = s.sb("comb", [HC, HA])
        st = s.sb("st", [HC, 3])
        at = s.sb("at", [P, NPAGE, HA])
        atn = s.sb("atn", [1, HA])
        orow = Q[0:HA, :, :]
        pQ = [s.ps(f"pQ{b}", [P, 512]) for b in range(2)]
        pN = s.ps("pN", [P, 512])
        pR = s.ps("pR", [HC, PAST])
        pA = s.ps("pA", [P, 16 * NPAGE, HA])[:, 0:NPAGE, :]
        pA1 = s.ps("pA1", [1, 512])
        pO = s.ps("pO", [HA, 512])
        names = ("taken", "step", "pstep", "prods", "newd", "newc", "qrep", "qcop", "sdone", "turned", "laid",
                 "maxed", "expd", "combd", "backt", "bcop", "summed", "kept", "gathered", "dstep", "astep")
        (taken, step, pstep, prods, newd, newc, qrep, qcop, sdone, turned, laid,
         maxed, expd, combd, backt, bcop, summed, kept, gathered, dstep, astep) = (s.sem(n) for n in names)
        kin, vin, kfree, vfree = ([s.sem(f"{n}{b}") for b in range(2)] for n in ("kin", "vin", "kfree", "vfree"))
        blk = s.block()

        def sequences(eng, first, middle, last):
            first(0, 0)
            with eng.Fori(0, DEC // 2 - 1) as i:
                middle(i, 1)
                middle(i, 2)
            middle(DEC // 2 - 1, 1)
            last(DEC // 2 - 1, 1)

        @blk.sync
        def _(sp):
            for b in range(2):
                sp.sem_inc(kin[b], 16 * NPAGE)
            with sp.Fori(1, DEC // 2) as i:
                for b in range(2):
                    sp.wait_ge(kfree[b], i)
                    load_pages(sp, past["ck"], pages, i * (2 * NPAGE) + b * NPAGE, K[b], kin[b])

        @blk.gpsimd
        def _(pool):
            chain = Chain(pool, pstep)
            chain(nc.gpsimd.iota(bias[:, :, :, :], pattern=[[-PAGE, NPAGE], [0, HC]], base=PAST, channel_multiplier=-1,
                                 allow_small_or_imprecise_dtypes=True))
            chain(nc.gpsimd.memset(comb0[:, :], 0.0))
            chain(nc.gpsimd.affine_select(out=comb0[:, :], in_=comb0[:, :], compare_op=ALU.not_equal, fill=1.0, base=0,
                                          pattern=[[-1, HA]], channel_multiplier=1))
            chain(nc.gpsimd.affine_select(out=comb0[:, :], in_=comb0[:, :], compare_op=ALU.not_equal, fill=2.0, base=-HA,
                                          pattern=[[-1, HA]], channel_multiplier=1))
            with pool.Fori(0, DEC // 2) as i:
                for b in range(2):
                    pool.wait_ge(vfree[b], i + 1)
                    load_pages(pool, past["cv"], pages, i * (2 * NPAGE) + b * NPAGE, V[b], vin[b])
                    pool.dma_start(vn[b][:, :], vnew[bass.ds(i * 2 + b, 1), :]).then_inc(vin[b], 16)

        @blk.tensor
        def _(pe):
            for b in range(2):
                pe.sem_inc(vfree[b], 1)
            for b in range(DEC):
                if b >= 2:
                    pe.wait_ge(qcop, b - 1)
                for h in range(HA):
                    q = proj[:, 14 + h, zs + b:zs + b + 1].to_broadcast([P, P])
                    last = nc.tensor.matmul(pQ[b % 2][:, h * P:(h + 1) * P], q, c["ident"][:, :], start=True, stop=True)
                last.then_inc(qrep, 1)
            pe.wait_ge(prods, 1)
            for b in range(DEC):
                last = nc.tensor.matmul(pN[0:HC, b:b + 1], qk[:, b, :, :].rearrange("p e h -> p (e h)"), c["ones"][:, 0:1],
                                        start=True, stop=True)
            last.then_inc(newd, 1)

            def turn(i, off):
                pe.wait_ge(sdone, i * 2 + (off + 1))
                for pg in range(NPAGE):
                    last = nc.tensor.transpose(pR[:, pg * P:(pg + 1) * P], Sc[:, pg, :, :].rearrange("p e h -> p (e h)"), c["ident"][:, :])
                last.then_inc(turned, 1)

            def combine(i, off):
                pe.wait_ge(combd, i * 2 + (off + 1))
                for pg in range(NPAGE):
                    nc.tensor.matmul(pA[:, pg, :], rows[:, pg * P:(pg + 1) * P], comb[:, :], start=True, stop=True)
                nc.tensor.matmul(pA1[:, 0:HA], rows[:, PAST:PAST + 1], comb[:, :], start=True, stop=True).then_inc(backt, 1)

            def values(i, off):
                b = off % 2
                pe.wait_ge(bcop, i * 2 + (off + 1))
                pe.wait_ge(kept, i * 2 + (off + 1))
                pe.wait_ge(vin[b], (i + (off // 2 + 1)) * (16 * (NPAGE + 1)))
                for pg in range(NPAGE):
                    nc.tensor.matmul(pO[:, :], at[:, pg, :], V[b][:, pg, :], start=(pg == 0), stop=False)
                nc.tensor.matmul(pO[:, :], atn[:, :], vn[b][:, :], start=False, stop=True).then_inc(summed, 1)

            def middle(i, off):
                combine(i, off - 1)
                turn(i, off)
                values(i, off - 1)

            def last_one(i, off):
                combine(i, off)
                values(i, off)

            pe.sem_inc(kept, 1)
            sequences(pe, turn, middle, last_one)
            pe.wait_ge(kept, DEC + 1)
            for b in range(DEC):
                for h in range(HA):
                    last = nc.tensor.matmul(pN[:, h * DEC + b:h * DEC + b + 1], orow[:, b, h * DV:(h + 1) * DV],
                                            c["ident"][0:HA, h:h + 1], start=True, stop=True)
            last.then_inc(gathered, 1)

        @blk.scalar
        def _(act):
            for b in range(DEC):
                act.wait_ge(qrep, b + 1)
                sc(nc)(Q[:, b, :], pQ[b % 2][:, :], ACT.Copy).then_inc(qcop, 1)
            act.wait_ge(newc, 1)

            def lay(i, off):
                act.wait_ge(turned, i * 2 + (off + 1))
                sc(nc)(rows[:, 0:PAST], pR[:, :], ACT.Copy).then_inc(laid, 1)
                sc(nc)(rows[:, PAST:PAST + 1], new[:, bass.ds(i * 2 + off, 1)], ACT.Copy).then_inc(laid, 1)

            def exponent(i, off):
                act.wait_ge(maxed, i * 2 + (off + 1))
                sc(nc)(rows[:, :], rows[:, :], ACT.Exp, bias=st[:, 0:1], accum_out=st[:, 1:2]).then_inc(expd, 1)

            def weights(i, off):
                act.wait_ge(backt, i * 2 + (off + 1))
                sc(nc)(at[:, :, :], pA[:, :, :], ACT.Copy).then_inc(astep, 1)
                act.wait_ge(astep, i * 2 + (off + 1))
                sc(nc)(atn[:, :], pA1[:, 0:HA], ACT.Copy).then_inc(bcop, 1)

            def keep(i, off):
                b = off % 2
                act.wait_ge(summed, i * 2 + (off + 1))
                sc(nc)(orow[:, bass.ds(i * 2 + off, 1), :], pO[:, :].unsqueeze(1), ACT.Copy).then_inc(kept, 1)
                act.sem_inc(vfree[b], 1)

            def first(i, off):
                lay(i, off)
                exponent(i, off)

            def middle(i, off):
                weights(i, off - 1)
                lay(i, off)
                exponent(i, off)
                keep(i, off - 1)

            def last_one(i, off):
                weights(i, off)
                keep(i, off)

            sequences(act, first, middle, last_one)

        @blk.vector
        def _(dve):
            chain = Chain(dve, step)
            for e in range(2):
                chain(nc.vector.memset(qk[64 * (1 - e):64 * (1 - e) + 64, :, e, :], 0.0))
                q = slice(64 * e, 64 * e + 64)
                chain(nc.vector.tensor_tensor(qk[q, :, e, :].rearrange("p b h -> p h b"), proj[q, 14:18, zs:zs + DEC],
                                              proj[q, 18:22, zs:zs + DEC], ALU.mult))
            dve.wait_ge(pstep, 4)
            for h in range(HA):
                chain(nc.vector.tensor_scalar(bias[:, :, :, h], bias[:, :, :, h], -SLOPE[h], None, ALU.mult))
            chain(nc.vector.tensor_scalar(comb[:, :], comb0[:, :], 2.0, None, ALU.is_equal))
            chain(nc.vector.tensor_scalar(comb0[:, :], comb0[:, :], 1.0, None, ALU.is_equal))
            nc.vector.scalar_tensor_tensor(out=comb0[:, :], in0=comb[:, :], scalar=c["lam"][0:HC, 1:2], in1=comb0[:, :],
                                           op0=ALU.mult, op1=ALU.add).then_inc(prods, 1)
            dve.wait_ge(newd, 1)
            nc.vector.tensor_copy(new[:, :], pN[0:HC, 0:DEC]).then_inc(newc, 1)
            dve.wait_ge(newc, 1)
            dve.wait_ge(prods, 1)
            def product(i, off):
                b = off % 2
                dve.wait_ge(kin[b], (i + (off // 2 + 1)) * (16 * NPAGE))
                nc.vector.tensor_tensor(K[b][:, :, :], K[b][:, :, :],
                                        Q[:, bass.ds(i * 2 + off, 1), :].to_broadcast([P, NPAGE, 512]), ALU.mult).then_inc(dstep, 1)

            def reduce(i, off, n):
                b = off % 2
                dve.wait_ge(dstep, i * 6 + n)
                nc.vector.tensor_reduce(Sc[:, :, :, :].rearrange("p g e h -> p g h e"),
                                        K[b][:, :, :].rearrange("p g (h e d) -> p g h e d", h=HA, e=2), AX.X, ALU.add).then_inc(dstep, 1)

            def bias_add(i, off, n):
                b = off % 2
                dve.wait_ge(dstep, i * 6 + n)
                dve.sem_inc(kfree[b], 1)
                nc.vector.tensor_tensor(Sc[:, :, :, :], Sc[:, :, :, :], bias[:, :, :, :], ALU.add).then_inc(sdone, 1)

            def maximum(i, off):
                dve.wait_ge(laid, (i * 2 + (off + 1)) * 2)
                nc.vector.tensor_reduce(st[:, 0:1], rows[:, :], AX.X, ALU.max, negate=True).then_inc(maxed, 1)

            def scale(i, off, n):
                dve.wait_ge(expd, i * 2 + (off + 1))
                nc.vector.reciprocal(st[:, 2:3], st[:, 1:2]).then_inc(dstep, 1)
                dve.wait_ge(dstep, i * 6 + n)
                nc.vector.tensor_scalar(comb[:, :], comb0[:, :], st[:, 2:3], None, ALU.mult).then_inc(combd, 1)

            def first(i, off):
                dve.wait_ge(qcop, 1)
                product(i, off)
                reduce(i, off, 1)
                bias_add(i, off, 2)
                dve.wait_ge(qcop, DEC)

            def middle(i, off):
                n = 2 + 3 * (off - 1)
                product(i, off)
                maximum(i, off - 1)
                reduce(i, off, n + 1)
                scale(i, off - 1, n + 3)
                bias_add(i, off, n + 2)

            def last_one(i, off):
                maximum(i, off)
                scale(i, off, 2 + 3 + 1)

            sequences(dve, first, middle, last_one)
            dve.wait_ge(gathered, 1)
            nc.vector.tensor_copy(oT[:, :, SEQ:TQ], pN[:, 0:HA * DEC].rearrange("p (h b) -> p h b", h=HA)).then_inc(taken, 1)


def head_norm(nc, c, oT):
    H = TQ // 2
    with Stage(nc, "subln") as s:
        sq = s.sb("sq", [P, HA, TQ])
        pm = [s.ps(f"pm{h}", [P, 2, 512]) for h in range(HA)]
        squared, summed, root, step = (s.sem(n) for n in ("squared", "summed", "root", "step"))
        blk = s.block()
        g = PCOL["da_subln_g"]

        @blk.scalar
        def _(act):
            for h in range(HA):
                sc(nc)(sq[:, h, :], oT[:, h, :], ACT.Square).then_inc(squared, 1)
            for h in range(HA):
                act.wait_ge(summed, h + 1)
                sc(nc)(halves(sq[:, h, :]), pm[h][:, :, 0:H], ACT.Sqrt, bias=c["eps"][:, 0:1], scale=1.0 / DV).then_inc(root, 1)

        @blk.tensor
        def _(pe):
            for h in range(HA):
                pe.wait_ge(squared, h + 1)
                for a in range(2):
                    last = nc.tensor.matmul(pm[h][:, a, 0:H], c["ones"][:, :], sq[:, h, a * H:a * H + H], start=True, stop=True)
                last.then_inc(summed, 1)

        @blk.vector
        def _(dve):
            chain = Chain(dve, step)
            for h in range(HA):
                dve.wait_ge(root, h + 1)
                chain(nc.vector.reciprocal(sq[:, h, :], sq[:, h, :]))
                chain(nc.vector.scalar_tensor_tensor(out=oT[:, h, :], in0=oT[:, h, :], scalar=c["par"][:, g:g + 1], in1=sq[:, h, :],
                                                     op0=ALU.mult, op1=ALU.mult))
                chain(nc.vector.tensor_scalar(oT[:, h, :], oT[:, h, :], 1.0 - LAM_INIT, None, ALU.mult))


def split_columns(nc, x, hi, lo):
    with Stage(nc, "split") as s:
        cut = s.sem("cut")
        blk = s.block()

        @blk.scalar
        def _(act):
            for k in range(KD):
                sc(nc)(hi[:, k, :], x[:, k, :], ACT.Copy).then_inc(cut, 1)

        @blk.vector
        def _(dve):
            for k in range(KD):
                dve.wait_ge(cut, k + 1)
                nc.vector.tensor_tensor(lo[:, k, :], x[:, k, :], hi[:, k, :].bitcast(F32), ALU.subtract)


SPREAD = [(0, P + DEC), (P + DEC, P), (2 * P + DEC, P), (3 * P + DEC, P)]
TS = 2
TB = 8


def peer_choose(nc, ins, c, xn, eT):
    w = TQ // TT
    h2 = TQ // 2
    wv = ins["peer_wq"][0].rearrange("(c p) n -> p c n", p=P)
    with Stage(nc, "pick") as s:
        wt = [s.sb(f"w{b}", [P, KD, P]) for b in range(2)]
        kr = s.sb("kr", [P, 2, P])
        kT = s.sb("kT", [P, 2, P])
        qT = s.sb("qT", [P, 2, TQ])
        S = [s.sb(f"S{g}", [P, TT * 2, KEYS])[0:w] for g in range(2)]
        S2 = [s.sb(f"S2{b}", [P, KEYS])[0:w] for b in range(2)]
        v = [s.sb(f"v{g}", [P, TT, 2, TOPK])[0:w] for g in range(2)]
        ix = s.sb("ix", [P, TT, 2, TOPK], U32)[0:w]
        ixf = [s.sb(f"ixf{g}", [P, TT, 2, TOPK])[0:w] for g in range(2)]
        cand = [s.sb(f"cand{g}", [P, TT, TOPK, TOPK])[0:w] for g in range(2)]
        cand2 = [s.sb(f"cand2{b}", [P, TOPK * TOPK])[0:w] for b in range(2)]
        best = s.sb("best", [P, TT, PH, TOPK])[0:w]
        ci = s.sb("ci", [P, TT, TOPK], U32)[0:w]
        r = s.sb("r", [P, 2, TT, TOPK], U32)[0:w]
        rf = s.sb("rf", [P, 2, TT, TOPK])[0:w]
        one = [s.sb(f"one{e}", [P, TT, TOPK, TOPK])[0:w] for e in range(2)]
        ex = s.sb("ex", [P, TT, 3, PH, TOPK])[0:w]
        z = s.sb("z", [P, TT, PH])[0:w]
        acc = s.ps("acc", [P, 4, 512])
        pS = s.ps("pS", [P, 12, KEYS])
        pk = s.ps("pk", [P, 512])
        (keys, kturn, kcop, scored, copied, step, halved, paired, matched, looked, shifted, expd, chosen, turned, taken) = (
            s.sem(n) for n in ("keys", "kturn", "kcop", "scored", "copied", "step", "halved", "paired", "matched", "looked",
                               "shifted", "expd", "chosen", "turned", "taken"))
        loaded, done, queried = ([s.sem(f"{n}{e}") for e in range(2)] for n in ("loaded", "done", "queried"))
        blk = s.block()
        NEG = -3.0e38

        @blk.sync
        def _(sp):
            sp.dma_start(kr[:, :, :], ins["peer_subkeys"][0].rearrange("c k d -> k c d")).then_inc(keys, 16)
            with sp.Fori(0, PH) as i:
                for e in range(2):
                    sp.wait_ge(done[e], i + 1)
                    sp.dma_start(wt[e][:, :, :], wv[:, :, bass.ds(i * (2 * P) + e * P, P)]).then_inc(loaded[e], 16)

        @blk.tensor
        def _(pe):
            for e in range(2):
                pe.sem_inc(done[e], 1)
            pe.wait_ge(keys, 16)
            for e in range(2):
                last = nc.tensor.transpose(pk[:, e * P:(e + 1) * P], kr[:, e, :], c["ident"][:, :])
            last.then_inc(kturn, 1)
            pe.wait_ge(kcop, 1)
            with pe.Fori(0, PH) as i:
                for e in range(2):
                    pe.wait_ge(loaded[e], i * 16 + 16)
                    pe.wait_ge(queried[e], i + 1)
                    for k in range(KD):
                        for a in range(2):
                            last = nc.tensor.matmul(acc[:, 2 * e + a, 0:h2], wt[e][:, k, :], xn[:, k, a * h2:a * h2 + h2],
                                                    start=(k == 0), stop=(k == KD - 1))
                    last.then_inc(done[e], 1)
                for e in range(2):
                    pe.wait_ge(queried[e], i + 2)
                    if e == 0:
                        pe.wait_ge(copied, i + 1)
                    for j in range(TT):
                        last = nc.tensor.matmul(pS[0:w, 2 * j + e, :], qT[:, e, j * w:(j + 1) * w], kT[:, e, :],
                                                start=True, stop=True)
                last.then_inc(scored, 1)
            pe.wait_ge(chosen, 1)
            slots = acc[:, :, :].rearrange("p a (s c) -> p (a s) c", c=P)
            for q in range(3):
                for j in range(TT):
                    last = nc.tensor.transpose(slots[:, q * TT + j, 0:w], ex[:, j, q, :, :].rearrange("p h k -> p (h k)"),
                                               c["ident"][0:w, 0:w])
            last.then_inc(turned, 1)

        @blk.scalar
        def _(act):
            act.wait_ge(kturn, 1)
            sc(nc)(kT[:, :, :], pk[:, 0:2 * P].rearrange("p (e k) -> p e k", e=2), ACT.Copy).then_inc(kcop, 1)
            for e in range(2):
                act.sem_inc(queried[e], 1)
            act.sem_inc(copied, 1)
            act.sem_inc(scored, 1)
            with act.Fori(0, PH // 2) as i:
                for g in range(2):
                    act.wait_ge(scored, i * 2 + (g + 1))
                    for e in range(2):
                        act.wait_ge(done[e], i * 2 + (g + 2))
                        sc(nc)(halves3(qT[:, e:e + 1, :]), acc[:, 2 * e:2 * e + 2, 0:h2], ACT.Copy).then_inc(queried[e], 1)
                    act.wait_ge(scored, i * 2 + (g + 2))
                    act.wait_ge(halved, i * 2 + (g + 1))
                    sc(nc)(S[g][:, :, :], pS[0:w, 0:2 * TT, :], ACT.Copy).then_inc(copied, 1)
            act.wait_ge(shifted, 1)
            sc(nc)(ex[:, :, 2, :, :], ex[:, :, 2, :, :], ACT.Exp).then_inc(expd, 1)
            act.wait_ge(turned, 1)
            slots = acc[:, :, :].rearrange("p a (s c) -> p (a s) c", c=P)
            for q in range(3):
                sc(nc)(eT[:, q, :].rearrange("p (j t) -> p j t", j=TT), slots[:, q * TT:(q + 1) * TT, 0:w], ACT.Copy).then_inc(taken, 1)

        @blk.gpsimd
        def _(pool):
            def pairs(i, off):
                g = off % 2
                pool.wait_ge(halved, i * 2 + (off + 3))
                nc.gpsimd.tensor_tensor(cand[g][:, :, :, :], v[g][:, :, 0, :].unsqueeze(3).to_broadcast([w, TT, TOPK, TOPK]),
                                        v[g][:, :, 1, :].unsqueeze(2).to_broadcast([w, TT, TOPK, TOPK]), ALU.add).then_inc(paired, 1)

            def look(i, off):
                g = off % 2
                for e in range(2):
                    pool.wait_ge(matched, i * 4 + (off * 2 + e + 1))
                    nc.gpsimd.tensor_tensor(one[e][:, :, :, :], one[e][:, :, :, :],
                                            ixf[g][:, :, e, :].unsqueeze(2).to_broadcast([w, TT, TOPK, TOPK]),
                                            ALU.mult).then_inc(looked, 1)

            pairs(0, 0)
            with pool.Fori(0, PH // 2 - 1) as i:
                for off in (1, 2):
                    pairs(i, off)
                    look(i, off - 1)
            pairs(PH // 2 - 1, 1)
            look(PH // 2 - 1, 0)
            look(PH // 2 - 1, 1)

        @blk.vector
        def _(dve):
            chain = Chain(dve, step)
            dve.sem_inc(halved, 2)

            def top16(jobs):
                ops = [(lambda val, idx, src, rest: nc.vector.max(val[:, 0:8], src)),
                       (lambda val, idx, src, rest: nc.vector.max_index(idx[:, 0:8], val[:, 0:8], src)),
                       (lambda val, idx, src, rest: nc.vector.match_replace(rest, val[:, 0:8], src, NEG)),
                       (lambda val, idx, src, rest: nc.vector.max(val[:, 8:16], rest)),
                       (lambda val, idx, src, rest: nc.vector.max_index(idx[:, 8:16], val[:, 8:16], rest))]
                for op in ops:
                    for job in jobs:
                        op(*job).then_inc(step, 1)
                        chain.n += 1
                        dve.wait_ge(step, chain.n - len(jobs) + 1)
                dve.wait_ge(step, chain.n)

            def best_of_halves(h):
                g = h % 2
                dve.wait_ge(copied, h + 2)
                for j in range(TT):
                    top16([(v[g][:, j, e, :], ix[:, j, e, :], S[g][:, 2 * j + e, :], S2[e][:, :]) for e in range(2)])

            def indices(h):
                nc.vector.tensor_copy(ixf[h % 2][:, :, :, :], ix[:, :, :, :]).then_inc(halved, 1)
                dve.wait_ge(halved, h + 3)

            def key_indices(h):
                for e in range(2):
                    dve.wait_ge(looked, 2 * h + e + 1)
                    chain(nc.vector.tensor_reduce(ex[:, :, e, h, :], one[e][:, :, :, :], AX.X, ALU.add))

            best_of_halves(0)
            indices(0)
            for h in range(PH):
                g = h % 2
                if h + 1 < PH:
                    best_of_halves(h + 1)
                if h:
                    key_indices(h - 1)
                if h + 1 < PH:
                    indices(h + 1)
                dve.wait_ge(paired, h + 1)
                for js in ((0, 1), (2, 3), (4,)):
                    top16([(best[:, j, h, :], ci[:, j, :], cand[g][:, j, :, :].rearrange("p a b -> p (a b)"), cand2[j % 2][:, :])
                           for j in js])
                chain(nc.vector.tensor_scalar(r[:, 0, :, :], ci[:, :, :], 4, None, ALU.logical_shift_right))
                chain(nc.vector.tensor_scalar(r[:, 1, :, :], ci[:, :, :], TOPK - 1, None, ALU.bitwise_and))
                chain(nc.vector.tensor_copy(rf[:, :, :, :], r[:, :, :, :]))
                iota = c["iota"][0:w, 0:TOPK].unsqueeze(1).to_broadcast([w, TT * TOPK, TOPK])
                for e in range(2):
                    pick = rf[:, e, :, :].rearrange("p j a -> p (j a)").unsqueeze(2).to_broadcast([w, TT * TOPK, TOPK])
                    nc.vector.tensor_tensor(one[e][:, :, :, :].rearrange("p j a b -> p (j a) b"), pick, iota,
                                            ALU.is_equal).then_inc(matched, 1)
            nc.vector.tensor_tensor(ex[:, :, 2, :, :], best[:, :, :, :], best[:, :, :, 0:1].to_broadcast([w, TT, PH, TOPK]),
                                    ALU.subtract).then_inc(shifted, 1)
            key_indices(PH - 1)
            dve.wait_ge(expd, 1)
            chain(nc.vector.tensor_reduce(z[:, :, :], ex[:, :, 2, :, :], AX.X, ALU.add))
            chain(nc.vector.reciprocal(z[:, :, :], z[:, :, :]))
            nc.vector.tensor_tensor(ex[:, :, 2, :, :], ex[:, :, 2, :, :], z[:, :, :].unsqueeze(3).to_broadcast([w, TT, PH, TOPK]),
                                    ALU.mult).then_inc(chosen, 1)


def peer_spread(nc, c, eT, mscr):
    NG = TB // TS
    with Stage(nc, "spread") as s:
        M = [s.sb(f"M{b}", [P, KEYS, P + DEC]) for b in range(2)]
        et = s.sb("et", [P, 3, TB])
        e1 = s.sb("e1", [P, 1, TB])
        e1used = s.sb("e1used", [P, NG])
        A = [s.sb(f"A{g}", [P, TS, KEYS]) for g in range(NG)]
        B = [s.sb(f"B{g}", [P, TS, KEYS]) for g in range(NG)]
        pm = [s.ps(f"pm{g}", [P, 4, KEYS])[:, 0:TS, :] for g in range(NG)]
        far = s.sb("far", [P, TS, KEYS])
        estep, e1step, hot, first_hot, ready, farstep, near = (
            s.sem(n) for n in ("estep", "e1step", "hot", "first_hot", "ready", "farstep", "near"))
        done, out = ([s.sem(f"{n}{g}") for g in range(NG)] for n in ("done", "out"))
        stored = [s.sem(f"stored{b}") for b in range(2)]
        blk = s.block()

        @blk.sync
        def _(sp):
            for n, (t0, w) in enumerate(SPREAD):
                sp.wait_ge(ready, n + 1)
                sp.dma_start(mscr[:, :, t0:t0 + w], M[n % 2][:, :, 0:w]).then_inc(stored[n % 2], 16)
            for b in range(2):
                sp.wait_ge(stored[b], 16 * len(SPREAD[b::2]))

        @blk.tensor
        def _(pe):
            for g in range(NG):
                pe.sem_inc(done[g], 1)
            with pe.Fori(0, TQ // TB) as i:
                for g in range(NG):
                    pe.wait_ge(hot, i * NG + (g + 2))
                    if g == 0:
                        pe.wait_ge(near, i + 1)
                    if g % 2:
                        pe.wait_ge(first_hot, i * (NG // 2) + (g // 2 + 2))
                    pe.wait_ge(out[g], i + 1)
                    for t in range(TS):
                        last = nc.tensor.matmul(pm[g][:, t, :], A[g][:, t, :], B[g][:, t, :], start=True, stop=True)
                    last.then_inc(done[g], 1)

        @blk.scalar
        def _(act):
            for g in range(NG):
                act.sem_inc(out[g], 1)

            keys1 = eT[:, :, :].rearrange("p q t -> p (q t)")

            def first_matrices(i):
                for t in range(TS):
                    sc(nc)(far[:, t, :], c["iota"][:, :], ACT.Abs, bias=keys1[:, bass.ds(i * TB + t, 1)], scale=-1.0).then_inc(farstep, 1)
                act.wait_ge(farstep, i * TS + TS)
                sc(nc)(A[0][:, :, :], far[:, :, :], ACT.Relu, bias=c["ones"][:, 0:1], scale=-1.0).then_inc(near, 1)

            first_matrices(0)
            for n, (t0, w) in enumerate(SPREAD):
                if n >= 2:
                    act.wait_ge(stored[n % 2], 16 * (n // 2))
                with act.Fori(t0 // TB, (t0 + w) // TB) as i:
                    act.wait_ge(near, i + 1)
                    act.wait_ge(done[0], i + 2)
                    first_matrices(i + 1)
                    for g in range(NG):
                        act.wait_ge(done[g], i + 2)
                        at = bass.ds(i * TB + (g * TS - t0), TS)
                        sc(nc)(M[n % 2][:, :, at].rearrange("p e t -> p t e"), pm[g][:, :, :], ACT.Copy).then_inc(out[g], 1)
                for g in range(NG):
                    act.wait_ge(out[g], (t0 + w) // TB + 1)
                act.sem_inc(ready, 1)

        @blk.gpsimd
        def _(pool):
            pool.sem_inc(first_hot, 1)
            with pool.Fori(0, TQ // TB) as i:
                pool.wait_ge(first_hot, i * (NG // 2) + 1)
                nc.gpsimd.tensor_copy(e1[:, :, :], eT[:, 0:1, bass.ds(i * TB, TB)]).then_inc(e1step, 1)
                for g in range(1, NG, 2):
                    if g == 1:
                        pool.wait_ge(e1step, i + 1)
                    pool.wait_ge(done[g], i + 1)
                    nc.gpsimd.tensor_tensor(e1used[:, g:g + 1], c["iota"][:, 0:1], c["iota"][:, 0:1], ALU.add)
                    for t in range(TS):
                        q = g * TS + t
                        last = nc.gpsimd.tensor_scalar(A[g][:, t, :], c["iota"][:, :], e1[:, 0, q:q + 1], None, ALU.is_equal)
                    last.then_inc(first_hot, 1)

        @blk.vector
        def _(dve):
            dve.sem_inc(hot, 1)
            with dve.Fori(0, TQ // TB) as i:
                dve.wait_ge(hot, i * NG + 1)
                nc.vector.tensor_copy(et[:, :, :], eT[:, :, bass.ds(i * TB, TB)]).then_inc(estep, 1)
                dve.wait_ge(estep, i + 1)
                for g in range(NG):
                    dve.wait_ge(done[g], i + 1)
                    for t in range(TS):
                        q = g * TS + t
                        if g % 2 == 0 and g > 0:
                            nc.vector.tensor_scalar(A[g][:, t, :], c["iota"][:, :], et[:, 0, q:q + 1], None, ALU.is_equal)
                        last = nc.vector.tensor_scalar(B[g][:, t, :], c["iota"][:, :], et[:, 1, q:q + 1], et[:, 2, q:q + 1],
                                                       ALU.is_equal, ALU.mult)
                    last.then_inc(hot, 1)


def peer_experts(nc, ins, c, xh, xl, mscr, acc):
    H = TQ // 2
    NQ = KEYS // 2
    uv = ins["peer_u"][0].rearrange("(a b) d -> a b d", b=KEYS)
    vv = ins["peer_v"][0].rearrange("(a b) d -> a b d", b=KEYS)
    with Stage(nc, "experts") as s:
        U = [s.sb(f"U{b}", [P, 2, D]) for b in range(2)]
        V = [s.sb(f"V{b}", [P, 2, D]) for b in range(2)]
        M = [s.sb(f"M{b}", [P, 2, TQ]) for b in range(2)]
        UH = [s.sb(f"UH{e}", [P, KD, P], F32R) for e in range(2)]
        UL = [s.sb(f"UL{e}", [P, KD, P], F32R) for e in range(2)]
        VH = [s.sb(f"VH{b}", [P, 2, D], F32R) for b in range(2)]
        VL = [s.sb(f"VL{b}", [P, 2, D], F32R) for b in range(2)]
        G = [s.sb(f"G{e}", [P, TQ]) for e in range(2)]
        GH = [s.sb(f"GH{b}", [P, 2, TQ], F32R) for b in range(2)]
        GL = [s.sb(f"GL{b}", [P, 2, TQ], F32R) for b in range(2)]
        pU = [s.ps(f"pU{a}", [P, 4, P]) for a in range(2)]
        pH = [s.ps(f"pH{a}", [P, 512]) for a in range(2)]
        pV = [s.ps(f"pV{a}", [P, 512]) for a in range(4)]
        u_in, v_in, m_in = ([s.sem(f"{n}{b}") for b in range(2)] for n in ("u_in", "v_in", "m_in"))
        turned, u_hi, u_lo, hidden, gelued, gated, g_hi, g_lo, v_hi, v_lo, summed, added = (
            s.sem(n) for n in ("turned", "u_hi", "u_lo", "hidden", "gelued", "gated", "g_hi", "g_lo", "v_hi", "v_lo",
                               "summed", "added"))
        blk = s.block()

        class Pair:

            def __init__(self, off, i=None):
                self.off, self.i, self.b = off, i, off % 2

            def count(self, per, n):
                return per * self.off + n if self.i is None else self.i * (2 * per) + (per * self.off + n)

            def loads(self):
                return 16 * (self.off // 2 + 1) if self.i is None else self.i * 16 + 16 * (self.off // 2 + 1)

            def after(self, n):
                return self.i is not None or self.off >= n

        def schedule(eng, first, body, tail):
            first()
            with eng.Fori(0, NQ // 2 - 1) as i:
                for off in range(2):
                    body(Pair(off, i), Pair(off + 1, i), Pair(off + 2, i))
            tail()

        def load(sp, q):
            k = q.b
            at = bass.ds(q.count(2, 0), 2)
            if q.after(2):
                sp.wait_ge(turned, q.count(4, -4))
            sp.dma_start(U[k][:, :, :], uv[:, at, :]).then_inc(u_in[k], 16)
            if q.after(2):
                sp.wait_ge(gated, q.count(2, -2))
            sp.dma_start(M[k][:, :, :], mscr[:, at, :]).then_inc(m_in[k], 16)
            if q.after(2):
                sp.wait_ge(v_lo, q.count(1, -1))
            sp.dma_start(V[k][:, :, :], vv[:, at, :]).then_inc(v_in[k], 16)

        @blk.sync
        def _(sp):
            schedule(sp, lambda: (load(sp, Pair(0)), load(sp, Pair(1))), lambda p, q, r: load(sp, r), lambda: None)

        def turn(pe, q, st):
            e, a = st // 2, st % 2
            if st == 0:
                pe.wait_ge(u_in[q.b], q.loads())
            if q.after(1) or st >= 2:
                pe.wait_ge(u_lo, q.count(4, st - 1))
            for k in range(4):
                last = nc.tensor.transpose(pU[a][:, k, :], U[q.b][:, e, (4 * a + k) * P:(4 * a + k + 1) * P], c["ident"][:, :])
            last.then_inc(turned, 1)

        def product_u(pe, q):
            for e in range(2):
                pe.wait_ge(u_lo, q.count(4, 2 * e + 2))
                for a in range(2):
                    if q.after(1) or e:
                        pe.wait_ge(gelued, q.count(4, 2 * e + a - 1))
                    ts = slice(a * H, (a + 1) * H)
                    for k in range(KD):
                        for n, (u, x) in enumerate(((UH, xh), (UH, xl), (UL, xh))):
                            last = nc.tensor.matmul(pH[a][:, 0:H], u[e][:, k, :], x[:, k, ts], start=(k == 0 and n == 0),
                                                    stop=(k == KD - 1 and n == 2))
                    last.then_inc(hidden, 1)

        def product_v(pe, q, n):
            k, a = n // 2, n % 2
            if n == 0:
                pe.wait_ge(v_lo, q.count(1, 1))
                pe.wait_ge(g_lo, q.count(2, 2))
            pe.wait_ge(added, q.count(16, n + 1))
            ts = slice(a * H, (a + 1) * H)
            terms = [(v[q.b][:, e, k * P:(k + 1) * P], g[q.b][:, e, ts]) for e in range(2) for v, g in ((VH, GH), (VH, GL), (VL, GH))]
            for t, (l, r) in enumerate(terms):
                last = nc.tensor.matmul(pV[n % 4][:, 0:H], l, r, start=(t == 0), stop=(t == 5))
            last.then_inc(summed, 1)

        @blk.tensor
        def _(pe):
            def first():
                for st in range(4):
                    turn(pe, Pair(0), st)
                product_u(pe, Pair(0))
                for st in range(4):
                    turn(pe, Pair(1), st)

            def body(p, q, r):
                product_u(pe, q)
                for n in range(16):
                    if n % 4 == 0:
                        turn(pe, r, n // 4)
                    product_v(pe, p, n)

            def tail():
                product_u(pe, Pair(NQ - 1))
                for p in (NQ - 2, NQ - 1):
                    for n in range(16):
                        product_v(pe, Pair(p), n)

            schedule(pe, first, body, tail)

        def cut_u(act, q, st):
            e, a = st // 2, st % 2
            act.wait_ge(turned, q.count(4, st + 1))
            if q.after(1):
                act.wait_ge(hidden, q.count(4, 2 * e - 2))
            sc(nc)(UH[e][:, 4 * a:4 * a + 4, :], pU[a][:, :, :], ACT.Copy).then_inc(u_hi, 1)

        def cut_v(act, q):
            act.wait_ge(v_in[q.b], q.loads())
            if q.after(2):
                act.wait_ge(summed, q.count(16, -16))
            sc(nc)(VH[q.b][:, :, :], V[q.b][:, :, :], ACT.Copy).then_inc(v_hi, 1)

        def gelu(act, q, e):
            for a in range(2):
                act.wait_ge(hidden, q.count(4, 2 * e + a + 1))
                if q.after(1):
                    act.wait_ge(g_lo, q.count(2, e - 1))
                sc(nc)(G[e][:, a * H:(a + 1) * H], pH[a][:, 0:H], ACT.Gelu).then_inc(gelued, 1)

        def cut_g(act, q, e):
            act.wait_ge(gated, q.count(2, e + 1))
            if q.after(2):
                act.wait_ge(summed, q.count(16, -16))
            sc(nc)(GH[q.b][:, e, :], G[e][:, :], ACT.Copy).then_inc(g_hi, 1)

        @blk.scalar
        def _(act):
            def hidden_values(q):
                gelu(act, q, 0)
                cut_v(act, q)
                cut_g(act, q, 0)
                gelu(act, q, 1)

            def first():
                for st in range(4):
                    cut_u(act, Pair(0), st)
                hidden_values(Pair(0))
                cut_g(act, Pair(0), 1)
                for st in range(4):
                    cut_u(act, Pair(1), st)

            def body(p, q, r):
                hidden_values(q)
                cut_u(act, r, 0)
                cut_g(act, q, 1)
                for st in range(1, 4):
                    cut_u(act, r, st)

            def tail():
                hidden_values(Pair(NQ - 1))
                cut_g(act, Pair(NQ - 1), 1)

            schedule(act, first, body, tail)

        def rest_g(pool, q, e):
            pool.wait_ge(g_hi, q.count(2, e + 1))
            nc.gpsimd.tensor_tensor(GL[q.b][:, e, :], G[e][:, :], GH[q.b][:, e, :].bitcast(F32), ALU.subtract).then_inc(g_lo, 1)

        def rest_v(pool, q):
            pool.wait_ge(v_hi, q.count(1, 1))
            nc.gpsimd.tensor_tensor(VL[q.b][:, :, :], V[q.b][:, :, :], VH[q.b][:, :, :].bitcast(F32), ALU.subtract).then_inc(v_lo, 1)

        @blk.gpsimd
        def _(pool):
            def all_of(q):
                rest_v(pool, q)
                rest_g(pool, q, 0)
                rest_g(pool, q, 1)

            schedule(pool, lambda: all_of(Pair(0)), lambda p, q, r: all_of(q), lambda: all_of(Pair(NQ - 1)))

        def rest_u(dve, q, st):
            e, a = st // 2, st % 2
            dve.wait_ge(u_hi, q.count(4, st + 1))
            nc.vector.tensor_tensor(UL[e][:, 4 * a:4 * a + 4, :], pU[a][:, :, :], UH[e][:, 4 * a:4 * a + 4, :].bitcast(F32),
                                    ALU.subtract).then_inc(u_lo, 1)

        def gate(dve, q, e):
            dve.wait_ge(m_in[q.b], q.loads())
            dve.wait_ge(gelued, q.count(4, 2 * e + 2))
            nc.vector.tensor_tensor(G[e][:, :], G[e][:, :], M[q.b][:, e, :], ALU.mult).then_inc(gated, 1)

        def add(dve, q, n):
            k, a = n // 2, n % 2
            dve.wait_ge(summed, q.count(16, n + 1))
            nc.vector.tensor_tensor(acc[:, k, a * H:(a + 1) * H], pV[n % 4][:, 0:H], acc[:, k, a * H:(a + 1) * H],
                                    ALU.add).then_inc(added, 1)

        @blk.vector
        def _(dve):
            def first():
                dve.sem_inc(added, 4)
                for st in range(4):
                    rest_u(dve, Pair(0), st)
                for e in range(2):
                    gate(dve, Pair(0), e)
                for st in range(4):
                    rest_u(dve, Pair(1), st)

            def body(p, q, r):
                for e in range(2):
                    gate(dve, q, e)
                for n in range(16):
                    if n % 4 == 0:
                        rest_u(dve, r, n // 4)
                    add(dve, p, n)

            def tail():
                for e in range(2):
                    gate(dve, Pair(NQ - 1), e)
                for p in (NQ - 2, NQ - 1):
                    for n in range(16):
                        add(dve, Pair(p), n)

            schedule(dve, first, body, tail)


def store_rows(nc, c, acc, outs):
    with Stage(nc, "store") as s:
        rows = [s.sb(f"rows{b}", [P, D]) for b in range(2)]
        pt = [s.ps(f"pt{b}", [P, 4, P]) for b in range(4)]
        turned, copied, stored = s.sem("turned"), s.sem("copied"), [s.sem(f"stored{b}") for b in range(2)]
        blk = s.block()

        @blk.tensor
        def _(pe):
            for n in range(2 * TT):
                j, half = n // 2, n % 2
                w = min(P, TQ - j * P)
                if n >= 4:
                    pe.wait_ge(copied, n - 3)
                for q in range(4):
                    last = nc.tensor.transpose(pt[n % 4][0:w, q, :], acc[:, 4 * half + q, j * P:j * P + w], c["ident"][:, :])
                last.then_inc(turned, 1)

        @blk.vector
        def _(dve):
            for n in range(2 * TT):
                j, half = n // 2, n % 2
                w = min(P, TQ - j * P)
                dve.wait_ge(turned, n + 1)
                if j >= 2:
                    dve.wait_ge(stored[j % 2], 16 * (j // 2))
                nc.vector.tensor_copy(rows[j % 2][0:w, 512 * half:512 * half + 512].rearrange("p (q d) -> p q d", q=4),
                                      pt[n % 4][0:w, :, :]).then_inc(copied, 1)

        @blk.sync
        def _(sp):
            for j in range(TT):
                sp.wait_ge(copied, 2 * j + 2)
                if j < 4:
                    dst = outs["y_prompt"][0, j * P:(j + 1) * P, :]
                    sp.dma_start(dst, rows[j % 2][:, :]).then_inc(stored[j % 2], 16)
                else:
                    sp.dma_start(outs["y_sample"][:, 0, :], rows[j % 2][0:DEC, :]).then_inc(stored[j % 2], 16)
            sp.wait_ge(stored[0], 48)
            sp.wait_ge(stored[1], 32)


def hybrid_step(nc, ins, outs, scr):
    def act_copy(dst):
        return lambda eng, i, b, p, tmp: sc(nc)(halves3(dst(i * 2 + b)), p, ACT.Copy)

    with ExitStack() as whole:
        def open_in(ctx):
            g = Stage(nc, "keep")
            ctx.enter_context(g)
            return g

        g = open_in(whole)
        c = constants(nc, g, ins)
        xT = g.sb("xT", [P, KD, T])
        xn = g.sb("xn", [P, KD, T])
        mixed = xn[:, :, 0:TQ]
        acc = xT[:, :, META:T]
        with ExitStack() as inner:
            b = open_in(inner)
            yo = b.sb("yo", [P, RB, TQ])
            oT = b.sb("oT", [P, HA, TQ])
            with ExitStack() as mixers:
                m = open_in(mixers)
                proj = m.sb("proj", [P, RWT + 2 * HA, TW])
                load_tokens(nc, ins, c, xT)
                channel_norm(nc, "norm1", c, xT, 0, T, PCOL["norm1_g"], xn)
                linear(nc, "inp", ins["w_in"][0], 0, RWT + 2 * HA, xn, 0, KD, T, "scalar",
                       act_copy(lambda n: proj[:, bass.ds(n, 1), PAD:TW]))
                shift_mix(nc, ins, c, proj, outs)
                with ExitStack() as rwkv:
                    r = open_in(rwkv)
                    rw = {n: r.sb(n, [P, RB, TW]) for n in ("lw", "L", "la", "kk", "b", "g")}
                    rw["bonus"] = r.sb("bonus", [P, RB, T])
                    yT = r.sb("yT", [P, RB, TW])
                    rwkv_prepare(nc, ins, c, proj, rw)
                    rwkv_chunks(nc, c, proj, rw, yT, outs, [yo, oT])
                    rwkv_sample(nc, c, proj, rw, yT, ins, outs, scr)
                    rwkv_output(nc, c, rw, yT, yo)
                v_tok = m.sb("v_tok", [P, TT, 512])
                attention_inputs(nc, ins, c, proj, xn, v_tok, outs, scr["v"])
                past = {"K": [m.sb(f"K{b}", [P, NPAGE, 512]) for b in range(2)],
                        "V": [m.sb(f"V{b}", [P, NPAGE, 512]) for b in range(2)],
                        "vn": [m.sb(f"vn{b}", [1, 512]) for b in range(2)],
                        "pages": m.sb("pages", [1, DEC * NPAGE], I32),
                        "ck": ins["cache_k"][0].rearrange("n p h c d -> n p (h c d)"),
                        "cv": ins["cache_v"][0].rearrange("n p h v -> n p (h v)")}
                attend_prompt(nc, ins, c, proj, v_tok, oT, past)
                attend_sample(nc, c, proj, oT, past, scr["v"])
            head_norm(nc, c, oT)
            gates = b.sb("gates", [P, 2 * KD, TQ])
            linear(nc, "gate", ins["w_in"][0], RW_PROJ + 3 * 512, 2 * KD, xn, META, KD, TQ, "scalar",
                   lambda eng, i, b, p, tmp: sc(nc)(halves3(gates[:, bass.ds(i * 2 + b, 1), :]), p, ACT.Sigmoid))
            linear(nc, "rwbr", ins["w_rw_br"][0], 0, KD, yo, 0, RB, TQ, "vector",
                   lambda eng, i, b, p, tmp: nc.vector.tensor_tensor(halves3(mixed[:, bass.ds(i * 2 + b, 1), :]), p,
                                                                     halves3(gates[:, bass.ds(i * 2 + b, 1), :]), ALU.mult))

            def add_branch(eng, i, b, p, tmp):
                t, sem = tmp
                gate = halves3(gates[:, bass.ds(i * 2 + (KD + b), 1), :])
                nc.vector.tensor_tensor(t[b][:, :, :], p, gate, ALU.mult).then_inc(sem, 1)
                eng.wait_ge(sem, i * 2 + b + 1)
                dst = halves3(mixed[:, bass.ds(i * 2 + b, 1), :])
                return nc.vector.tensor_tensor(dst, t[b][:, :, :], dst, ALU.add)

            linear(nc, "dabr", ins["w_da_br"][0], 0, KD, oT, 0, HA, TQ, "vector", add_branch,
                   extra=lambda s: ([s.sb(f"t{b}", [P, 2, TQ // 2]) for b in range(2)], s.sem("gated")))

        def add_residual(eng, i, b, p, tmp):
            return nc.vector.tensor_tensor(halves3(acc[:, bass.ds(i * 2 + b, 1), :]), p,
                                           halves3(xT[:, bass.ds(i * 2 + b, 1), META:T]), ALU.add)

        linear(nc, "out", ins["w_out"][0], 0, KD, mixed, 0, KD, TQ, "vector", add_residual)
        channel_norm(nc, "norm2", c, acc, 0, TQ, PCOL["norm2_g"], mixed)
        with ExitStack() as inner:
            b = open_in(inner)
            eT = b.sb("eT", [P, 3, TQ])
            peer_choose(nc, ins, c, mixed, eT)
            peer_spread(nc, c, eT, scr["gates"])
        with ExitStack() as inner:
            b = open_in(inner)
            xh = b.sb("xh", [P, KD, TQ], F32R)
            xl = b.sb("xl", [P, KD, TQ], F32R)
            split_columns(nc, mixed, xh, xl)
            peer_experts(nc, ins, c, xh, xl, scr["gates"], acc)
        store_rows(nc, c, acc, outs)


_INS = ["x_prompt", "x_sample", "cache_k", "cache_v", "state_wkv", "state_shift", "page_table", "meta", "norm1_g", "w_in",
        "rw_mu", "rw_w0", "rw_w2", "rw_a0", "rw_a2", "rw_g2", "rw_kk", "rw_ka", "rw_rk", "rw_ln_g", "rw_ln_b", "w_rw_br",
        "da_qn_g", "da_kn_g", "da_lam", "da_subln_g", "w_da_br", "w_out", "norm2_g", "peer_wq", "peer_subkeys", "peer_u",
        "peer_v"]
_OUTS = {"y_prompt": (1, SEQ, D), "y_sample": (DEC, 1, D), "k_prompt": (1, 1, NP_, HA, 2, 64), "v_prompt": (1, 1, NP_, HA, DV),
         "k_sample": (1, DEC, 1, HA, 2, 64), "v_sample": (1, DEC, 1, HA, DV), "wkv_prompt": (1, 1, 8, 64, 64),
         "wkv_sample": (1, DEC, 8, 64, 64), "shift_prompt": (1, 1, RW_PROJ), "shift_sample": (1, DEC, RW_PROJ)}
_SCRATCH = {"vec": (6, DEC, RW_DIM), "y": (DEC, RW_DIM), "v": (DEC, 512),
            "gates": (KEYS, KEYS, TQ)}


def kernel(**inputs):
    import numpy as _np
    import concourse.bacc as _bacc
    from concourse import mybir as _mybir
    from concourse.bass_utils import run_bass_kernel_spmd as _run

    nc = _bacc.Bacc("TRN2", target_bir_lowering=False, num_devices=1)
    arrays, ins, outs, scr = {}, {}, {}, {}
    for name in _INS:
        a = _np.ascontiguousarray(inputs[name])
        arrays[f"in_{name}"] = a
        ins[name] = nc.dram_tensor(f"in_{name}", a.shape, _mybir.dt.from_np(a.dtype), kind="ExternalInput").ap()
    for name, shape in _OUTS.items():
        outs[name] = nc.dram_tensor(f"out_{name}", shape, F32, kind="ExternalOutput").ap()
    for name, shape in _SCRATCH.items():
        scr[name] = nc.dram_tensor(f"scratch_{name}", shape, F32, kind="Internal").ap()
    hybrid_step(nc, ins, outs, scr)
    r = _run(nc, [arrays], core_ids=[0])
    return tuple(r.results[0][f"out_{name}"] for name in _OUTS)
```
